# Optimizing a Trainium2 kernel written in Bass

```python
import jax
import jax.numpy as jnp
from jax import lax
import numpy as np

D_MODEL = 1024
BATCH = 1
SEQ = 512
DEPTH = 1

RET_HEADS = 4
RET_DK = 64
RET_DV = 128
RET_CHUNK = 128
NSA_HEADS = 8
NSA_GROUPS = 2
NSA_HPG = NSA_HEADS // NSA_GROUPS
NSA_DH = 64
CMP_LEN = 32
CMP_STRIDE = 16
CMP_HIDDEN = 128
SLC_LEN = 64
SLC_TOPK = 16
WIN = 512
NSA_QB = 64
D_FF = ((8 * D_MODEL + 3 * 256 - 1) // (3 * 256)) * 256
ROPE_THETA = 10000.0
EPS = 1e-6
NEG = -1e30
FORCE = 1e6
IN_SIZES = (RET_HEADS * RET_DK, RET_HEADS * RET_DK, RET_HEADS * RET_DV, RET_HEADS * RET_DV,
            NSA_HEADS * NSA_DH,
            NSA_GROUPS * NSA_DH, NSA_GROUPS * NSA_DH,
            NSA_GROUPS * NSA_DH, NSA_GROUPS * NSA_DH,
            NSA_GROUPS * NSA_DH, NSA_GROUPS * NSA_DH,
            3 * NSA_HEADS)
IN_COLS = sum(IN_SIZES)
IN_SPLITS = tuple(int(v) for v in np.cumsum(IN_SIZES)[:-1])
MIX_WIDTH = RET_HEADS * RET_DV + NSA_HEADS * NSA_DH

kernel_name = 'hybrid_retention_nsa_block'

def rmsnorm(x, g):
    xf = x.astype(jnp.float32)
    y = xf * lax.rsqrt(jnp.mean(xf * xf, axis=-1, keepdims=True) + EPS)
    return (y * g.astype(jnp.float32)).astype(x.dtype)

def rope(x, pos):
    half = x.shape[-1] // 2
    inv = ROPE_THETA ** (-jnp.arange(half, dtype=jnp.float32) / half)
    ang = pos.astype(jnp.float32)[:, None] * inv
    cos, sin = jnp.cos(ang), jnp.sin(ang)
    x1 = x[..., :half].astype(jnp.float32)
    x2 = x[..., half:].astype(jnp.float32)
    return jnp.concatenate([x1 * cos - x2 * sin, x2 * cos + x1 * sin], axis=-1).astype(x.dtype)

def heads(t, n):
    b, s, _ = t.shape
    return t.reshape(b, s, n, -1).transpose(0, 2, 1, 3)

def retention(q, k, v):
    b, h, s, dk = q.shape
    dv = v.shape[-1]
    c = RET_CHUNK
    n = s // c
    log_g = jnp.log(1.0 - 2.0 ** (-5.0 - jnp.arange(h, dtype=jnp.float32)))
    idx = jnp.arange(c, dtype=jnp.float32)
    diff = idx[:, None] - idx[None, :]
    causal = diff >= 0
    decay = jnp.where(causal, jnp.exp(log_g[:, None, None] * jnp.where(causal, diff, 0.0)), 0.0)
    qc = q.reshape(b, h, n, c, dk).astype(jnp.float32)
    kc = k.reshape(b, h, n, c, dk).astype(jnp.float32)
    vc = v.reshape(b, h, n, c, dv).astype(jnp.float32)
    att = jnp.einsum('bhncd,bhnmd->bhncm', qc, kc) * decay[None, :, None]
    y_intra = jnp.einsum('bhncm,bhnme->bhnce', att, vc)
    zeta = jnp.exp(log_g[:, None] * (c - 1.0 - idx))
    kv = jnp.einsum('bhncd,bhnce->bhnde', kc * zeta[None, :, None, :, None], vc)
    g_chunk = jnp.exp(log_g * c)[None, :, None, None]

    def step(state, kv_n):
        return state * g_chunk + kv_n, state

    _, prev = lax.scan(step, jnp.zeros((b, h, dk, dv), jnp.float32), jnp.moveaxis(kv, 2, 0))
    prev = jnp.moveaxis(prev, 0, 2)
    xi = jnp.exp(log_g[:, None] * (idx + 1.0))
    y_cross = jnp.einsum('bhncd,bhnde->bhnce', qc * xi[None, :, None, :, None], prev)
    y = (y_intra + y_cross).reshape(b, h, s, dv)
    y = y * lax.rsqrt(jnp.mean(y * y, axis=-1, keepdims=True) + EPS)
    return y.astype(v.dtype)

def compress(t, pe, w1, w2):
    b, g, s, dh = t.shape
    r = CMP_LEN // CMP_STRIDE
    pieces = t.reshape(b, g, s // CMP_STRIDE, CMP_STRIDE, dh)
    n_c = s // CMP_STRIDE - r + 1
    blocks = jnp.concatenate([pieces[:, :, i:i + n_c] for i in range(r)], axis=3) + pe
    flat = blocks.reshape(b, g, n_c, CMP_LEN * dh)
    return jax.nn.silu(flat @ w1) @ w2

def nsa(q, kc, vc, ks, vs, kw, vw, gate_logits, pe_k, w1_k, w2_k, pe_v, w1_v, w2_v):
    b, s, _ = q.shape
    G, HPG, DH, QB = NSA_GROUPS, NSA_HPG, NSA_DH, NSA_QB
    pos = jnp.arange(s, dtype=jnp.int32)
    scale = DH ** -0.5
    q = rope(heads(q, NSA_HEADS), pos).reshape(b, G, HPG, s, DH)
    kc, vc = heads(kc, G), heads(vc, G)
    ks, vs = rope(heads(ks, G), pos), heads(vs, G)
    kw, vw = rope(heads(kw, G), pos), heads(vw, G)

    k_cmp = compress(kc, pe_k, w1_k, w2_k)
    v_cmp = compress(vc, pe_v, w1_v, w2_v)
    n_c = k_cmp.shape[2]
    cmp_end = jnp.arange(n_c, dtype=jnp.int32) * CMP_STRIDE + CMP_LEN - 1
    k_cmp = rope(k_cmp, cmp_end)
    s_cmp = jnp.einsum('bghsd,bgcd->bghsc', q, k_cmp).astype(jnp.float32) * scale
    cmask = cmp_end[None, :] <= pos[:, None]
    p_cmp = jnp.where(cmask, jax.nn.softmax(jnp.where(cmask, s_cmp, NEG), axis=-1), 0.0)
    o_cmp = jnp.einsum('bghsc,bgce->bghse', p_cmp.astype(v_cmp.dtype), v_cmp)

    nb = s // SLC_LEN
    n_sel = min(SLC_TOPK, nb)
    cs = jnp.arange(n_c) * CMP_STRIDE
    bs = jnp.arange(nb) * SLC_LEN
    overlap = jnp.maximum(jnp.minimum(cs[:, None] + CMP_LEN, bs[None] + SLC_LEN)
                          - jnp.maximum(cs[:, None], bs[None]), 0).astype(jnp.float32) / CMP_LEN
    imp = jnp.einsum('bghsc,cj->bgsj', p_cmp, overlap)
    blk = jnp.arange(nb)
    cur = pos // SLC_LEN
    forced = (blk[None] == 0) | (blk[None] == cur[:, None]) | (blk[None] == cur[:, None] - 1)
    bcausal = blk[None] * SLC_LEN <= pos[:, None]
    imp = jnp.where(bcausal, jnp.where(forced, FORCE, imp), NEG)
    top_val, top_idx = lax.top_k(imp, n_sel)
    top_ok = top_val > 0.5 * NEG

    ks_blk = ks.reshape(b, G, nb, SLC_LEN, DH)
    vs_blk = vs.reshape(b, G, nb, SLC_LEN, DH)
    kw_pad = jnp.pad(kw, ((0, 0), (0, 0), (WIN, 0), (0, 0)))
    vw_pad = jnp.pad(vw, ((0, 0), (0, 0), (WIN, 0), (0, 0)))
    nq = s // QB
    q_b = jnp.moveaxis(q.reshape(b, G, HPG, nq, QB, DH), 3, 0)
    idx_b = jnp.moveaxis(top_idx.reshape(b, G, nq, QB, n_sel), 2, 0)
    ok_b = jnp.moveaxis(top_ok.reshape(b, G, nq, QB, n_sel), 2, 0)
    gather = jax.vmap(jax.vmap(lambda kb, ix: kb[ix]))

    def query_block(args):
        i, qi, ix, ok = args
        t = i * QB + jnp.arange(QB, dtype=jnp.int32)
        k_sel = gather(ks_blk, ix)
        v_sel = gather(vs_blk, ix)
        s_sel = jnp.einsum('bghqd,bgqnld->bghqnl', qi, k_sel).astype(jnp.float32) * scale
        kpos = ix[..., None] * SLC_LEN + jnp.arange(SLC_LEN, dtype=jnp.int32)
        m_sel = (ok[..., None] & (kpos <= t[:, None, None]))[:, :, None]
        s_sel = jnp.where(m_sel, s_sel, NEG).reshape(b, G, HPG, QB, n_sel * SLC_LEN)
        p_sel = jax.nn.softmax(s_sel, axis=-1).reshape(b, G, HPG, QB, n_sel, SLC_LEN)
        o_sel = jnp.einsum('bghqnl,bgqnle->bghqe', p_sel.astype(v_sel.dtype), v_sel)
        start = i * QB
        k_win = lax.dynamic_slice_in_dim(kw_pad, start, WIN + QB, axis=2)
        v_win = lax.dynamic_slice_in_dim(vw_pad, start, WIN + QB, axis=2)
        wpos = start - WIN + jnp.arange(WIN + QB, dtype=jnp.int32)
        m_win = (wpos[None] <= t[:, None]) & (wpos[None] > t[:, None] - WIN) & (wpos[None] >= 0)
        s_win = jnp.einsum('bghqd,bgkd->bghqk', qi, k_win).astype(jnp.float32) * scale
        p_win = jax.nn.softmax(jnp.where(m_win, s_win, NEG), axis=-1)
        o_win = jnp.einsum('bghqk,bgke->bghqe', p_win.astype(v_win.dtype), v_win)
        return o_sel, o_win

    o_sel, o_win = lax.map(query_block, (jnp.arange(nq, dtype=jnp.int32), q_b, idx_b, ok_b))
    o_sel = jnp.moveaxis(o_sel, 0, 3).reshape(b, G, HPG, s, DH)
    o_win = jnp.moveaxis(o_win, 0, 3).reshape(b, G, HPG, s, DH)

    g = jax.nn.sigmoid(gate_logits.astype(jnp.float32)).astype(q.dtype)
    g = g.reshape(b, s, 3, NSA_HEADS).transpose(2, 0, 3, 1).reshape(3, b, G, HPG, s)[..., None]
    o = g[0] * o_cmp + g[1] * o_sel + g[2] * o_win
    return o.reshape(b, NSA_HEADS, s, DH).transpose(0, 2, 1, 3).reshape(b, s, NSA_HEADS * DH)

def setup_inputs(seed: int = 0) -> dict:
    key = jax.random.key(seed)
    k = jax.random.split(key, 20)

    def nrm(kk, shape, s):
        return jax.random.normal(kk, shape, jnp.float32) * s

    L, D, DH = DEPTH, D_MODEL, NSA_DH
    return {
        'x': nrm(k[0], (BATCH, SEQ, D), 1.0),
        'c': nrm(k[1], (BATCH, D), 1.0),
        'ln_mix_g': 1.0 + nrm(k[2], (L, D), 0.02),
        'ln_ffn_g': 1.0 + nrm(k[3], (L, D), 0.02),
        'w_ada': nrm(k[4], (L, D, 6 * D), 0.5 * D ** -0.5),
        'b_ada': nrm(k[5], (L, 6 * D), 0.01),
        'w_in': nrm(k[6], (L, D, IN_COLS), D ** -0.5),
        'cmp_pe_k': nrm(k[7], (L, CMP_LEN, DH), 0.02),
        'cmp_w1_k': nrm(k[8], (L, CMP_LEN * DH, CMP_HIDDEN), (CMP_LEN * DH) ** -0.5),
        'cmp_w2_k': nrm(k[9], (L, CMP_HIDDEN, DH), CMP_HIDDEN ** -0.5),
        'cmp_pe_v': nrm(k[10], (L, CMP_LEN, DH), 0.02),
        'cmp_w1_v': nrm(k[11], (L, CMP_LEN * DH, CMP_HIDDEN), (CMP_LEN * DH) ** -0.5),
        'cmp_w2_v': nrm(k[12], (L, CMP_HIDDEN, DH), CMP_HIDDEN ** -0.5),
        'w_out': nrm(k[13], (L, MIX_WIDTH, D), MIX_WIDTH ** -0.5),
        'w_ff_gate': nrm(k[14], (L, D, D_FF), D ** -0.5),
        'w_ff_up': nrm(k[15], (L, D, D_FF), D ** -0.5),
        'w_ff_down': nrm(k[16], (L, D_FF, D), D_FF ** -0.5),
        'ln_final_g': 1.0 + nrm(k[17], (D,), 0.02),
    }

def reference(x, c, ln_mix_g, ln_ffn_g, w_ada, b_ada, w_in, cmp_pe_k, cmp_w1_k, cmp_w2_k,
              cmp_pe_v, cmp_w1_v, cmp_w2_v, w_out, w_ff_gate, w_ff_up, w_ff_down, ln_final_g):
    b, s, _ = x.shape
    pos = jnp.arange(s, dtype=jnp.int32)
    for l in range(DEPTH):
        mod = jax.nn.silu(c) @ w_ada[l] + b_ada[l]
        sh1, sc1, ga1, sh2, sc2, ga2 = jnp.split(mod[:, None, :], 6, axis=-1)
        h = rmsnorm(x, ln_mix_g[l]) * (1.0 + sc1) + sh1
        (rq, rk, rv, rg, nq_, nkc, nvc, nks, nvs, nkw, nvw, ngate) = jnp.split(h @ w_in[l], IN_SPLITS, axis=-1)
        rq = rope(heads(rq, RET_HEADS), pos)
        rk = rope(heads(rk, RET_HEADS), pos) * (RET_DK ** -0.5)
        y_ret = retention(rq, rk, heads(rv, RET_HEADS))
        y_ret = y_ret.transpose(0, 2, 1, 3).reshape(b, s, RET_HEADS * RET_DV) * jax.nn.silu(rg)
        y_nsa = nsa(nq_, nkc, nvc, nks, nvs, nkw, nvw, ngate,
                    cmp_pe_k[l], cmp_w1_k[l], cmp_w2_k[l], cmp_pe_v[l], cmp_w1_v[l], cmp_w2_v[l])
        mix = jnp.concatenate([y_ret, y_nsa], axis=-1) @ w_out[l]
        x = x + ga1 * mix
        h2 = rmsnorm(x, ln_ffn_g[l]) * (1.0 + sc2) + sh2
        ffn = (jax.nn.silu(h2 @ w_ff_gate[l]) * (h2 @ w_ff_up[l])) @ w_ff_down[l]
        x = x + ga2 * ffn
    return rmsnorm(x, ln_final_g)


_drawn_inputs = setup_inputs


def setup_inputs(seed=0):
    import zlib

    import numpy as np

    out = dict(_drawn_inputs(seed))
    spreads = {}
    factors = {'ln_mix_g': 8.0,
     'ln_ffn_g': 8.0,
     'b_ada': 5.059,
     'cmp_pe_k': 8.0,
     'cmp_w1_k': 4.308,
     'cmp_w2_k': 4.128,
     'cmp_pe_v': 51.091,
     'ln_final_g': 8.009}
    for name, (base, spread) in spreads.items():
        noise = np.random.default_rng([zlib.crc32(name.encode()), seed]).standard_normal(out[name].shape)
        drawn = base * np.exp(spread * noise) if base else spread * noise
        out[name] = jnp.asarray(drawn.astype(out[name].dtype))
    for name, factor in factors.items():
        out[name] = (out[name] * factor).astype(out[name].dtype)
    return out
```

```python
from contextlib import ExitStack

import numpy as np

import concourse.bass as bass
from concourse import mybir

F32 = mybir.dt.float32
F32R = mybir.dt.float32r
ALU = mybir.AluOpType
ACT = mybir.ActivationFunctionType
AX = mybir.AxisListType

P = 128
T, D, DFF = 512, 1024, 2816
TT, KT, FT = T // P, D // P, DFF // P
RH, RDK, RDV = 4, 64, 128
NH, NG, HPG, DH = 8, 2, 4, 64
CL, CS, CHID = 32, 16, 128
NC = T // CS - CL // CS + 1
CP = 32
EPS = 1e-6
BIG = 1e30
QSCALE = -(DH ** -0.5)

C_CMP = 2048
C_Q = 1536
C_WIN = 2560
C_RQK = 0
C_RV = 512
C_RG = 1024
CHUNKS = [(C_CMP, 512), (C_Q, 512), (C_WIN, 280), (C_RQK, 512), (C_RV, 512), (C_RG, 512)]
K_CMP, K_Q, K_WIN, K_RQK, K_RV, K_RG = range(6)
UPC = 4
U_IN, U_OUT, U_GU, U_DOWN = UPC * len(CHUNKS), KT, 2 * FT, FT
U0_OUT = U_IN
U0_GU = U0_OUT + U_OUT
U0_DOWN = U0_GU + U_GU
UNITS = U0_DOWN + U_DOWN
TAIL = 2
SPLIT = 4
RAW = 7

ADA = [1, 0, 2, 4, 3, 5]
ADA_START = 16

K_ID, K_MASK, K_ROPE, K_CMASK, K_VALID, K_CROPE = 0, 128, 256, 768, 896, 900
K_N = 1028


def stream():
    items = [("ada", a) for a in range(ADA_START - 4)] + [("w", 0)]
    items += [("ada", a) for a in range(ADA_START - 4, ADA_START)] + [("w", 1), ("w", 2)]
    a, n_ada, span = ADA_START, KT * len(ADA), U_IN - 4
    for u in range(3, UNITS):
        items.append(("w", u))
        upto = min(n_ada, ADA_START + -(-(n_ada - ADA_START) * (u - 2) // span))
        while a < upto:
            items.append(("ada", a))
            a += 1
    return items


def block_kernel(nc, x, c, ln_mix_g, ln_ffn_g, w_ada, b_ada, w_in, cmp_pe_k, cmp_w1_k, cmp_w2_k,
                 cmp_pe_v, cmp_w1_v, cmp_w2_v, w_out, w_ff_gate, w_ff_up, w_ff_down, ln_final_g,
                 consts, decays, out):
    items = stream()
    place = {it: (n % RAW, 16 * (n // RAW + 1)) for n, it in enumerate(items)}
    ada_after = {}
    last_w = -1
    for kind, j in items:
        if kind == "w":
            last_w = j
        else:
            ada_after.setdefault(last_w, []).append(j)

    with ExitStack() as ctx:
        KB = 1024
        BASE = 16512

        def at(name, shape, dt, kb):
            return nc.alloc_sbuf_tensor_at(name, shape, dt, offset=BASE + int(kb * KB))

        small_at = [112 * KB + 4128]

        def small(name, shape, dt=F32):
            kb = small_at[0] / KB
            small_at[0] += (4 * int(np.prod(shape[1:])) + 31) // 32 * 32
            return at(name, shape, dt, kb)

        hTh = at("hTh", [P, KT, T], F32R, 0)
        hTl = at("hTl", [P, KT, T], F32R, 16)
        ga1 = at("ga1", [P, D], F32, 32)
        ga2 = at("ga2", [P, D], F32, 36)
        gfin = at("gfin", [P, D], F32, 40)
        flatT = at("flatT", [P, CL // 2, P], F32, 36)
        wh = at("wh", [P, SPLIT, D], F32R, 44)
        wl = at("wl", [P, SPLIT, D], F32R, 60)
        raw = at("raw", [P, RAW, D], F32, 76)
        acc = at("acc", [P, 2, D], F32, 104)
        cst = at("cst", [P, K_N], F32, 112)
        R = 122
        xT = at("xT", [P, KT, T], F32, R)
        xs = at("xs", [P, TT, D], F32, R + 54)
        hf = at("hf", [P, 2, T], F32, R + 70)
        junk = at("junk", [P, D], F32, R + 74)
        QTh = at("QTh", [P, HPG, T], F32R, R)
        QTl = at("QTl", [P, HPG, T], F32R, R + 8)
        KTh = at("KTh", [P, 2, T], F32R, R + 16)
        KTl = at("KTl", [P, 2, T], F32R, R + 20)
        V = at("V", [P, TT, 2, P], F32, R + 24)
        rqT = at("rqT", [P, 2, T], F32, R + 28)
        rkT = at("rkT", [P, 2, T], F32, R + 32)
        w1 = at("w1", [P, 2, CL // 2, CHID], F32, R + 36)
        rv = at("rv", [P, TT, RH * RDV], F32, R + 36)
        rg = at("rg", [P, TT, RH * RDV], F32, R + 44)
        stage = at("stage", [P, TT, 512], F32, R + 54)
        rot = at("rot", [P, TT, 512], F32, R + 62)
        rt = at("rt", [P, 2, 512], F32, R + 70)
        flat = at("flat", [P, CL * DH], F32, R + 74)
        Pr = at("Pr", [P, 3, T], F32, R + 54)
        PT = at("PT", [P, 2, T], F32, R + 60)
        mix = at("mix", [P, 2, D], F32, R + 64)
        ats = at("ats", [P, 2, T], F32, R + 72)
        decay = at("decay", [P, RH, T], F32, R + 76)
        sc = at("sc", [P, NH, CP], F32, 104)
        pc = at("pc", [P, NH, CP], F32, 105)
        pcT = at("pcT", [P, NG, P], F32, 106)
        tmpo = at("tmpo", [P, T], F32, 107)
        sqj = at("sqj", [P, T], F32, 109)
        x1 = at("x1", [P, TT, D], F32, R)
        act = at("act", [P, FT, T], F32, R + 16)
        ah = at("ah", [P, SPLIT, T], F32R, R + 60)
        al = at("al", [P, SPLIT, T], F32R, R + 68)
        xb = at("xb", [P, 2, D], F32, R + 76)
        sg = at("sg", [P, 2, T], F32, R + 76)
        tmp = at("tmp", [P, D], F32, 104)
        h2 = at("h2", [P, 2, 4, P], F32, 108)
        BD = small("BD", [P, NG, HPG * DH])
        w2 = small("w2", [P, 2, DH])
        identR = small("identR", [P, P], F32R)
        maskR = small("maskR", [P, P], F32R)
        KCh = small("KCh", [P, CP], F32R)
        KCl = small("KCl", [P, CP], F32R)
        rows = at("rows", [P, P], F32, 108)
        cols = small("cols", [P, 88])
        cs = small("cs", [P, KT])
        mods = small("mods", [P, 4, KT])
        ones = at("ones", [P, P], F32, R + 52)
        ssq = small("ssq", [P, TT])
        rstd = small("rstd", [P, TT])
        expo = small("expo", [P, TT])
        mn = small("mn", [P, 8])
        den = small("den", [P, 2, 2, NH])
        gates = small("gates", [P, TT, 3 * NH])
        rgt = small("rgt", [P, NH])
        mnc = small("mnc", [P, NH])
        yss = small("yss", [P, RH])
        hs = small("hs", [P, 2, 2 * CP])
        assert small_at[0] <= 122 * KB, small_at[0] / KB
        kcr = at("kcr", [CP, P], F32, R + 52.5)

        ident = cst[:, K_ID:K_ID + P]
        rope = cst[:, K_ROPE:K_ROPE + TT * P].rearrange("p (t n) -> p t n", t=TT)
        cmask = cst[:, K_CMASK:K_CMASK + TT * CP].rearrange("p (t n) -> p t n", t=TT)

        ps = ctx.enter_context(nc.psum_tensor("ps", [P, 8, 512], F32))

        kv_dram = nc.dram_tensor("kv_scratch", (T, 2 * P), F32, kind="Internal").ap()

        def sem(name):
            return ctx.enter_context(nc.semaphore(name))

        raw_in = [sem(f"raw_in{i}") for i in range(RAW)]
        rows_in, const_in, w1_in, w2_in = sem("rows_in"), sem("const_in"), sem("w1_in"), sem("w2_in")
        bias1_in, bias2_in = sem("bias1_in"), sem("bias2_in")
        gfin_in, decay_in, flat_in, x_in = sem("gfin_in"), sem("decay_in"), sem("flat_in"), sem("x_in")
        xagain_in, kv_out = sem("xagain_in"), sem("kv_out")
        out_done = [sem(f"out_done{t}") for t in range(TT)]
        w_hi, w_lo, unit_used, ada_used = sem("w_hi"), sem("w_lo"), sem("unit_used"), sem("ada_used")
        ones_set, rowsT, cols_ok, c_silu, mod_sum, mod_read = (sem(n) for n in ("ones_set", "rowsT", "cols_ok", "c_silu", "mod_sum", "mod_read"))
        sq_done, xn_done, xT_ps, xT_ok, h_hi, h_lo = (sem(n) for n in ("sq_done", "xn_done", "xT_ps", "xT_ok", "h_hi", "h_lo"))
        proj_ev, roped, rotT, rot_hi, rot_lo = (sem(n) for n in ("proj_ev", "roped", "rotT", "rot_hi", "rot_lo"))
        flat_zero, flatT_ps, flatT_ok, mlp1, mlp1_silu, mlp2, kc_rot, bd_ok, kcT, kcT_hi, kcT_lo = (
            sem(n) for n in ("flat_zero", "flatT_ps", "flatT_ok", "mlp1", "mlp1_silu", "mlp2", "kc_rot", "bd_ok", "kcT", "kcT_hi", "kcT_lo"))
        consts_r, var_ok, rstd_ok = sem("consts_r"), sem("var_ok"), sem("rstd_ok")
        N_X, N_RET, N_X1, N_X2 = 1, 2, 2 + TT, 2 + 2 * TT
        s_ps, s_min, p_exp, p_T, pT_ok, pv = (sem(n) for n in ("s_ps", "s_min", "p_exp", "p_T", "pT_ok", "pv"))
        cs_ps, c_pre, c_exp, c_den, c_T, cT_ok, c_o = (sem(n) for n in ("cs_ps", "c_pre", "c_exp", "c_den", "c_T", "cT_ok", "c_o"))
        y_sum, r_s, r_dec, r_y, r_sq, r_norm = (sem(n) for n in ("y_sum", "r_s", "r_dec", "r_y", "r_sq", "r_norm"))
        mixT_ps, mix_hi, mix_lo = (sem(n) for n in ("mixT_ps", "mix_hi", "mix_lo"))
        o_ps, x1_ok, sq2, xb_ok, xbT, h2_ok, h2_hi, h2_lo = (sem(n) for n in ("o_ps", "x1_ok", "sq2", "xb_ok", "xbT", "h2_ok", "h2_hi", "h2_lo"))
        gate_ps, up_ps, sg_ok, act_ok, a_hi, a_lo, a_used = (sem(n) for n in ("gate_ps", "up_ps", "sg_ok", "act_ok", "a_hi", "a_lo", "a_used"))
        d_ps, x2_ok, sq3, y_ok = (sem(n) for n in ("d_ps", "x2_ok", "sq3", "y_ok"))
        dve_step, act_step = sem("dve_step"), sem("act_step")

        block = ctx.enter_context(nc.Block())

        def unit(u):
            if u < U0_OUT:
                c0, n = CHUNKS[u // UPC]
                k = 2 * (u % UPC)
                return (w_in[k * P:(k + 2) * P, c0:c0 + n].rearrange("(k p) n -> p k n", p=P),
                        lambda s: s[:, 0:2 * n].rearrange("p (k n) -> p k n", k=2))
            if u < U0_GU:
                k = u - U0_OUT
                return w_out[k * P:(k + 1) * P, :], lambda s: s
            if u < U0_DOWN:
                f, up = divmod(u - U0_GU, 2)
                w = w_ff_up if up else w_ff_gate
                return (w[:, f * P:(f + 1) * P].rearrange("(k p) n -> p k n", p=P),
                        lambda s: s.rearrange("p (k n) -> p k n", k=KT))
            f = u - U0_DOWN
            return w_ff_down[f * P:(f + 1) * P, :], lambda s: s

        def size(u):
            return 2 * CHUNKS[u // UPC][1] if u < U0_OUT else D

        @block.sync
        def _(sp):
            def refill(n):
                if n >= RAW:
                    kind, j = items[n - RAW]
                    sp.wait_ge(w_lo if kind == "w" else ada_used, j + 1)
                kind, j = items[n]
                slot = n % RAW
                if kind == "w":
                    src, view = unit(j)
                    sp.dma_start(view(raw[:, slot, :]), src).then_inc(raw_in[slot], 16)
                else:
                    g, k = divmod(j, KT)
                    col = ADA[g] * D
                    sp.dma_start(raw[:, slot, :], w_ada[k * P:(k + 1) * P, col:col + D]).then_inc(raw_in[slot], 16)

            for t in range(TT):
                sp.dma_start(xs[:, t, :], x[t * P:(t + 1) * P, :]).then_inc(x_in, 16)
            for n, (kind, j) in enumerate(items):
                if (kind, j) == ("w", 2):
                    for i, w in enumerate((cmp_w1_k, cmp_w1_v)):
                        sp.dma_start(w1[:, i, :, :], w.rearrange("(j p) n -> p j n", p=P)).then_inc(w1_in, 16)
                if (kind, j) == ("w", 20):
                    sp.wait_ge(mlp1, 1)
                    sp.dma_start(gfin[:, :], ln_final_g.partition_broadcast(P)).then_inc(gfin_in, 16)
                    sp.wait_ge(flatT_ok, 4)
                    sp.dma_start(decay[:, :, :], decays).then_inc(decay_in, 16)
                if (kind, j) == ("w", U0_GU - 1):
                    sp.wait_ge(s_ps, 16 * TT)
                    sp.wait_ge(cs_ps, TT)
                    for t in range(TT):
                        sp.dma_start(x1[:, t, :], x[t * P:(t + 1) * P, :]).then_inc(xagain_in, 16)
                refill(n)
            for t in range(TT):
                sp.wait_ge(y_ok, t + 1)
                sp.dma_start(out[t * P:(t + 1) * P, :], xb[:, t % 2, :]).then_inc(out_done[t], 16)
            for t in range(TT):
                sp.wait_ge(out_done[t], 16)

        @block.gpsimd
        def _(pool):
            pool.memset(rows[:, :], 0.0).then_inc(ones_set, 1)
            pool.memset(ones[:, :], 1.0).then_inc(ones_set, 1)
            pool.memset(BD[:, :, :], 0.0).then_inc(ones_set, 1)
            pool.memset(expo[:, :], -0.5).then_inc(ones_set, 1)
            pool.dma_start(ga1[:, :], b_ada[2 * D:3 * D].partition_broadcast(P)).then_inc(bias1_in, 16)

            def low(u):
                slot, count = place[("w", u)]
                n = size(u)
                pool.wait_ge(raw_in[slot], count)
                pool.wait_ge(w_hi, u + 1)
                pool.tensor_tensor(wl[:, u % SPLIT, 0:n], raw[:, slot, 0:n],
                                   wh[:, u % SPLIT, 0:n].bitcast(F32), ALU.subtract).then_inc(w_lo, 1)

            def power(n, buf):
                pool.wait_ge(var_ok, n)
                pool.tensor_tensor(buf, buf, expo[:, 0:buf.shape[1]], ALU.pow).then_inc(rstd_ok, 1)

            pool.wait_ge(ones_set, 4)
            power(N_X, rstd[:, :])
            for u in range(UNITS):
                if u == U0_OUT + 4:
                    for i in range(TT):
                        power(N_RET + i, yss[:, :])
                if u == U0_GU + 2:
                    for t in range(TT):
                        power(N_X1 + t, rstd[:, t:t + 1])
                if u == 3:
                    pool.wait_ge(sq_done, TT)
                    pool.memset(flat[:, :], 0.0).then_inc(flat_zero, 1)
                if u == 4 + UPC:
                    for t in range(TT):
                        pool.wait_ge(proj_ev, t + 1)
                        pool.dma_start(kv_dram[t * P:(t + 1) * P, :], stage[:, t, 0:2 * P]).then_inc(kv_out, 16)
                    pool.wait_ge(kv_out, 16 * TT)
                    pool.wait_ge(flat_zero, 1)
                    for kv in range(2):
                        for g in range(NG):
                            row = (kv * NG + g) * CP
                            col = (kv * NG + g) * DH
                            src = kv_dram[0:NC * CS, col:col + DH].rearrange("(c l) d -> c l d", l=CS)
                            nxt = kv_dram[CS:(NC + 1) * CS, col:col + DH].rearrange("(c l) d -> c l d", l=CS)
                            dst = flat[row:row + NC, :].rearrange("c (h l d) -> c h l d", h=2, d=DH)
                            pool.dma_start(dst[:, 0], src).then_inc(flat_in, 16)
                            pool.dma_start(dst[:, 1], nxt).then_inc(flat_in, 16)
                if u == 15:
                    pool.wait_ge(mlp1, 1)
                    pool.dma_start(ga2[:, :], b_ada[5 * D:6 * D].partition_broadcast(P)).then_inc(bias2_in, 16)
                low(u)
            for t in range(TT):
                power(N_X2 + t, rstd[:, t:t + 1])

        @block.scalar
        def _(a):
            steps = [0]

            def then(ins):
                steps[0] += 1
                ins.then_inc(act_step, 1)
                a.wait_ge(act_step, steps[0])

            def wait_used(u):
                if u < U0_GU - TAIL:
                    a.wait_ge(unit_used, u + 1)
                elif u < U0_GU:
                    a.wait_ge(d_ps, TT)
                elif u < U0_DOWN:
                    f, up = divmod(u - U0_GU, 2)
                    a.wait_ge(up_ps if up else gate_ps, f + 1)
                else:
                    a.wait_ge(a_used, u - U0_DOWN + 1)

            def high(u):
                slot, count = place[("w", u)]
                n = size(u)
                a.wait_ge(raw_in[slot], count)
                if u >= SPLIT:
                    wait_used(u - SPLIT)
                a.activation(wh[:, u % SPLIT, 0:n], raw[:, slot, 0:n], ACT.Copy).then_inc(w_hi, 1)

            a.wait_ge(ones_set, 1)
            for dst, src in ((0, c), (8, ln_mix_g), (16, ln_ffn_g), (24, b_ada[0:2 * D]), (40, b_ada[3 * D:5 * D])):
                v = src.rearrange("(r n) -> r n", n=P)
                a.dma_start(rows[dst:dst + v.shape[0], :], v).then_inc(rows_in, 16)
            for dst, pe_ in ((56, cmp_pe_k), (72, cmp_pe_v)):
                a.dma_start(rows[dst:dst + CL // 2, :].rearrange("j (l d) -> j l d", d=DH),
                            pe_.rearrange("(j l) d -> j l d", l=2)).then_inc(rows_in, 16)
            a.dma_start(cst[:, :], consts).then_inc(const_in, 16)
            a.dma_start(w2[:, 0, :], cmp_w2_k).then_inc(w2_in, 16)
            a.dma_start(w2[:, 1, :], cmp_w2_v).then_inc(w2_in, 16)

            a.wait_ge(cols_ok, 1)
            a.activation(cs[:, :], cols[:, 0:KT], ACT.Silu).then_inc(c_silu, 1)
            for t in range(TT):
                a.wait_ge(x_in, 16 * TT)
                if t:
                    a.wait_ge(sq_done, t)
                a.activation(junk[:, :], xs[:, t, :], ACT.Square, accum_out=ssq[:, t:t + 1]).then_inc(sq_done, 1)
            for k in range(KT):
                a.wait_ge(xT_ps, k + 1)
                a.activation(xT[:, k, :], ps[:, k % 4, :], ACT.Copy).then_inc(xT_ok, 1)
            high(0)
            a.wait_ge(const_in, 16)
            a.activation(identR[:, :], ident, ACT.Copy).then_inc(consts_r, 1)
            a.activation(maskR[:, :], cst[:, K_MASK:K_MASK + P], ACT.Copy).then_inc(consts_r, 1)
            a.wait_ge(mod_read, 2)
            for k in range(KT):
                a.wait_ge(xT_ok, k + 1)
                a.activation(hTh[:, k, :], xT[:, k, :], ACT.Identity, bias=mods[:, 1, k:k + 1],
                             scale=mods[:, 0, k:k + 1]).then_inc(h_hi, 1)
                if k == 1:
                    high(1)
                if k == 3:
                    high(2)

            def evacuate(ch):
                for t in range(TT):
                    if t < TT - 1:
                        a.wait_ge(o_ps, (TT - 1) * ch + t + 1)
                    else:
                        a.wait_ge(unit_used, UPC * (ch + 1))
                    if ch == K_CMP:
                        a.activation(stage[:, t, 0:384], ps[:, t, 0:384], ACT.Copy)
                        ins = a.activation(V[:, t, 0, :], ps[:, t, 384:512], ACT.Copy)
                    elif ch == K_Q:
                        a.wait_ge(roped, t + 1)
                        a.wait_ge(kv_out, 16 * TT)
                        ins = a.activation(stage[:, t, :], ps[:, t, :], ACT.Copy)
                    elif ch == K_WIN:
                        a.wait_ge(roped, TT + t + 1)
                        a.activation(stage[:, t, 0:P], ps[:, t, 0:P], ACT.Copy)
                        a.activation(V[:, t, 1, :], ps[:, t, P:2 * P], ACT.Copy)
                        ins = a.activation(gates[:, t, :], ps[:, t, 2 * P:2 * P + 3 * NH], ACT.Tanh, scale=0.5)
                    elif ch == K_RQK:
                        a.wait_ge(roped, 2 * TT + t + 1)
                        ins = a.activation(stage[:, t, :], ps[:, t, :], ACT.Copy)
                    elif ch == K_RV:
                        ins = a.activation(rv[:, t, :], ps[:, t, :], ACT.Copy)
                    else:
                        ins = a.activation(rg[:, t, :], ps[:, t, :], ACT.Silu)
                    ins.then_inc(proj_ev, 1)

            def rot_high(n):
                a.wait_ge(rotT, n + 1)
                src = ps[:, 4 + n % 2, :]
                if n == 0 or n == 5:
                    ins = a.activation(KTh[:, n // 5, :], src, ACT.Copy)
                elif n < 5:
                    t = n - 1
                    ins = a.activation(QTh[:, :, t * P:(t + 1) * P], src.rearrange("p (h q) -> p h q", h=HPG),
                                       ACT.Copy, scale=QSCALE)
                else:
                    t = n - 6
                    v = src.rearrange("p (h q) -> p h q", h=4)
                    a.activation(rqT[:, :, t * P:(t + 1) * P], v[:, 0:2], ACT.Copy)
                    ins = a.activation(rkT[:, :, t * P:(t + 1) * P], v[:, 2:4], ACT.Copy, scale=RDK ** -0.5)
                ins.then_inc(rot_hi, 1)

            for v in range(U_IN):
                if v and v % UPC == 0:
                    evacuate(v // UPC - 1)
                high(v + 3)
                for n in {7: [0], 10: [1, 2], 12: [3, 4], 15: [5], 18: [6, 7], 19: [8, 9]}.get(v, []):
                    rot_high(n)
                if v == 12:
                    a.wait_ge(mlp1, 1)
                    a.activation(hs[:, :, :], ps[:, 7, 0:4 * CP].rearrange("p (i n) -> p i n", i=2), ACT.Silu).then_inc(mlp1_silu, 1)
                if v == 16:
                    a.wait_ge(kcT, 1)
                    a.activation(KCh[:, :], ps[:, 7, 0:CP], ACT.Copy).then_inc(kcT_hi, 1)
            evacuate(K_RG)
            high(U_IN + 3)

            def exp(n):
                i = n // 16
                w = (i + 1) * P
                b, hd = divmod(n % 16, 8)
                head = hd % NG * HPG + hd // NG
                a.wait_ge(s_min, n + 1)
                if n >= 3:
                    a.wait_ge(p_T, n - 2)
                a.activation(Pr[:, n % 3, 0:w], ps[:, n % 2, 0:w], ACT.Exp, bias=mn[:, n % 8:n % 8 + 1], scale=-1.0,
                             accum_out=den[:, i % 2, b, head:head + 1]).then_inc(p_exp, 1)

            def pT_copy(n):
                w = (n // 16 + 1) * P
                a.wait_ge(p_T, n + 1)
                if n >= 2:
                    a.wait_ge(pv, n - 1)
                a.activation(PT[:, n % 2, 0:w], ps[:, 2 + n % 2, 0:w], ACT.Copy).then_inc(pT_ok, 1)

            def mix_high(i):
                a.wait_ge(mixT_ps, i + 1)
                a.activation(hTh[:, :, i * P:(i + 1) * P], ps[:, 6:8, :].rearrange("p b (k q) -> p (b k) q", k=4),
                             ACT.Copy).then_inc(mix_hi, 1)

            def ret_squares(i):
                a.wait_ge(r_y, RH * (i + 1))
                for h in range(RH):
                    ins = a.activation(sqj[:, h * P:(h + 1) * P], ps[:, 7, h * P:(h + 1) * P], ACT.Square,
                                       accum_out=yss[:, h:h + 1])
                ins.then_inc(r_sq, 1)

            for n in range(16 * TT + 6):
                i, s = divmod(n, 16)
                if 1 <= n <= 16 * TT:
                    exp(n - 1)
                if 2 <= n <= 16 * TT + 1:
                    pT_copy(n - 2)
                if s == 1 and i >= 1:
                    ret_squares(i - 1)
                if s == 7 and i < TT:
                    a.wait_ge(c_pre, i + 1)
                    a.activation(pc[:, :, :], sc[:, :, :], ACT.Exp, scale=-1.0).then_inc(c_exp, 1)
                if s == 9 and i < TT:
                    a.wait_ge(c_T, i + 1)
                    a.activation(pcT[:, :, :], ps[:, 6, 0:2 * P].rearrange("p (g q) -> p g q", g=NG), ACT.Copy).then_inc(cT_ok, 1)
                if s == 5 and i >= 1:
                    mix_high(i - 1)

            for u in range(U0_OUT + 4, U0_GU + 2):
                high(u)

            def x1_square(t):
                a.wait_ge(x1_ok, t + 1)
                a.activation(xb[:, t % 2, :], x1[:, t, :], ACT.Square, accum_out=ssq[:, t:t + 1]).then_inc(sq2, 1)

            x1_square(0)
            for t in range(TT):
                if t == TT - 2:
                    high(U0_GU + 2)
                    high(U0_GU + 3)
                if t < TT - 1:
                    x1_square(t + 1)
                for b in range(2):
                    a.wait_ge(h2_ok, 2 * t + b + 1)
                    a.activation(hTh[:, 4 * b:4 * b + 4, t * P:(t + 1) * P], h2[:, b], ACT.Copy).then_inc(h2_hi, 1)

            for f in range(FT):
                a.wait_ge(gate_ps, f + 1)
                if f >= 2:
                    a.wait_ge(act_ok, f - 1)
                a.activation(sg[:, f % 2, :], ps[:, 2 * (f % 2), :], ACT.Silu).then_inc(sg_ok, 1)
                high(U0_GU + 2 * f + 4)
                high(U0_GU + 2 * f + 5)

            def a_high(f):
                a.wait_ge(act_ok, f + 1)
                if f >= SPLIT:
                    a.wait_ge(a_used, f - SPLIT + 1)
                a.activation(ah[:, f % SPLIT, :], act[:, f, :], ACT.Copy).then_inc(a_hi, 1)

            for f in range(SPLIT):
                a_high(f)
            for f in range(SPLIT, FT):
                a_high(f)
                high(U0_DOWN + f)
            for t in range(TT):
                a.wait_ge(x2_ok, t + 1)
                if t >= 2:
                    a.wait_ge(out_done[t - 2], 16)
                a.activation(xb[:, t % 2, :], x1[:, t, :], ACT.Square, accum_out=ssq[:, t:t + 1]).then_inc(sq3, 1)

        @block.vector
        def _(v_):
            d = v_
            steps = [0]

            def then(ins):
                steps[0] += 1
                ins.then_inc(dve_step, 1)
                d.wait_ge(dve_step, steps[0])

            d.wait_ge(rowsT, 1)
            d.tensor_copy(cols[:, :], ps[:, 4, 0:88]).then_inc(cols_ok, 1)
            d.wait_ge(cols_ok, 1)
            for i in (0, 2):
                off = 32 if i == 0 else 48
                then(d.tensor_scalar(cols[:, off:off + KT], cols[:, off:off + KT], 1.0, None, ALU.add))
            d.wait_ge(sq_done, TT)
            d.tensor_scalar(rstd[:, :], ssq[:, :], 1.0 / D, EPS, ALU.mult, ALU.add).then_inc(var_ok, 1)
            d.wait_ge(rstd_ok, N_X)
            for t in range(TT):
                d.tensor_scalar(xs[:, t, :], xs[:, t, :], rstd[:, t:t + 1], None, ALU.mult).then_inc(xn_done, 1)

            def ada(j):
                g, k = divmod(j, KT)
                slot, count = place[("ada", j)]
                if j == 0:
                    d.wait_ge(c_silu, 1)
                if k == 0 and g >= 2:
                    d.wait_ge(mod_sum, {2: 1, 3: 2, 4: 4, 5: 5}[g])
                d.wait_ge(raw_in[slot], count)
                dst = acc[:, g % 2, :]
                if k == 0:
                    d.tensor_scalar(dst, raw[:, slot, :], cs[:, k:k + 1], None, ALU.mult).then_inc(ada_used, 1)
                else:
                    d.wait_ge(ada_used, j)
                    d.scalar_tensor_tensor(dst, raw[:, slot, :], cs[:, k:k + 1], dst, ALU.mult, ALU.add).then_inc(ada_used, 1)

            def mod_columns(n, i, b_off, g_off):
                d.wait_ge(mod_sum, n)
                add = d.tensor_tensor(mods[:, i, :], ps[:, min(4 + n, 7), (n - 1) * KT:n * KT], cols[:, b_off:b_off + KT], ALU.add)
                if g_off is None:
                    add.then_inc(mod_read, 1)
                else:
                    then(add)
                    d.tensor_tensor(mods[:, i, :], mods[:, i, :], cols[:, g_off:g_off + KT], ALU.mult).then_inc(mod_read, 1)

            def mod_rows(n, ga, half):
                d.wait_ge(mod_sum, n)
                d.wait_ge(bias1_in if ga is ga1 else bias2_in, 16)
                h = ga[:, half * 512:(half + 1) * 512]
                d.tensor_tensor(h, ps[:, 7, :], h, ALU.add).then_inc(mod_read, 1)

            for j in range(ADA_START):
                ada(j)
            mod_columns(1, 0, 32, 8)
            mod_columns(2, 1, 24, None)
            d.wait_ge(mod_read, 2)
            for k in range(KT):
                d.wait_ge(xT_ok, k + 1)
                if k >= 2:
                    d.wait_ge(h_lo, k - 1)
                then(d.tensor_scalar(hf[:, k % 2, :], xT[:, k, :], mods[:, 0, k:k + 1], mods[:, 1, k:k + 1], ALU.mult, ALU.add))
                d.wait_ge(h_hi, k + 1)
                d.tensor_tensor(hTl[:, k, :], hf[:, k % 2, :], hTh[:, k, :].bitcast(F32), ALU.subtract).then_inc(h_lo, 1)

            def rotate(src, table, n, dst, view=lambda x: x, parts=P):
                a0 = rt[0:parts, 0, 0:n * DH].rearrange("p (h x) -> p h x", x=DH)
                a1 = rt[0:parts, 1, 0:n * DH].rearrange("p (h x) -> p h x", x=DH)
                cos = table[:, 0:DH].unsqueeze(1).broadcast_to([parts, n, DH])
                s0 = table[:, DH:DH + 32].unsqueeze(1).broadcast_to([parts, n, 32])
                s1 = table[:, DH + 32:2 * DH].unsqueeze(1).broadcast_to([parts, n, 32])
                d.tensor_tensor(a0, src, cos, ALU.mult)
                d.tensor_tensor(a1[:, :, 0:32], src[:, :, 32:64], s0, ALU.mult)
                then(d.tensor_tensor(a1[:, :, 32:64], src[:, :, 0:32], s1, ALU.mult))
                return d.tensor_tensor(dst, view(a0), view(a1), ALU.add)

            def rope_chunk(ch, tiles):
                for t in tiles:
                    if TT * ch + t:
                        d.wait_ge(roped, TT * ch + t)
                    d.wait_ge(proj_ev, TT * ch + t + 1)
                    if ch == K_CMP:
                        src = stage[:, t, 2 * P:3 * P].rearrange("p (h x) -> p h x", x=DH)
                        dst = rot[:, t, 0:P].rearrange("p (h x) -> p h x", x=DH)
                        rotate(src, rope[:, t, :], 2, dst).then_inc(roped, 1)
                    elif ch == K_Q:
                        if t == 0:
                            d.wait_ge(rotT, 1)
                        src = stage[:, t, :].rearrange("p (h x) -> p h x", x=DH)
                        dst = rot[:, t, :].rearrange("p (h g x) -> p g h x", g=NG, x=DH)
                        rotate(src, rope[:, t, :], NH, dst, lambda z: z.rearrange("p (g h) x -> p g h x", g=NG)).then_inc(roped, 1)
                    elif ch == K_WIN:
                        if t == 0:
                            d.wait_ge(rotT, 5)
                        src = stage[:, t, 0:P].rearrange("p (h x) -> p h x", x=DH)
                        dst = rot[:, t, 0:P].rearrange("p (h x) -> p h x", x=DH)
                        rotate(src, rope[:, t, :], 2, dst).then_inc(roped, 1)
                    else:
                        if t == 0:
                            d.wait_ge(rotT, 6)
                        src = stage[:, t, :].rearrange("p (h x) -> p h x", x=DH)
                        dst = rot[:, t, :].rearrange("p (h x) -> p h x", x=DH)
                        rotate(src, rope[:, t, :], NH, dst).then_inc(roped, 1)

            def rot_low(n):
                d.wait_ge(rotT, n + 1)
                d.wait_ge(rot_hi, n + 1)
                src = ps[:, 4 + n % 2, :]
                if n == 0 or n == 5:
                    ins = d.tensor_tensor(KTl[:, n // 5, :], src, KTh[:, n // 5, :].bitcast(F32), ALU.subtract)
                else:
                    t = n - 1
                    ins = d.scalar_tensor_tensor(QTl[:, :, t * P:(t + 1) * P], src.rearrange("p (h q) -> p h q", h=HPG), QSCALE,
                                                 QTh[:, :, t * P:(t + 1) * P].bitcast(F32), ALU.mult, ALU.subtract)
                ins.then_inc(rot_lo, 1)

            def flat_add(b):
                d.wait_ge(flatT_ps, b + 1)
                for kv in range(2):
                    src = ps[:, 6, :].rearrange("p (j n) -> p j n", j=4)[:, :, kv * 2 * CP:(kv + 1) * 2 * CP]
                    pe_ = cols[:, 56 + 16 * kv + 4 * b:60 + 16 * kv + 4 * b].unsqueeze(2).broadcast_to([P, 4, 2 * CP])
                    ins = d.tensor_tensor(flatT[:, 4 * b:4 * b + 4, kv * 2 * CP:(kv + 1) * 2 * CP], src, pe_, ALU.add)
                ins.then_inc(flatT_ok, 1)

            def compressed():
                d.wait_ge(proj_ev, TT * 3)
                d.tensor_scalar(gates[:, :, :], gates[:, :, :], 0.5, 0.5, ALU.mult, ALU.add)
                d.wait_ge(mlp2, 1)
                d.wait_ge(roped, TT * K_WIN + 2)
                kc = ps[0:CP, 6, 0:P].rearrange("p (g x) -> p g x", g=NG)
                rotate(kc, cst[0:CP, K_CROPE:K_CROPE + P], NG, kcr[:, :].rearrange("p (g x) -> p g x", g=NG),
                       parts=CP).then_inc(kc_rot, 1)
                d.wait_ge(kc_rot, 1)
                d.wait_ge(ones_set, 3)
                for g in range(NG):
                    for h in range(HPG):
                        ins = d.tensor_copy(BD[CP * h:CP * (h + 1), g, h * DH:(h + 1) * DH],
                                            ps[0:CP, 6, P + g * DH:P + (g + 1) * DH])
                ins.then_inc(bd_ok, 1)

            for v in range(U_IN):
                for n in {7: [0], 10: [1, 2], 12: [3, 4], 15: [5]}.get(v, []):
                    rot_low(n)
                if 8 <= v <= 11:
                    flat_add(v - 8)
                if v == 8:
                    mod_rows(3, ga1, 0)
                if v == 10:
                    mod_rows(4, ga1, 1)
                if v == 13:
                    compressed()
                if v == 14:
                    mod_columns(5, 2, 48, 16)
                if v == 16:
                    d.wait_ge(kcT_hi, 1)
                    d.tensor_tensor(KCl[:, :], ps[:, 7, 0:CP], KCh[:, :].bitcast(F32), ALU.subtract).then_inc(kcT_lo, 1)
                if v == 18:
                    mod_columns(6, 3, 40, None)
                if v == 22:
                    mod_rows(7, ga2, 0)
                if v == 23:
                    mod_rows(8, ga2, 1)
                if 4 <= v and v // UPC - 1 <= K_RQK and v % UPC < 2:
                    rope_chunk(v // UPC - 1, (0, 1) if v % UPC == 0 else (2, 3))
                for j in ada_after.get(v + 3, []):
                    ada(j)

            def row_min(n):
                w = (n // 16 + 1) * P
                d.wait_ge(s_ps, n + 1)
                if n >= 8:
                    d.wait_ge(p_exp, n - 7)
                d.tensor_reduce(mn[:, n % 8:n % 8 + 1], ps[:, n % 2, 0:w], AX.X, ALU.min).then_inc(s_min, 1)

            def heads_view(ap, n=NH):
                return ap.rearrange("p (h x) -> p h x", h=n)

            def add_branch(i, b):
                d.wait_ge(pv, 16 * i + 8 * b)
                then(d.reciprocal(rgt[:, :], den[:, i % 2, b - 1, :]))
                then(d.tensor_tensor(rgt[:, :], rgt[:, :], gates[:, i, b * NH:(b + 1) * NH], ALU.mult))
                then(d.tensor_tensor(heads_view(tmpo[:, :]), heads_view(ps[:, 3 + b, :]),
                                     rgt[:, :].unsqueeze(2).broadcast_to([P, NH, DH]), ALU.mult))
                y = mix[:, i % 2, 512:1024]
                d.tensor_tensor(y, y, tmpo[:, :], ALU.add).then_inc(y_sum, 1)
                d.wait_ge(y_sum, 3 * i + b + 1)

            def cmp_scores(i):
                d.wait_ge(cs_ps, i + 1)
                for g in range(NG):
                    ins = d.tensor_tensor(sc[:, g * HPG:(g + 1) * HPG, :], ps[:, 6 + g, 0:P].rearrange("p (h n) -> p h n", h=HPG),
                                          cmask[:, i, :].unsqueeze(1).broadcast_to([P, HPG, CP]), ALU.add)
                then(ins)
                then(d.tensor_reduce(mnc[:, :], sc[:, :, :], AX.X, ALU.min))
                d.tensor_tensor(sc[:, :, :], sc[:, :, :], mnc[:, :].unsqueeze(2).broadcast_to([P, NH, CP]), ALU.subtract).then_inc(c_pre, 1)

            def cmp_out(i):
                d.wait_ge(c_exp, i + 1)
                then(d.tensor_reduce(mnc[:, :], pc[:, :, :], AX.X, ALU.add))
                then(d.reciprocal(mnc[:, :], mnc[:, :]))
                then(d.tensor_tensor(mnc[:, :], mnc[:, :], gates[:, i, 0:NH], ALU.mult))
                if i == 0:
                    then(d.tensor_scalar(mnc[:, :], mnc[:, :], cst[:, K_VALID:K_VALID + 1], None, ALU.mult))
                d.wait_ge(c_o, i + 1)
                if i >= 2:
                    d.wait_ge(mixT_ps, i - 1)
                d.tensor_tensor(heads_view(mix[:, i % 2, 512:1024]), heads_view(ps[:, 7, :]),
                                mnc[:, :].unsqueeze(2).broadcast_to([P, NH, DH]), ALU.mult).then_inc(y_sum, 1)
                d.wait_ge(y_sum, 3 * i + 1)

            def ret_decay(i, h):
                d.wait_ge(r_s, RH * i + h + 1)
                if i == 0 and h == 0:
                    d.wait_ge(decay_in, 16)
                if RH * i + h >= 2:
                    d.wait_ge(r_y, RH * i + h - 1)
                w = (i + 1) * P
                d.tensor_tensor(ats[:, h % 2, 0:w], ps[:, 6, 0:w], decay[:, h, (TT - 1 - i) * P:TT * P], ALU.mult).then_inc(r_dec, 1)

            def ret_norm(i):
                d.wait_ge(r_sq, i + 1)
                d.tensor_scalar(yss[:, :], yss[:, :], 1.0 / RDV, EPS, ALU.mult, ALU.add).then_inc(var_ok, 1)
                d.wait_ge(rstd_ok, N_RET + i)
                then(d.tensor_tensor(heads_view(tmpo[:, :], RH), heads_view(ps[:, 7, :], RH),
                                     yss[:, :].unsqueeze(2).broadcast_to([P, RH, RDV]), ALU.mult))
                if i == 0:
                    d.wait_ge(proj_ev, TT * 6)
                d.tensor_tensor(mix[:, i % 2, 0:512], tmpo[:, :], rg[:, i, :], ALU.mult).then_inc(r_norm, 1)
                d.wait_ge(r_norm, i + 1)

            def mix_low(i):
                d.wait_ge(mix_hi, i + 1)
                d.tensor_tensor(hTl[:, :, i * P:(i + 1) * P], ps[:, 6:8, :].rearrange("p b (k q) -> p (b k) q", k=4),
                                hTh[:, :, i * P:(i + 1) * P].bitcast(F32), ALU.subtract).then_inc(mix_lo, 1)

            for n in range(16 * TT + 6):
                i, s = divmod(n, 16)
                if n < 16 * TT:
                    row_min(n)
                if s == 1 and i >= 1:
                    ret_norm(i - 1)
                if s == 3 and i >= 1:
                    add_branch(i - 1, 2)
                if s == 5 and i >= 1:
                    mix_low(i - 1)
                if s == 6 and i < TT:
                    cmp_scores(i)
                if s == 11:
                    cmp_out(i)
                    add_branch(i, 1)
                if s >= 12:
                    ret_decay(i, s - 12)

            def residual(t):
                d.wait_ge(d_ps, t + 1)
                for b in range(2):
                    h = slice(b * 512, (b + 1) * 512)
                    ins = d.tensor_tensor(tmp[:, h], ps[:, 2 * t + b, :], ga1[:, h], ALU.mult)
                then(ins)
                d.wait_ge(xagain_in, 16 * TT)
                d.tensor_tensor(x1[:, t, :], x1[:, t, :], tmp[:, :], ALU.add).then_inc(x1_ok, 1)
                d.wait_ge(sq2, t + 1)
                d.tensor_scalar(rstd[:, t:t + 1], ssq[:, t:t + 1], 1.0 / D, EPS, ALU.mult, ALU.add).then_inc(var_ok, 1)
                d.wait_ge(rstd_ok, N_X1 + t)
                d.tensor_scalar(xb[:, t % 2, :], x1[:, t, :], rstd[:, t:t + 1], None, ALU.mult).then_inc(xb_ok, 1)

            def modulate(t):
                for b in range(2):
                    d.wait_ge(xbT, 2 * t + b + 1)
                    if t:
                        d.wait_ge(h2_lo, 2 * (t - 1) + b + 1)
                    ks = slice(4 * b, 4 * b + 4)
                    then(d.tensor_tensor(h2[:, b], ps[:, 2 * t + b, :].rearrange("p (k q) -> p k q", k=4),
                                         mods[:, 2, ks].unsqueeze(2).broadcast_to([P, 4, P]), ALU.mult))
                    d.tensor_tensor(h2[:, b], h2[:, b], mods[:, 3, ks].unsqueeze(2).broadcast_to([P, 4, P]), ALU.add).then_inc(h2_ok, 1)
                for b in range(2):
                    ks = slice(4 * b, 4 * b + 4)
                    d.wait_ge(h2_hi, 2 * t + b + 1)
                    d.tensor_tensor(hTl[:, ks, t * P:(t + 1) * P], h2[:, b], hTh[:, ks, t * P:(t + 1) * P].bitcast(F32),
                                    ALU.subtract).then_inc(h2_lo, 1)

            residual(0)
            for t in range(TT):
                if t < TT - 1:
                    residual(t + 1)
                modulate(t)

            for f in range(FT):
                d.wait_ge(sg_ok, f + 1)
                d.wait_ge(up_ps, f + 1)
                d.tensor_tensor(act[:, f, :], ps[:, 2 * (f % 2) + 1, :], sg[:, f % 2, :], ALU.mult).then_inc(act_ok, 1)
            for f in range(FT):
                d.wait_ge(a_hi, f + 1)
                d.tensor_tensor(al[:, f % SPLIT, :], act[:, f, :], ah[:, f % SPLIT, :].bitcast(F32), ALU.subtract).then_inc(a_lo, 1)
            d.wait_ge(gfin_in, 16)
            for t in range(TT):
                d.wait_ge(d_ps, TT + t + 1)
                for b in range(2):
                    h = slice(b * 512, (b + 1) * 512)
                    ins = d.tensor_tensor(tmp[:, h], ps[:, 2 * t + b, :], ga2[:, h], ALU.mult)
                then(ins)
                d.tensor_tensor(x1[:, t, :], x1[:, t, :], tmp[:, :], ALU.add).then_inc(x2_ok, 1)
                d.wait_ge(sq3, t + 1)
                d.tensor_scalar(rstd[:, t:t + 1], ssq[:, t:t + 1], 1.0 / D, EPS, ALU.mult, ALU.add).then_inc(var_ok, 1)
                d.wait_ge(rstd_ok, N_X2 + t)
                d.scalar_tensor_tensor(xb[:, t % 2, :], x1[:, t, :], rstd[:, t:t + 1], gfin[:, :], ALU.mult, ALU.mult).then_inc(y_ok, 1)

        @block.tensor
        def _(pe):
            mm = pe.matmul

            def product(o, ah_, al_, bh_, bl_, first, last):
                mm(o, ah_, bh_, start=first, stop=False)
                mm(o, ah_, bl_, start=False, stop=False)
                return mm(o, al_, bh_, start=False, stop=last)

            pe.wait_ge(const_in, 16)
            pe.wait_ge(rows_in, 16 * 7)
            pe.transpose(ps[:, 4, 0:P], rows[:, :], ident).then_inc(rowsT, 1)
            for k in range(KT):
                if k >= 4:
                    pe.wait_ge(xT_ok, k - 3)
                for t in range(TT):
                    if k == 0:
                        pe.wait_ge(xn_done, t + 1)
                    ins = pe.transpose(ps[:, k % 4, t * P:(t + 1) * P], xs[:, t, k * P:(k + 1) * P], ident)
                ins.then_inc(xT_ps, 1)

            def sum_columns(g, n):
                pe.wait_ge(ada_used, KT * (g + 1))
                bank = min(4 + n, 7)
                for k in range(KT):
                    ins = mm(ps[:, bank, (n - 1) * KT + k:(n - 1) * KT + k + 1], acc[:, g % 2, k * P:(k + 1) * P], ones[:, 0:1],
                             start=True, stop=True)
                ins.then_inc(mod_sum, 1)

            def sum_rows(g, half):
                pe.wait_ge(ada_used, KT * (g + 1))
                mm(ps[:, 7, :], ones[:, :], acc[:, g % 2, half * 512:(half + 1) * 512], start=True, stop=True).then_inc(mod_sum, 1)

            pe.wait_ge(ones_set, 2)
            sum_columns(0, 1)
            sum_columns(1, 2)

            def flat_transposes(b):
                if b == 0:
                    pe.wait_ge(flat_in, 16 * 8)
                else:
                    pe.wait_ge(flatT_ok, b)
                for j in range(4):
                    ins = pe.transpose(ps[:, 6, j * P:(j + 1) * P], flat[:, (4 * b + j) * P:(4 * b + j + 1) * P], ident)
                ins.then_inc(flatT_ps, 1)

            def rot_transposes(n):
                if n >= 2:
                    pe.wait_ge(rot_hi, n - 1)
                    pe.wait_ge(rot_lo, min(n - 1, 6))
                if n == 0 or n == 5:
                    pe.wait_ge(roped, TT if n == 0 else 3 * TT)
                    for t in range(TT):
                        ins = pe.transpose(ps[:, 4 + n % 2, t * P:(t + 1) * P], rot[:, t, 0:P], ident)
                else:
                    t = n - 1 if n < 5 else n - 6
                    pe.wait_ge(roped, (TT if n < 5 else 3 * TT) + t + 1)
                    for h in range(4):
                        ins = pe.transpose(ps[:, 4 + n % 2, h * P:(h + 1) * P], rot[:, t, h * P:(h + 1) * P], ident)
                ins.then_inc(rotT, 1)

            for v in range(U_IN):
                ch, q = divmod(v, UPC)
                n = CHUNKS[ch][1]
                s = v % SPLIT
                pe.wait_ge(w_lo, v + 1)
                bh = wh[:, s, 0:2 * n].rearrange("p (k n) -> p k n", k=2)
                bl = wl[:, s, 0:2 * n].rearrange("p (k n) -> p k n", k=2)
                for t in range(TT):
                    if ch and q == 0:
                        pe.wait_ge(proj_ev, TT * (ch - 1) + t + 1)
                    for kk in range(2):
                        k = 2 * q + kk
                        if ch == 0 and t == 0:
                            pe.wait_ge(h_lo, k + 1)
                        tok = slice(t * P, (t + 1) * P)
                        ins = product(ps[:, t, 0:n], hTh[:, k, tok], hTl[:, k, tok], bh[:, kk, :], bl[:, kk, :], k == 0, k == KT - 1)
                    if q == UPC - 1 and t < TT - 1:
                        ins.then_inc(o_ps, 1)
                ins.then_inc(unit_used, 1)
                for m in {6: [0], 9: [1, 2], 11: [3, 4], 14: [5], 17: [6, 7], 18: [8, 9]}.get(v, []):
                    rot_transposes(m)
                if 7 <= v <= 10:
                    flat_transposes(v - 7)
                if v == 7:
                    sum_rows(2, 0)
                if v == 9:
                    pe.wait_ge(mod_read, 3)
                    sum_rows(2, 1)
                if v == 11:
                    pe.wait_ge(flatT_ok, 4)
                    pe.wait_ge(w1_in, 32)
                    pe.wait_ge(mod_read, 4)
                    for kv in range(2):
                        for j in range(CL // 2):
                            ins = mm(ps[:, 7, kv * 2 * CP:(kv + 1) * 2 * CP], w1[:, kv, j, :], flatT[:, j, kv * 2 * CP:(kv + 1) * 2 * CP],
                                     start=j == 0, stop=j == CL // 2 - 1)
                    ins.then_inc(mlp1, 1)
                if v == 12:
                    pe.wait_ge(mlp1_silu, 1)
                    pe.wait_ge(w2_in, 32)
                    for kv in range(2):
                        for g in range(NG):
                            ins = mm(ps[0:CP, 6, kv * P + g * DH:kv * P + (g + 1) * DH], hs[:, kv, g * CP:(g + 1) * CP], w2[:, kv, :],
                                     start=True, stop=True)
                    ins.then_inc(mlp2, 1)
                if v == 13:
                    sum_columns(3, 5)
                if v == 15:
                    pe.wait_ge(kc_rot, 1)
                    pe.wait_ge(mod_read, 5)
                    pe.transpose(ps[:, 7, 0:CP], kcr[:, :], ident[0:CP, 0:CP]).then_inc(kcT, 1)
                if v == 17:
                    pe.wait_ge(kcT_lo, 1)
                    sum_columns(4, 6)
                if v == 21:
                    pe.wait_ge(mod_read, 6)
                    sum_rows(5, 0)
                if v == 22:
                    pe.wait_ge(mod_read, 7)
                    sum_rows(5, 1)

            def scores(n):
                i = n // 16
                b, hd = divmod(n % 16, 8)
                h, g = divmod(hd, 2)
                w = (i + 1) * P
                if n >= 2:
                    pe.wait_ge(p_exp, n - 1)
                g0, g1 = g * DH, (g + 1) * DH
                qs = slice(i * P, (i + 1) * P)
                o = ps[:, n % 2, 0:w]
                product(o, QTh[g0:g1, h, qs], QTl[g0:g1, h, qs], KTh[g0:g1, b, 0:w], KTl[g0:g1, b, 0:w], True, False)
                mm(ps[:, n % 2, i * P:w], identR[:, :], maskR[:, :], start=False, stop=True).then_inc(s_ps, 1)

            def transposes(n):
                i = n // 16
                pe.wait_ge(p_exp, n + 1)
                if n >= 2:
                    pe.wait_ge(pT_ok, n - 1)
                for j in range(i + 1):
                    ins = pe.transpose(ps[:, 2 + n % 2, j * P:(j + 1) * P], Pr[:, n % 3, j * P:(j + 1) * P], ident)
                ins.then_inc(p_T, 1)

            def values(n):
                i = n // 16
                b, hd = divmod(n % 16, 8)
                h, g = divmod(hd, 2)
                head = g * HPG + h
                pe.wait_ge(pT_ok, n + 1)
                if hd == 0 and i:
                    pe.wait_ge(y_sum, 3 * (i - 1) + b + 2)
                for j in range(i + 1):
                    ins = mm(ps[:, 4 + b, head * DH:(head + 1) * DH], PT[:, n % 2, j * P:(j + 1) * P],
                             V[:, j, b, g * DH:(g + 1) * DH], start=j == 0, stop=j == i)
                ins.then_inc(pv, 1)

            def cmp_scores(i):
                if i == 0:
                    pe.wait_ge(kcT_lo, 1)
                    pe.wait_ge(mod_read, 8)
                else:
                    pe.wait_ge(mix_lo, i)
                qs = slice(i * P, (i + 1) * P)
                for g in range(NG):
                    g0, g1 = g * DH, (g + 1) * DH
                    for h in range(HPG):
                        ins = product(ps[:, 6 + g, h * CP:(h + 1) * CP], QTh[g0:g1, h, qs], QTl[g0:g1, h, qs],
                                      KCh[g0:g1, :], KCl[g0:g1, :], True, True)
                ins.then_inc(cs_ps, 1)

            def ret_scores(i, h):
                p0 = (h % 2) * RDK
                if h == 0:
                    pe.wait_ge(cT_ok, i + 1)
                if RH * i + h:
                    pe.wait_ge(r_dec, RH * i + h)
                for j in range(i + 1):
                    ins = mm(ps[:, 6, j * P:(j + 1) * P], rkT[p0:p0 + RDK, h // 2, j * P:(j + 1) * P],
                             rqT[p0:p0 + RDK, h // 2, i * P:(i + 1) * P], start=True, stop=True)
                ins.then_inc(r_s, 1)

            def ret_values(i, h):
                pe.wait_ge(r_dec, RH * i + h + 1)
                if h == 0:
                    pe.wait_ge(y_sum, 3 * i + 1)
                for j in range(i + 1):
                    ins = mm(ps[:, 7, h * P:(h + 1) * P], ats[:, h % 2, j * P:(j + 1) * P], rv[:, j, h * P:(h + 1) * P],
                             start=j == 0, stop=j == i)
                ins.then_inc(r_y, 1)

            pe.wait_ge(proj_ev, TT * 6)
            pe.wait_ge(rot_hi, 10)
            for n in range(16 * TT + 6):
                i, s = divmod(n, 16)
                if n < 16 * TT:
                    scores(n)
                if 2 <= n <= 16 * TT + 1:
                    transposes(n - 2)
                if 3 <= n <= 16 * TT + 2:
                    values(n - 3)
                if s == 0 and i >= 1:
                    ret_values(i - 1, RH - 1)
                if s == 4 and i >= 1:
                    pe.wait_ge(y_sum, 3 * i)
                    pe.wait_ge(r_norm, i)
                    for k in range(KT):
                        ins = pe.transpose(ps[:, 6 + k // 4, (k % 4) * P:(k % 4 + 1) * P], mix[:, (i - 1) % 2, k * P:(k + 1) * P], ident)
                    ins.then_inc(mixT_ps, 1)
                if s == 6 and i < TT:
                    cmp_scores(i)
                if s == 8 and i < TT:
                    pe.wait_ge(c_exp, i + 1)
                    for g in range(NG):
                        ins = pe.transpose(ps[:, 6, g * P:(g + 1) * P], pc[:, g * HPG:(g + 1) * HPG, :], ident)
                    ins.then_inc(c_T, 1)
                if s == 10 and i < TT:
                    pe.wait_ge(cT_ok, i + 1)
                    pe.wait_ge(bd_ok, 1)
                    for g in range(NG):
                        ins = mm(ps[:, 7, g * 256:(g + 1) * 256], pcT[:, g, :], BD[:, g, :], start=True, stop=True)
                    ins.then_inc(c_o, 1)
                if s >= 12:
                    ret_scores(i, s - 12)
                if s >= 13:
                    ret_values(i, s - 13)

            def two_halves(t, u, last_unit, stat, first, last):
                s = u % SPLIT
                for b in range(2):
                    cols_ = slice(b * 512, (b + 1) * 512)
                    ins = product(ps[:, 2 * t + b, :], stat[0], stat[1], wh[:, s, cols_], wl[:, s, cols_], first, last)
                return ins

            pe.wait_ge(mix_lo, TT)
            for k in range(KT - TAIL):
                pe.wait_ge(w_lo, U0_OUT + k + 1)
                for t in range(TT):
                    tok = slice(t * P, (t + 1) * P)
                    ins = two_halves(t, U0_OUT + k, False, (hTh[:, k, tok], hTl[:, k, tok]), k == 0, False)
                ins.then_inc(unit_used, 1)
            pe.wait_ge(w_lo, U0_OUT + KT)

            def h2_transposes(t):
                pe.wait_ge(xb_ok, t + 1)
                for b in range(2):
                    for k in range(4):
                        ins = pe.transpose(ps[:, 2 * t + b, k * P:(k + 1) * P], xb[:, t % 2, (4 * b + k) * P:(4 * b + k + 1) * P], ident)
                    ins.then_inc(xbT, 1)

            for t in range(TT):
                tok = slice(t * P, (t + 1) * P)
                for k in range(KT - TAIL, KT):
                    ins = two_halves(t, U0_OUT + k, False, (hTh[:, k, tok], hTl[:, k, tok]), False, k == KT - 1)
                ins.then_inc(d_ps, 1)
                if t >= 2:
                    h2_transposes(t - 2)
            for t in range(2, TT):
                h2_transposes(t)

            for f in range(FT):
                for up in range(2):
                    u = U0_GU + 2 * f + up
                    s = u % SPLIT
                    pe.wait_ge(w_lo, u + 1)
                    if f == 0:
                        pe.wait_ge(h2_lo, 2 * TT)
                    if f >= 2:
                        pe.wait_ge(act_ok, f - 1)
                    for k in range(KT):
                        ks = slice(k * P, (k + 1) * P)
                        o = ps[:, 2 * (f % 2) + up, :]
                        mm(o, wh[:, s, ks], hTh[:, k, :], start=k == 0, stop=False)
                        mm(o, wh[:, s, ks], hTl[:, k, :], start=False, stop=False)
                        ins = mm(o, wl[:, s, ks], hTh[:, k, :], start=False, stop=k == KT - 1)
                    ins.then_inc(up_ps if up else gate_ps, 1)

            pe.wait_ge(act_ok, FT)
            for f in range(FT - SPLIT):
                pe.wait_ge(w_lo, U0_DOWN + f + 1)
                pe.wait_ge(a_lo, f + 1)
                for t in range(TT):
                    tok = slice(t * P, (t + 1) * P)
                    ins = two_halves(t, U0_DOWN + f, False, (ah[:, f % SPLIT, tok], al[:, f % SPLIT, tok]), f == 0, False)
                ins.then_inc(a_used, 1)
            pe.wait_ge(w_lo, UNITS)
            pe.wait_ge(a_lo, FT)
            for t in range(TT):
                tok = slice(t * P, (t + 1) * P)
                for f in range(FT - SPLIT, FT):
                    ins = two_halves(t, U0_DOWN + f, False, (ah[:, f % SPLIT, tok], al[:, f % SPLIT, tok]), False, f == FT - 1)
                ins.then_inc(d_ps, 1)


def shape_constants():
    k = np.zeros((P, K_N), np.float32)
    k[:, K_ID:K_ID + P] = np.eye(P, dtype=np.float32)
    q = np.arange(P)
    k[:, K_MASK:K_MASK + P] = np.where(q[None, :] > q[:, None], BIG, 0.0)

    def rope_rows(pos):
        half = DH // 2
        inv = np.float32(10000.0) ** (-np.arange(half, dtype=np.float32) / np.float32(half))
        ang = pos.astype(np.float32)[:, None] * inv
        cos, sin = np.cos(ang), np.sin(ang)
        return np.concatenate([cos, cos, -sin, sin], axis=1)

    r = rope_rows(np.arange(T))
    k[:, K_ROPE:K_ROPE + TT * P] = r.reshape(TT, P, P).transpose(1, 0, 2).reshape(P, TT * P)
    end = np.arange(CP) * CS + CL - 1
    seen = (end[None, :] <= np.arange(T)[:, None]) & (np.arange(CP) < NC)[None, :]
    m = np.where(seen, 0.0, BIG).astype(np.float32)
    k[:, K_CMASK:K_CMASK + TT * CP] = m.reshape(TT, P, CP).transpose(1, 0, 2).reshape(P, TT * CP)
    k[:, K_VALID] = (q >= CL - 1)
    k[0:CP, K_CROPE:K_CROPE + P] = rope_rows(end)
    log_g = np.log(1.0 - 2.0 ** (-5.0 - np.arange(RH)))
    x = np.arange(T)
    diff = (TT - 1 - x[None, :] // P) * P + x[None, :] % P - q[:, None]
    dec = np.where(diff[None] >= 0, np.exp(log_g[:, None, None] * np.maximum(diff, 0)[None]), 0.0)
    return k, np.ascontiguousarray(dec.transpose(1, 0, 2)).astype(np.float32)


_INS = ['x', 'c', 'ln_mix_g', 'ln_ffn_g', 'w_ada', 'b_ada', 'w_in', 'cmp_pe_k', 'cmp_w1_k', 'cmp_w2_k',
        'cmp_pe_v', 'cmp_w1_v', 'cmp_w2_v', 'w_out', 'w_ff_gate', 'w_ff_up', 'w_ff_down', 'ln_final_g']


def kernel(**inputs):
    import numpy as _np
    import concourse.bacc as _bacc
    from concourse import mybir as _mybir
    from concourse.bass_utils import run_bass_kernel_spmd as _run

    nc = _bacc.Bacc("TRN2", target_bir_lowering=False, num_devices=1)
    arrays, args = {}, []
    for name in _INS:
        a = _np.ascontiguousarray(inputs[name])
        if name != 'ln_final_g':
            a = a[0]
        arrays[f"in_{name}"] = a
        args.append(nc.dram_tensor(f"in_{name}", a.shape, _mybir.dt.from_np(a.dtype), kind="ExternalInput").ap())
    for name, a in zip(("consts", "decays"), shape_constants()):
        arrays[f"in_{name}"] = a
        args.append(nc.dram_tensor(f"in_{name}", a.shape, _mybir.dt.float32, kind="ExternalInput").ap())
    args.append(nc.dram_tensor("out_0", (T, D), _mybir.dt.float32, kind="ExternalOutput").ap())
    block_kernel(nc, *args)
    r = _run(nc, [arrays], core_ids=[0])
    return r.results[0]["out_0"].reshape(1, T, D)
```

```python
from contextlib import ExitStack

import numpy as np

import concourse.bass as bass
from concourse import mybir

F32 = mybir.dt.float32
F32R = mybir.dt.float32r
ALU = mybir.AluOpType
ACT = mybir.ActivationFunctionType
AX = mybir.AxisListType

P = 128
T, D, DFF = 512, 1024, 2816
TT, KT, FT = T // P, D // P, DFF // P
RH, RDK, RDV = 4, 64, 128
NH, NG, HPG, DH = 8, 2, 4, 64
CL, CS, CHID = 32, 16, 128
NC = T // CS - CL // CS + 1
CP = 32
EPS = 1e-6
BIG = 1e30
QSCALE = -(DH ** -0.5)

C_CMP = 2048
C_Q = 1536
C_WIN = 2560
C_RQK = 0
C_RV = 512
C_RG = 1024
CHUNKS = [(C_CMP, 512), (C_Q, 512), (C_WIN, 280), (C_RQK, 512), (C_RG, 512), (C_RV, 512)]
K_CMP, K_Q, K_WIN, K_RQK, K_RG, K_RV = range(6)
UPC = 4
U_PROJ = UPC * K_RV
U_IN, U_OUT, U_GU, U_DOWN = UPC * len(CHUNKS), KT, 2 * FT, FT
U0_OUT = U_IN
U0_GU = U0_OUT + U_OUT
U0_DOWN = U0_GU + U_GU
UNITS = U0_DOWN + U_DOWN
TAIL = 3
RV_STEPS = 16
SPLIT = 4
RAW = 7
EARLY = 8

ADA = [1, 0, 2, 4, 3, 5]
ADA_START = 16
ADA_LATE = 5 * KT
ADA_OPS = 4 * ADA_START

K_ID, K_MASK, K_ROPE, K_CMASK, K_VALID, K_CROPE = 0, 128, 256, 768, 896, 900
K_N = 1028


def stream():
    items = []
    for q in range(UPC):
        items += [("early", 4 * q + j) for j in range(4)] + [("w", q)]
    a = ADA_START
    for u in range(3, UNITS):
        if u > 3:
            items.append(("w", u))
        if u <= U_PROJ:
            upto = ADA_START - (-(ADA_LATE - ADA_START) * (u - 2) // (U_PROJ - 2))
        else:
            upto = min(KT * len(ADA), a + 2)
        while a < upto:
            items.append(("ada", a))
            a += 1
    return items


def block_kernel(nc, x, c, ln_mix_g, ln_ffn_g, w_ada, b_ada, w_in, cmp_pe_k, cmp_w1_k, cmp_w2_k,
                 cmp_pe_v, cmp_w1_v, cmp_w2_v, w_out, w_ff_gate, w_ff_up, w_ff_down, ln_final_g,
                 consts, decays, out):
    items = stream()
    ring = [it for it in items if it[0] != "early"]
    place = {it: (n % RAW, 16 * (n // RAW + 1)) for n, it in enumerate(ring)}
    ada_after = {}
    last_w = -1
    for kind, j in items:
        if kind == "w":
            last_w = j
        elif kind == "ada" and j < ADA_LATE:
            ada_after.setdefault(last_w, []).append(j)

    def ada_ops(j):
        return 8 * (j // 2 + 1) - (j + 1) % 2 if j < ADA_START else ADA_OPS + j - ADA_START + 1

    with ExitStack() as ctx:
        KB = 1024
        BASE = 16512

        def at(name, shape, dt, kb):
            return nc.alloc_sbuf_tensor_at(name, shape, dt, offset=BASE + int(kb * KB))

        small_at = [112 * KB + 4128]

        def small(name, shape, dt=F32):
            kb = small_at[0] / KB
            small_at[0] += (4 * int(np.prod(shape[1:])) + 31) // 32 * 32
            return at(name, shape, dt, kb)

        hTh = at("hTh", [P, KT, T], F32R, 0)
        hTl = at("hTl", [P, KT, T], F32R, 16)
        ga1 = at("ga1", [P, D], F32, 32)
        ga2 = at("ga2", [P, D], F32, 36)
        gfin = at("gfin", [P, D], F32, 40)
        acc2 = at("acc2", [P, D], F32, 40)
        flatT = at("flatT", [P, CL // 2, P], F32, 36)
        wh = at("wh", [P, SPLIT, D], F32R, 44)
        wl = at("wl", [P, SPLIT, D], F32R, 60)
        raw = at("raw", [P, RAW, D], F32, 76)
        acc = at("acc", [P, 2, D], F32, 104)
        cst = at("cst", [P, K_N], F32, 112)
        R = 122
        xT = at("xT", [P, KT, T], F32, R)
        early = at("early", [P, EARLY, D], F32, R + 16)
        xs = at("xs", [P, TT, D], F32, R + 54)
        hf = at("hf", [P, 2, T], F32, R + 70)
        junk = at("junk", [P, D], F32, R + 74)
        QTh = at("QTh", [P, HPG, T], F32R, R)
        QTl = at("QTl", [P, HPG, T], F32R, R + 8)
        KTh = at("KTh", [P, 2, T], F32R, R + 16)
        KTl = at("KTl", [P, 2, T], F32R, R + 20)
        V = at("V", [P, TT, 2, P], F32, R + 24)
        rqT = at("rqT", [P, 2, T], F32, R + 28)
        rkT = at("rkT", [P, 2, T], F32, R + 32)
        w1 = at("w1", [P, 2, CL // 2, CHID], F32, R + 36)
        rv = at("rv", [P, TT, RH * RDV], F32, R + 36)
        rg = at("rg", [P, TT, RH * RDV], F32, R + 44)
        stage = at("stage", [P, TT, 512], F32, R + 54)
        rot = at("rot", [P, TT, 512], F32, R + 62)
        rt = at("rt", [P, 2, 512], F32, R + 70)
        flat = at("flat", [P, CL * DH], F32, R + 74)
        Pr = at("Pr", [P, 3, T], F32, R + 54)
        PT = at("PT", [P, 2, T], F32, R + 60)
        mix = at("mix", [P, 2, D], F32, R + 64)
        ats = at("ats", [P, 2, T], F32, R + 72)
        decay = at("decay", [P, RH, T], F32, R + 76)
        sc = at("sc", [P, NH, CP], F32, 104)
        pc = at("pc", [P, NH, CP], F32, 105)
        pcT = at("pcT", [P, NG, P], F32, 106)
        tmpo = at("tmpo", [P, T], F32, 107)
        sqj = at("sqj", [P, T], F32, 109)
        x1 = at("x1", [P, TT, D], F32, R)
        act = at("act", [P, FT, T], F32, R + 16)
        ah = at("ah", [P, SPLIT, T], F32R, R + 60)
        al = at("al", [P, SPLIT, T], F32R, R + 68)
        xb = at("xb", [P, 2, D], F32, R + 76)
        sg = at("sg", [P, 2, T], F32, R + 76)
        h2 = at("h2", [P, 2, 4, P], F32, 108)
        BD = small("BD", [P, NG, HPG * DH])
        w2 = small("w2", [P, 2, DH])
        identR = small("identR", [P, P], F32R)
        maskR = small("maskR", [P, P], F32R)
        KCh = small("KCh", [P, CP], F32R)
        KCl = small("KCl", [P, CP], F32R)
        rows = at("rows", [P, P], F32, 108)
        cols = small("cols", [P, 88])
        cs = small("cs", [P, KT])
        mods = small("mods", [P, 4, KT])
        ones = at("ones", [P, P], F32, R + 52)
        ssq = small("ssq", [P, TT])
        rstd = small("rstd", [P, TT])
        expo = small("expo", [P, TT])
        mn = small("mn", [P, 8])
        den = small("den", [P, 2, 2, NH])
        gates = small("gates", [P, TT, 3 * NH])
        rgt = small("rgt", [P, NH])
        mnc = small("mnc", [P, NH])
        yss = small("yss", [P, RH])
        hs = small("hs", [P, 2, 2 * CP])
        assert small_at[0] <= 122 * KB, small_at[0] / KB
        kcr = at("kcr", [CP, P], F32, R + 52.5)

        ident = cst[:, K_ID:K_ID + P]
        rope = cst[:, K_ROPE:K_ROPE + TT * P].rearrange("p (t n) -> p t n", t=TT)
        cmask = cst[:, K_CMASK:K_CMASK + TT * CP].rearrange("p (t n) -> p t n", t=TT)

        ps = ctx.enter_context(nc.psum_tensor("ps", [P, 8, 512], F32))

        kv_dram = nc.dram_tensor("kv_scratch", (T, 2 * P), F32, kind="Internal").ap()

        def sem(name):
            return ctx.enter_context(nc.semaphore(name))

        raw_in = [sem(f"raw_in{i}") for i in range(RAW)]
        early_in = [sem(f"early_in{i}") for i in range(EARLY)]
        rows_in, biases_in, ident_in, const_in, w1_in, w2_in = sem("rows_in"), sem("biases_in"), sem("ident_in"), sem("const_in"), sem("w1_in"), sem("w2_in")
        bias1_in, bias2_in = sem("bias1_in"), sem("bias2_in")
        gfin_in, decay_in, flat_in = sem("gfin_in"), sem("decay_in"), sem("flat_in")
        x_in = [sem(f"x_in{t}") for t in range(TT)]
        xagain_in, kv_out = sem("xagain_in"), sem("kv_out")
        out_done = [sem(f"out_done{t}") for t in range(TT)]
        w_hi, w_lo, unit_used, ada_used = sem("w_hi"), sem("w_lo"), sem("unit_used"), sem("ada_used")
        ones_set, rowsT, cols_ok, c_silu, mod_sum, mod_read = (sem(n) for n in ("ones_set", "rowsT", "cols_ok", "c_silu", "mod_sum", "mod_read"))
        w_scaled = sem("w_scaled")
        h2b_ok, sqv_done = sem("h2b_ok"), sem("sqv_done")
        h_full = sem("h_full")
        sq_done, xn_done, xT_ps, xT_ok, h_hi, h_lo = (sem(n) for n in ("sq_done", "xn_done", "xT_ps", "xT_ok", "h_hi", "h_lo"))
        proj_ev, roped, rotT, rot_hi, rot_lo = (sem(n) for n in ("proj_ev", "roped", "rotT", "rot_hi", "rot_lo"))
        flat_zero, flatT_ps, flatT_ok, mlp1, mlp1_silu, mlp2, kc_rot, bd_ok, kcT, kcT_hi, kcT_lo = (
            sem(n) for n in ("flat_zero", "flatT_ps", "flatT_ok", "mlp1", "mlp1_silu", "mlp2", "kc_rot", "bd_ok", "kcT", "kcT_hi", "kcT_lo"))
        consts_r, var_ok, rstd_ok = sem("consts_r"), sem("var_ok"), sem("rstd_ok")
        N_X, N_RET, N_X1, N_X2 = 1, 2, 2 + TT, 2 + 2 * TT
        s_ps, s_min, p_exp, p_T, pT_ok, pv = (sem(n) for n in ("s_ps", "s_min", "p_exp", "p_T", "pT_ok", "pv"))
        cs_ps, c_pre, c_exp, c_den, c_T, cT_ok, c_o = (sem(n) for n in ("cs_ps", "c_pre", "c_exp", "c_den", "c_T", "cT_ok", "c_o"))
        y_sum, r_s, r_dec, r_y, r_sq, r_norm = (sem(n) for n in ("y_sum", "r_s", "r_dec", "r_y", "r_sq", "r_norm"))
        mixT_ps, mix_hi, mix_lo = (sem(n) for n in ("mixT_ps", "mix_hi", "mix_lo"))
        o_ps, x1_ok, sq2, xb_ok, xbT, h2_ok, h2_hi, h2_lo = (sem(n) for n in ("o_ps", "x1_ok", "sq2", "xb_ok", "xbT", "h2_ok", "h2_hi", "h2_lo"))
        gate_ps, up_ps, sg_ok, act_ok, a_hi, a_lo, a_used = (sem(n) for n in ("gate_ps", "up_ps", "sg_ok", "act_ok", "a_hi", "a_lo", "a_used"))
        d_ps, x2_ok, sq3, y_ok = (sem(n) for n in ("d_ps", "x2_ok", "sq3", "y_ok"))
        dve_step, act_step = sem("dve_step"), sem("act_step")

        block = ctx.enter_context(nc.Block())

        def unit(u):
            if u < U0_OUT:
                c0, n = CHUNKS[u // UPC]
                k = 2 * (u % UPC)
                return (w_in[k * P:(k + 2) * P, c0:c0 + n].rearrange("(k p) n -> p k n", p=P),
                        lambda s: s[:, 0:2 * n].rearrange("p (k n) -> p k n", k=2))
            if u < U0_GU:
                k = u - U0_OUT
                return w_out[k * P:(k + 1) * P, :], lambda s: s
            if u < U0_DOWN:
                f, up = divmod(u - U0_GU, 2)
                w = w_ff_up if up else w_ff_gate
                return (w[:, f * P:(f + 1) * P].rearrange("(k p) n -> p k n", p=P),
                        lambda s: s.rearrange("p (k n) -> p k n", k=KT))
            f = u - U0_DOWN
            return w_ff_down[f * P:(f + 1) * P, :], lambda s: s

        def mix_step(i):
            return 6 if i == 1 else 5

        def s_bank(n):
            return n % 2 if n < RV_STEPS + 2 else (0, 1, 3)[n % 3]

        def size(u):
            return 2 * CHUNKS[u // UPC][1] if u < U0_OUT else D

        @block.sync
        def _(sp):
            def refill(n):
                if n >= RAW:
                    kind, j = ring[n - RAW]
                    if kind == "w":
                        sp.wait_ge(w_lo, j + 1)
                    else:
                        sp.wait_ge(ada_used, ada_ops(j))
                kind, j = ring[n]
                slot = n % RAW
                if kind == "w":
                    src, view = unit(j)
                    sp.dma_start(view(raw[:, slot, :]), src).then_inc(raw_in[slot], 16)
                else:
                    g, k = divmod(j, KT)
                    col = ADA[g] * D
                    sp.dma_start(raw[:, slot, :], w_ada[k * P:(k + 1) * P, col:col + D]).then_inc(raw_in[slot], 16)

            def load_early(j):
                if j >= EARLY:
                    sp.wait_ge(ada_used, ada_ops(j - EARLY))
                q, kh, i = j // 4, j // 2 % 2, j % 2
                col = ADA[i] * D + 2 * q * P
                sp.dma_start(early[:, j % EARLY, :].rearrange("p (k n) -> p k n", k=4),
                             w_ada[4 * kh * P:4 * (kh + 1) * P, col:col + 2 * P].rearrange("(k p) n -> p k n", p=P))\
                  .then_inc(early_in[j % EARLY], 16)

            for t in range(TT):
                sp.dma_start(xs[:, t, :], x[t * P:(t + 1) * P, :]).then_inc(x_in[t], 16)
            for kind, j in items:
                if kind == "early":
                    load_early(j)
                    continue
                if (kind, j) == ("w", 8):
                    sp.wait_ge(ada_used, ADA_OPS)
                    for i, w in enumerate((cmp_w1_k, cmp_w1_v)):
                        sp.dma_start(w1[:, i, :, :], w.rearrange("(j p) n -> p j n", p=P)).then_inc(w1_in, 16)
                if (kind, j) == ("w", 20):
                    sp.wait_ge(flatT_ok, 4)
                    sp.dma_start(decay[:, :, :], decays).then_inc(decay_in, 16)
                if (kind, j) == ("w", U0_GU - 1):
                    sp.wait_ge(mod_read, 10)
                    sp.dma_start(gfin[:, :], ln_final_g.partition_broadcast(P)).then_inc(gfin_in, 16)
                    sp.wait_ge(s_ps, 16 * TT)
                    sp.wait_ge(cs_ps, TT)
                    for t in range(TT):
                        sp.dma_start(x1[:, t, :], x[t * P:(t + 1) * P, :]).then_inc(xagain_in, 16)
                refill(ring.index((kind, j)))
            for t in range(TT):
                sp.wait_ge(y_ok, t + 1)
                sp.dma_start(out[t * P:(t + 1) * P, :], xb[:, t % 2, :]).then_inc(out_done[t], 16)
            for t in range(TT):
                sp.wait_ge(out_done[t], 16)

        @block.gpsimd
        def _(pool):
            pool.memset(rows[:, :], 0.0).then_inc(ones_set, 1)
            pool.memset(ones[:, :], 1.0).then_inc(ones_set, 1)
            pool.memset(BD[:, :, :], 0.0).then_inc(ones_set, 1)
            pool.memset(expo[:, :], -0.5).then_inc(ones_set, 1)
            pool.wait_ge(ones_set, 1)
            for dst, src in ((24, b_ada[0:2 * D]), (40, b_ada[3 * D:5 * D])):
                v = src.rearrange("(r n) -> r n", n=P)
                pool.dma_start(rows[dst:dst + v.shape[0], :], v).then_inc(biases_in, 16)
            for dst, pe_ in ((56, cmp_pe_k), (72, cmp_pe_v)):
                pool.dma_start(rows[dst:dst + CL // 2, :].rearrange("j (l d) -> j l d", d=DH),
                               pe_.rearrange("(j l) d -> j l d", l=2)).then_inc(biases_in, 16)

            def low(u):
                slot, count = place[("w", u)]
                n = size(u)
                pool.wait_ge(raw_in[slot], count)
                pool.wait_ge(w_hi, u + 1)
                pool.tensor_tensor(wl[:, u % SPLIT, 0:n], raw[:, slot, 0:n],
                                   wh[:, u % SPLIT, 0:n].bitcast(F32), ALU.subtract).then_inc(w_lo, 1)

            def power(n, buf):
                pool.wait_ge(var_ok, n)
                pool.tensor_tensor(buf, buf, expo[:, 0:buf.shape[1]], ALU.pow).then_inc(rstd_ok, 1)

            pool.wait_ge(ones_set, 4)
            power(N_X, rstd[:, :])
            pool.dma_start(ga1[:, :], b_ada[2 * D:3 * D].partition_broadcast(P)).then_inc(bias1_in, 16)
            for u in range(UNITS):
                if u == U0_OUT:
                    power(N_RET, yss[:, :])
                if u == U0_OUT + 4:
                    for i in range(1, TT):
                        power(N_RET + i, yss[:, :])
                if u == U0_GU + 1:
                    for t in range(TT):
                        power(N_X1 + t, rstd[:, t:t + 1])
                if u == 3:
                    pool.wait_ge(sq_done, TT // 2)
                    pool.memset(flat[:, :], 0.0).then_inc(flat_zero, 1)
                if u == 18:
                    pool.wait_ge(mlp1, 1)
                    pool.dma_start(ga2[:, :], b_ada[5 * D:6 * D].partition_broadcast(P)).then_inc(bias2_in, 16)
                low(u)
            for t in range(TT):
                power(N_X2 + t, rstd[:, t:t + 1])

        @block.scalar
        def _(a):
            steps = [0]

            def then(ins):
                steps[0] += 1
                ins.then_inc(act_step, 1)
                a.wait_ge(act_step, steps[0])

            def wait_used(u):
                if u < U_PROJ:
                    a.wait_ge(unit_used, u + 1)
                elif u < U0_OUT:
                    a.wait_ge(o_ps, (TT - 1) * K_RV + TT)
                elif u < U0_GU - TAIL:
                    a.wait_ge(unit_used, u + 1 - UPC)
                elif u < U0_GU:
                    a.wait_ge(d_ps, TT)
                elif u < U0_DOWN:
                    f, up = divmod(u - U0_GU, 2)
                    a.wait_ge(up_ps if up else gate_ps, f + 1)
                else:
                    a.wait_ge(a_used, u - U0_DOWN + 1)

            def high(u):
                slot, count = place[("w", u)]
                n = size(u)
                a.wait_ge(raw_in[slot], count)
                if u >= SPLIT:
                    wait_used(u - SPLIT)
                if U0_OUT <= u < U0_GU or u >= U0_DOWN:
                    a.wait_ge(w_scaled, u - U0_OUT + 1 if u < U0_GU else U_OUT + u - U0_DOWN + 1)
                a.activation(wh[:, u % SPLIT, 0:n], raw[:, slot, 0:n], ACT.Copy).then_inc(w_hi, 1)

            a.dma_start(cst[:, 0:P], consts[:, 0:P]).then_inc(ident_in, 16)
            a.wait_ge(ones_set, 1)
            for dst, src in ((0, c), (8, ln_mix_g), (16, ln_ffn_g)):
                v = src.rearrange("(r n) -> r n", n=P)
                a.dma_start(rows[dst:dst + v.shape[0], :], v).then_inc(rows_in, 16)
            a.dma_start(cst[:, P:K_N], consts[:, P:K_N]).then_inc(const_in, 16)
            a.dma_start(w2[:, 0, :], cmp_w2_k).then_inc(w2_in, 16)
            a.dma_start(w2[:, 1, :], cmp_w2_v).then_inc(w2_in, 16)

            for t in range(0, TT, 2):
                a.wait_ge(x_in[t], 16)
                if t:
                    a.wait_ge(sq_done, t // 2)
                a.activation(junk[:, :], xs[:, t, :], ACT.Square, accum_out=ssq[:, t:t + 1]).then_inc(sq_done, 1)
            a.wait_ge(cols_ok, 1)
            a.activation(cs[:, :], cols[:, 0:KT], ACT.Silu).then_inc(c_silu, 1)
            a.wait_ge(ident_in, 16)
            a.activation(identR[:, :], ident, ACT.Copy).then_inc(consts_r, 1)
            a.wait_ge(const_in, 16)
            a.activation(maskR[:, :], cst[:, K_MASK:K_MASK + P], ACT.Copy).then_inc(consts_r, 1)
            high(0)
            for k in range(KT):
                a.wait_ge(xT_ps, k + 1)
                a.activation(xT[:, k, :], ps[:, k % 4, :], ACT.Copy).then_inc(xT_ok, 1)
            for k in range(KT):
                if k % 2 and k < KT - 1:
                    high(k // 2 + 1)
                a.wait_ge(mod_read, k // 2 + 1)
                a.wait_ge(xT_ok, k + 1)
                if k >= 2:
                    a.wait_ge(h_lo, k - 1)
                a.activation(hf[:, k % 2, :], xT[:, k, :], ACT.Identity, bias=mods[:, 1, k:k + 1],
                             scale=mods[:, 0, k:k + 1]).then_inc(h_full, 1)
                a.wait_ge(h_full, k + 1)
                a.activation(hTh[:, k, :], hf[:, k % 2, :], ACT.Copy).then_inc(h_hi, 1)

            def evacuate(ch, tiles=range(TT)):
                for t in tiles:
                    if ch == K_RV or t < TT - 1:
                        a.wait_ge(o_ps, (TT - 1) * ch + t + 1)
                    else:
                        a.wait_ge(unit_used, UPC * (ch + 1))
                    if ch == K_CMP:
                        a.activation(stage[:, t, 0:384], ps[:, t, 0:384], ACT.Copy)
                        ins = a.activation(V[:, t, 0, :], ps[:, t, 384:512], ACT.Copy)
                    elif ch == K_Q:
                        a.wait_ge(roped, t + 1)
                        a.wait_ge(kv_out, 16 * TT)
                        ins = a.activation(stage[:, t, :], ps[:, t, :], ACT.Copy)
                    elif ch == K_WIN:
                        a.wait_ge(roped, TT + t + 1)
                        a.activation(stage[:, t, 0:P], ps[:, t, 0:P], ACT.Copy)
                        a.activation(V[:, t, 1, :], ps[:, t, P:2 * P], ACT.Copy)
                        ins = a.activation(gates[:, t, :], ps[:, t, 2 * P:2 * P + 3 * NH], ACT.Tanh, scale=0.5)
                    elif ch == K_RQK:
                        a.wait_ge(roped, 2 * TT + t + 1)
                        ins = a.activation(stage[:, t, :], ps[:, t, :], ACT.Copy)
                    elif ch == K_RG:
                        ins = a.activation(rg[:, t, :], ps[:, t, :], ACT.Silu)
                    else:
                        ins = a.activation(rv[:, t, :], ps[:, 3, :], ACT.Copy)
                    ins.then_inc(proj_ev, 1)
                    if ch == K_CMP:
                        a.wait_ge(proj_ev, t + 1)
                        a.dma_start(kv_dram[t * P:(t + 1) * P, :], stage[:, t, 0:2 * P]).then_inc(kv_out, 16)

            def load_blocks():
                a.wait_ge(kv_out, 16 * TT)
                a.wait_ge(flat_zero, 1)
                for kv in range(2):
                    for g in range(NG):
                        row = (kv * NG + g) * CP
                        col = (kv * NG + g) * DH
                        src = kv_dram[0:NC * CS, col:col + DH].rearrange("(c l) d -> c l d", l=CS)
                        nxt = kv_dram[CS:(NC + 1) * CS, col:col + DH].rearrange("(c l) d -> c l d", l=CS)
                        dst = flat[row:row + NC, :].rearrange("c (h l d) -> c h l d", h=2, d=DH)
                        a.dma_start(dst[:, 0], src).then_inc(flat_in, 16)
                        a.dma_start(dst[:, 1], nxt).then_inc(flat_in, 16)

            def rot_high(n):
                a.wait_ge(rotT, n + 1)
                src = ps[:, 4 + n % 2, :]
                if n == 0 or n == 5:
                    ins = a.activation(KTh[:, n // 5, :], src, ACT.Copy)
                elif n < 5:
                    t = n - 1
                    ins = a.activation(QTh[:, :, t * P:(t + 1) * P], src.rearrange("p (h q) -> p h q", h=HPG),
                                       ACT.Copy, scale=QSCALE)
                else:
                    t = n - 6
                    v = src.rearrange("p (h q) -> p h q", h=4)
                    a.activation(rqT[:, :, t * P:(t + 1) * P], v[:, 0:2], ACT.Copy)
                    ins = a.activation(rkT[:, :, t * P:(t + 1) * P], v[:, 2:4], ACT.Copy, scale=RDK ** -0.5)
                ins.then_inc(rot_hi, 1)

            for v in range(U_PROJ):
                if v and v % UPC == 0:
                    evacuate(v // UPC - 1)
                if v:
                    high(v + 3)
                if v == 5:
                    load_blocks()
                for n in {7: [0], 10: [1, 2], 12: [3, 4], 15: [5], 18: [6, 7], 19: [8, 9]}.get(v, []):
                    rot_high(n)
                if v == 14:
                    a.wait_ge(mlp1, 1)
                    a.activation(hs[:, :, :], ps[:, 7, 0:4 * CP].rearrange("p (i n) -> p i n", i=2), ACT.Silu).then_inc(mlp1_silu, 1)
                if v == 18:
                    a.wait_ge(kcT, 1)
                    a.activation(KCh[:, :], ps[:, 7, 0:CP], ACT.Copy).then_inc(kcT_hi, 1)
            evacuate(K_RG)
            high(U_PROJ + 3)

            def exp(n):
                i = n // 16
                w = (i + 1) * P
                b, hd = divmod(n % 16, 8)
                head = hd % NG * HPG + hd // NG
                a.wait_ge(s_min, n + 1)
                if n >= 3:
                    a.wait_ge(p_T, n - 2)
                a.activation(Pr[:, n % 3, 0:w], ps[:, s_bank(n), 0:w], ACT.Exp, bias=mn[:, n % 8:n % 8 + 1], scale=-1.0,
                             accum_out=den[:, i % 2, b, head:head + 1]).then_inc(p_exp, 1)

            def pT_copy(n):
                w = (n // 16 + 1) * P
                a.wait_ge(p_T, n + 1)
                if n >= 2:
                    a.wait_ge(pv, n - 1)
                a.activation(PT[:, n % 2, 0:w], ps[:, 2, 0:w], ACT.Copy).then_inc(pT_ok, 1)

            def mix_high(i):
                a.wait_ge(mixT_ps, i + 1)
                a.activation(hTh[:, :, i * P:(i + 1) * P], ps[:, 6:8, :].rearrange("p b (k q) -> p (b k) q", k=4),
                             ACT.Copy).then_inc(mix_hi, 1)

            def ret_squares(i):
                a.wait_ge(r_y, RH * (i + 1))
                for h in range(RH):
                    ins = a.activation(sqj[:, h * P:(h + 1) * P], ps[:, 7, h * P:(h + 1) * P], ACT.Square,
                                       accum_out=yss[:, h:h + 1])
                ins.then_inc(r_sq, 1)

            for n in range(16 * TT + 7):
                i, s = divmod(n, 16)
                if n % 4 == 0 and 4 <= n <= RV_STEPS:
                    evacuate(K_RV, [n // 4 - 1])
                if 1 <= n <= 16 * TT:
                    exp(n - 1)
                if 3 <= n <= 16 * TT + 2:
                    pT_copy(n - 3)
                if RV_STEPS + 4 <= n < RV_STEPS + 12 and n % 2 == 0:
                    high(U0_OUT + (n - RV_STEPS - 4) // 2)
                if s == 1 and i >= 1:
                    ret_squares(i - 1)
                if i >= 1 and s == mix_step(i) + 1:
                    mix_high(i - 1)
                if s == 9 and i < TT:
                    a.wait_ge(c_pre, i + 1)
                    a.activation(pc[:, :, :], sc[:, :, :], ACT.Exp, scale=-1.0).then_inc(c_exp, 1)
                if s == 10 and i < TT:
                    a.wait_ge(c_T, i + 1)
                    a.activation(pcT[:, :, :], ps[:, 6, 0:2 * P].rearrange("p (g q) -> p g q", g=NG), ACT.Copy).then_inc(cT_ok, 1)

            for u in range(U0_OUT + 4, U0_GU + 1):
                high(u)

            def x1_square(t):
                a.wait_ge(x1_ok, t + 1)
                a.activation(xb[:, t % 2, :], x1[:, t, :], ACT.Square, accum_out=ssq[:, t:t + 1]).then_inc(sq2, 1)

            def modulate(t):
                a.wait_ge(xbT, 2 * t + 2)
                if t:
                    a.wait_ge(h2_lo, 2 * t - 1)
                for k in range(4):
                    ins = a.activation(h2[:, 1, k, :], ps[:, 2 * t + 1, k * P:(k + 1) * P], ACT.Identity,
                                       bias=mods[:, 3, 4 + k:5 + k], scale=mods[:, 2, 4 + k:5 + k])
                ins.then_inc(h2b_ok, 1)
                a.wait_ge(h2b_ok, t + 1)
                a.activation(hTh[:, 4:8, t * P:(t + 1) * P], h2[:, 1], ACT.Copy).then_inc(h2_hi, 1)
                a.wait_ge(h2_ok, t + 1)
                a.activation(hTh[:, 0:4, t * P:(t + 1) * P], h2[:, 0], ACT.Copy).then_inc(h2_hi, 1)

            x1_square(0)
            for t in range(TT):
                if t == TT - 2:
                    high(U0_GU + 1)
                    high(U0_GU + 2)
                    high(U0_GU + 3)
                if t < TT - 1:
                    x1_square(t + 1)
                modulate(t)

            def a_high(f):
                a.wait_ge(act_ok, f + 1)
                if f >= SPLIT:
                    a.wait_ge(a_used, f - SPLIT + 1)
                a.activation(ah[:, f % SPLIT, :], act[:, f, :], ACT.Copy).then_inc(a_hi, 1)

            for f in range(FT):
                a.wait_ge(gate_ps, f + 1)
                if f >= 2:
                    a.wait_ge(act_ok, f - 1)
                a.activation(sg[:, f % 2, :], ps[:, 2 * (f % 2), :], ACT.Silu).then_inc(sg_ok, 1)
                high(U0_GU + 2 * f + 4)
                high(U0_GU + 2 * f + 5)
                if 2 <= f < 2 + SPLIT:
                    a_high(f - 2)

            for f in range(SPLIT, FT):
                a_high(f)
                high(U0_DOWN + f)
            for t in range(TT):
                a.wait_ge(x2_ok, t + 1)
                if t >= 2:
                    a.wait_ge(out_done[t - 2], 16)
                a.activation(xb[:, t % 2, :], x1[:, t, :], ACT.Square, accum_out=ssq[:, t:t + 1]).then_inc(sq3, 1)

        @block.vector
        def _(v_):
            d = v_
            steps = [0]

            def then(ins):
                steps[0] += 1
                ins.then_inc(dve_step, 1)
                d.wait_ge(dve_step, steps[0])

            def ada_early(q, ops):
                for o in ops:
                    p, (kk, i) = 2 * q + o // 8, divmod(o % 8, 2)
                    j, k = 2 * p + i, 4 * (p % 2) + kk
                    d.wait_ge(early_in[j % EARLY], 16 * (j // EARLY + 1))
                    dst = acc[:, i, 2 * q * P:2 * (q + 1) * P]
                    src = early[:, j % EARLY, 2 * kk * P:2 * (kk + 1) * P]
                    if k == 0:
                        d.tensor_scalar(dst, src, cs[:, k:k + 1], None, ALU.mult).then_inc(ada_used, 1)
                    else:
                        d.wait_ge(ada_used, 16 * q + o - 1)
                        d.scalar_tensor_tensor(dst, src, cs[:, k:k + 1], dst, ALU.mult, ALU.add).then_inc(ada_used, 1)

            def ada(j):
                g, k = divmod(j, KT)
                slot, count = place[("ada", j)]
                if k == 0 and g in (3, 4):
                    d.wait_ge(mod_sum, {3: 4, 4: 6}[g])
                if k == 0 and g == 5:
                    d.wait_ge(mlp1, 1)
                d.wait_ge(raw_in[slot], count)
                dst = acc2[:, :] if g == 5 else acc[:, g % 2, :]
                if k == 0:
                    d.tensor_scalar(dst, raw[:, slot, :], cs[:, k:k + 1], None, ALU.mult).then_inc(ada_used, 1)
                else:
                    d.wait_ge(ada_used, ada_ops(j) - 1)
                    d.scalar_tensor_tensor(dst, raw[:, slot, :], cs[:, k:k + 1], dst, ALU.mult, ALU.add).then_inc(ada_used, 1)

            def mod_columns(n, i, c0, k0, k1, b_off, g_off):
                d.wait_ge(mod_sum, n)
                dst = mods[:, i, k0:k1]
                add = d.tensor_tensor(dst, ps[:, 7, c0:c0 + k1 - k0], cols[:, b_off + k0:b_off + k1], ALU.add)
                if g_off is None:
                    return add
                then(add)
                return d.tensor_tensor(dst, dst, cols[:, g_off + k0:g_off + k1], ALU.mult)

            for t in range(1, TT, 2):
                d.wait_ge(x_in[t], 16)
                then(d.tensor_tensor_reduce(out=hf[:, :, :].rearrange("p a b -> p (a b)"), in0=xs[:, t, :], in1=xs[:, t, :], scale=1.0,
                                            scalar=0.0, op0=ALU.mult, op1=ALU.add, accum_out=ssq[:, t:t + 1]))
            d.wait_ge(sq_done, TT // 2)
            d.tensor_scalar(rstd[:, :], ssq[:, :], 1.0 / D, EPS, ALU.mult, ALU.add).then_inc(var_ok, 1)
            d.wait_ge(rowsT, 1)
            d.tensor_copy(cols[:, :], ps[:, 4, 0:88]).then_inc(cols_ok, 1)
            d.wait_ge(cols_ok, 1)
            for i in (0, 2):
                off = 32 if i == 0 else 48
                then(d.tensor_scalar(cols[:, off:off + KT], cols[:, off:off + KT], 1.0, None, ALU.add))
            d.wait_ge(rstd_ok, N_X)
            for t in range(TT):
                d.tensor_scalar(xs[:, t, :], xs[:, t, :], rstd[:, t:t + 1], None, ALU.mult).then_inc(xn_done, 1)

            def mod_rows(n, ga, half, bank=7):
                d.wait_ge(mod_sum, n)
                d.wait_ge(bias1_in if ga is ga1 else bias2_in, 16)
                h = ga[:, half * 512:(half + 1) * 512]
                d.tensor_tensor(h, ps[:, bank, :], h, ALU.add).then_inc(mod_read, 1)

            d.wait_ge(c_silu, 1)
            def h_low(k):
                d.wait_ge(h_hi, k + 1)
                d.tensor_tensor(hTl[:, k, :], hf[:, k % 2, :], hTh[:, k, :].bitcast(F32), ALU.subtract).then_inc(h_lo, 1)

            ada_early(0, range(16))
            for q in range(UPC):
                mod_columns(q + 1, 0, 4 * q, 2 * q, 2 * q + 2, 32, 8)
                mod_columns(q + 1, 1, 4 * q + 2, 2 * q, 2 * q + 2, 24, None).then_inc(mod_read, 1)
                if q < UPC - 1:
                    ada_early(q + 1, range(4))
                h_low(2 * q)
                if q < UPC - 1:
                    ada_early(q + 1, range(4, 6))
                h_low(2 * q + 1)
                if q < UPC - 1:
                    ada_early(q + 1, range(6, 16))

            def scale_unit(u):
                slot, count = place[("w", u)]
                ga = ga1 if u < U0_GU else ga2
                if u == U0_OUT:
                    d.wait_ge(mod_read, 6)
                if u == U0_DOWN:
                    d.wait_ge(mod_read, 10)
                d.wait_ge(raw_in[slot], count)
                d.tensor_tensor(raw[:, slot, :], raw[:, slot, :], ga[:, :], ALU.mult).then_inc(w_scaled, 1)

            def rotate(src, table, n, dst, view=lambda x: x, parts=P):
                a0 = rt[0:parts, 0, 0:n * DH].rearrange("p (h x) -> p h x", x=DH)
                a1 = rt[0:parts, 1, 0:n * DH].rearrange("p (h x) -> p h x", x=DH)
                cos = table[:, 0:DH].unsqueeze(1).broadcast_to([parts, n, DH])
                s0 = table[:, DH:DH + 32].unsqueeze(1).broadcast_to([parts, n, 32])
                s1 = table[:, DH + 32:2 * DH].unsqueeze(1).broadcast_to([parts, n, 32])
                d.tensor_tensor(a0, src, cos, ALU.mult)
                d.tensor_tensor(a1[:, :, 0:32], src[:, :, 32:64], s0, ALU.mult)
                then(d.tensor_tensor(a1[:, :, 32:64], src[:, :, 0:32], s1, ALU.mult))
                return d.tensor_tensor(dst, view(a0), view(a1), ALU.add)

            def rope_chunk(ch, tiles):
                for t in tiles:
                    if TT * ch + t:
                        d.wait_ge(roped, TT * ch + t)
                    d.wait_ge(proj_ev, TT * ch + t + 1)
                    if ch == K_CMP:
                        src = stage[:, t, 2 * P:3 * P].rearrange("p (h x) -> p h x", x=DH)
                        dst = rot[:, t, 0:P].rearrange("p (h x) -> p h x", x=DH)
                        rotate(src, rope[:, t, :], 2, dst).then_inc(roped, 1)
                    elif ch == K_Q:
                        if t == 0:
                            d.wait_ge(rotT, 1)
                        src = stage[:, t, :].rearrange("p (h x) -> p h x", x=DH)
                        dst = rot[:, t, :].rearrange("p (h g x) -> p g h x", g=NG, x=DH)
                        rotate(src, rope[:, t, :], NH, dst, lambda z: z.rearrange("p (g h) x -> p g h x", g=NG)).then_inc(roped, 1)
                    elif ch == K_WIN:
                        if t == 0:
                            d.wait_ge(rotT, 5)
                        src = stage[:, t, 0:P].rearrange("p (h x) -> p h x", x=DH)
                        dst = rot[:, t, 0:P].rearrange("p (h x) -> p h x", x=DH)
                        rotate(src, rope[:, t, :], 2, dst).then_inc(roped, 1)
                    else:
                        if t == 0:
                            d.wait_ge(rotT, 6)
                        src = stage[:, t, :].rearrange("p (h x) -> p h x", x=DH)
                        dst = rot[:, t, :].rearrange("p (h x) -> p h x", x=DH)
                        rotate(src, rope[:, t, :], NH, dst).then_inc(roped, 1)

            def rot_low(n):
                d.wait_ge(rotT, n + 1)
                d.wait_ge(rot_hi, n + 1)
                src = ps[:, 4 + n % 2, :]
                if n == 0 or n == 5:
                    ins = d.tensor_tensor(KTl[:, n // 5, :], src, KTh[:, n // 5, :].bitcast(F32), ALU.subtract)
                else:
                    t = n - 1
                    ins = d.scalar_tensor_tensor(QTl[:, :, t * P:(t + 1) * P], src.rearrange("p (h q) -> p h q", h=HPG), QSCALE,
                                                 QTh[:, :, t * P:(t + 1) * P].bitcast(F32), ALU.mult, ALU.subtract)
                ins.then_inc(rot_lo, 1)

            def flat_add(b):
                d.wait_ge(flatT_ps, b + 1)
                for kv in range(2):
                    src = ps[:, 6, :].rearrange("p (j n) -> p j n", j=4)[:, :, kv * 2 * CP:(kv + 1) * 2 * CP]
                    pe_ = cols[:, 56 + 16 * kv + 4 * b:60 + 16 * kv + 4 * b].unsqueeze(2).broadcast_to([P, 4, 2 * CP])
                    ins = d.tensor_tensor(flatT[:, 4 * b:4 * b + 4, kv * 2 * CP:(kv + 1) * 2 * CP], src, pe_, ALU.add)
                ins.then_inc(flatT_ok, 1)

            def compressed():
                d.wait_ge(proj_ev, TT * 3)
                d.tensor_scalar(gates[:, :, :], gates[:, :, :], 0.5, 0.5, ALU.mult, ALU.add)
                d.wait_ge(mlp2, 1)
                d.wait_ge(roped, TT * K_WIN + 2)
                kc = ps[0:CP, 6, 0:P].rearrange("p (g x) -> p g x", g=NG)
                rotate(kc, cst[0:CP, K_CROPE:K_CROPE + P], NG, kcr[:, :].rearrange("p (g x) -> p g x", g=NG),
                       parts=CP).then_inc(kc_rot, 1)
                d.wait_ge(kc_rot, 1)
                d.wait_ge(ones_set, 3)
                for g in range(NG):
                    for h in range(HPG):
                        ins = d.tensor_copy(BD[CP * h:CP * (h + 1), g, h * DH:(h + 1) * DH],
                                            ps[0:CP, 6, P + g * DH:P + (g + 1) * DH])
                ins.then_inc(bd_ok, 1)

            d.wait_ge(const_in, 16)
            for v in range(U_PROJ):
                for n in {7: [0], 10: [1, 2], 12: [3, 4], 15: [5]}.get(v, []):
                    rot_low(n)
                if 9 <= v <= 12:
                    flat_add(v - 9)
                if v == 8:
                    mod_rows(5, ga1, 0)
                if v == 10:
                    mod_rows(6, ga1, 1)
                if v == 15:
                    compressed()
                if v == 16:
                    mod_columns(7, 2, 32, 0, KT, 48, 16).then_inc(mod_read, 1)
                if v == 18:
                    d.wait_ge(kcT_hi, 1)
                    d.tensor_tensor(KCl[:, :], ps[:, 7, 0:CP], KCh[:, :].bitcast(F32), ALU.subtract).then_inc(kcT_lo, 1)
                if 4 <= v and v // UPC - 1 <= K_RQK and v % UPC < 2:
                    rope_chunk(v // UPC - 1, (0, 1) if v % UPC == 0 else (2, 3))
                for j in ada_after.get(v + 3, []):
                    ada(j)

            mod_columns(8, 3, 40, 0, KT, 40, None).then_inc(mod_read, 1)

            def row_min(n):
                w = (n // 16 + 1) * P
                d.wait_ge(s_ps, n + 1)
                if n >= 8:
                    d.wait_ge(p_exp, n - 7)
                d.tensor_reduce(mn[:, n % 8:n % 8 + 1], ps[:, s_bank(n), 0:w], AX.X, ALU.min).then_inc(s_min, 1)

            def heads_view(ap, n=NH):
                return ap.rearrange("p (h x) -> p h x", h=n)

            def add_branch(i, b):
                d.wait_ge(pv, 16 * i + 8 * b)
                then(d.reciprocal(rgt[:, :], den[:, i % 2, b - 1, :]))
                then(d.tensor_tensor(rgt[:, :], rgt[:, :], gates[:, i, b * NH:(b + 1) * NH], ALU.mult))
                then(d.tensor_tensor(heads_view(tmpo[:, :]), heads_view(ps[:, 3 + b, :]),
                                     rgt[:, :].unsqueeze(2).broadcast_to([P, NH, DH]), ALU.mult))
                y = mix[:, i % 2, 512:1024]
                d.tensor_tensor(y, y, tmpo[:, :], ALU.add).then_inc(y_sum, 1)
                d.wait_ge(y_sum, 3 * i + b + 1)

            def cmp_scores(i):
                d.wait_ge(cs_ps, i + 1)
                for g in range(NG):
                    ins = d.tensor_tensor(sc[:, g * HPG:(g + 1) * HPG, :], ps[:, 6 + g, 0:P].rearrange("p (h n) -> p h n", h=HPG),
                                          cmask[:, i, :].unsqueeze(1).broadcast_to([P, HPG, CP]), ALU.add)
                then(ins)
                then(d.tensor_reduce(mnc[:, :], sc[:, :, :], AX.X, ALU.min))
                d.tensor_tensor(sc[:, :, :], sc[:, :, :], mnc[:, :].unsqueeze(2).broadcast_to([P, NH, CP]), ALU.subtract).then_inc(c_pre, 1)

            def cmp_gates(i):
                d.wait_ge(c_exp, i + 1)
                then(d.tensor_reduce(mnc[:, :], pc[:, :, :], AX.X, ALU.add))
                then(d.reciprocal(mnc[:, :], mnc[:, :]))
                then(d.tensor_tensor(mnc[:, :], mnc[:, :], gates[:, i, 0:NH], ALU.mult))
                if i == 0:
                    then(d.tensor_scalar(mnc[:, :], mnc[:, :], cst[:, K_VALID:K_VALID + 1], None, ALU.mult))

            def cmp_out(i):
                d.wait_ge(c_o, i + 1)
                if i >= 2:
                    d.wait_ge(mixT_ps, i - 1)
                d.tensor_tensor(heads_view(mix[:, i % 2, 512:1024]), heads_view(ps[:, 7, :]),
                                mnc[:, :].unsqueeze(2).broadcast_to([P, NH, DH]), ALU.mult).then_inc(y_sum, 1)
                d.wait_ge(y_sum, 3 * i + 1)

            def ret_decay(i, h):
                d.wait_ge(r_s, RH * i + h + 1)
                if i == 0 and h == 0:
                    d.wait_ge(decay_in, 16)
                if RH * i + h >= 2:
                    d.wait_ge(r_y, RH * i + h - 1)
                w = (i + 1) * P
                d.tensor_tensor(ats[:, h % 2, 0:w], ps[:, 6, 0:w], decay[:, h, (TT - 1 - i) * P:TT * P], ALU.mult).then_inc(r_dec, 1)

            def ret_var(i):
                d.wait_ge(r_sq, i + 1)
                d.tensor_scalar(yss[:, :], yss[:, :], 1.0 / RDV, EPS, ALU.mult, ALU.add).then_inc(var_ok, 1)

            def ret_norm(i):
                d.wait_ge(rstd_ok, N_RET + i)
                then(d.tensor_tensor(heads_view(tmpo[:, :], RH), heads_view(ps[:, 7, :], RH),
                                     yss[:, :].unsqueeze(2).broadcast_to([P, RH, RDV]), ALU.mult))
                if i == 0:
                    d.wait_ge(proj_ev, TT * (K_RG + 1))
                d.tensor_tensor(mix[:, i % 2, 0:512], tmpo[:, :], rg[:, i, :], ALU.mult).then_inc(r_norm, 1)
                d.wait_ge(r_norm, i + 1)

            def mix_low(i):
                d.wait_ge(mix_hi, i + 1)
                d.tensor_tensor(hTl[:, :, i * P:(i + 1) * P], ps[:, 6:8, :].rearrange("p b (k q) -> p (b k) q", k=4),
                                hTh[:, :, i * P:(i + 1) * P].bitcast(F32), ALU.subtract).then_inc(mix_lo, 1)

            for n in range(16 * TT + 7):
                i, s = divmod(n, 16)
                if n < 16 * TT:
                    row_min(n)
                if 2 <= n < 2 + KT:
                    ada(ADA_LATE + n - 2)
                if n == RV_STEPS + 4:
                    mod_rows(9, ga2, 0)
                    mod_rows(10, ga2, 1, bank=6)
                if RV_STEPS + 2 <= n < RV_STEPS + 10 and n % 2 == 0:
                    scale_unit(U0_OUT + (n - RV_STEPS - 2) // 2)
                if s == 1 and i >= 1:
                    ret_var(i - 1)
                if s == 2 and i >= 1:
                    ret_norm(i - 1)
                if s == 4 and i >= 1:
                    add_branch(i - 1, 2)
                if i >= 1 and s == mix_step(i) + 1:
                    mix_low(i - 1)
                if s == 8 and i < TT:
                    cmp_scores(i)
                if s == 10 and i < TT:
                    cmp_gates(i)
                if s == 12:
                    cmp_out(i)
                if s == 13:
                    add_branch(i, 1)
                if s >= 12:
                    ret_decay(i, s - 12)

            def residual(t):
                d.wait_ge(d_ps, t + 1)
                d.wait_ge(xagain_in, 16 * TT)
                d.tensor_tensor(x1[:, t, :], ps[:, 2 * t:2 * t + 2, :].rearrange("p b n -> p (b n)"), x1[:, t, :], ALU.add).then_inc(x1_ok, 1)
                d.wait_ge(sq2, t + 1)
                d.tensor_scalar(rstd[:, t:t + 1], ssq[:, t:t + 1], 1.0 / D, EPS, ALU.mult, ALU.add).then_inc(var_ok, 1)
                d.wait_ge(rstd_ok, N_X1 + t)
                d.tensor_scalar(xb[:, t % 2, :], x1[:, t, :], rstd[:, t:t + 1], None, ALU.mult).then_inc(xb_ok, 1)

            def modulate(t):
                d.wait_ge(xbT, 2 * t + 1)
                if t:
                    d.wait_ge(h2_lo, 2 * t)
                for k in range(4):
                    ins = d.tensor_scalar(h2[:, 0, k, :], ps[:, 2 * t, k * P:(k + 1) * P], mods[:, 2, k:k + 1], mods[:, 3, k:k + 1],
                                          ALU.mult, ALU.add)
                ins.then_inc(h2_ok, 1)
                for b in (1, 0):
                    ks = slice(4 * b, 4 * b + 4)
                    d.wait_ge(h2_hi, 2 * t + 2 - b)
                    if b == 0:
                        d.wait_ge(h2_ok, t + 1)
                    d.tensor_tensor(hTl[:, ks, t * P:(t + 1) * P], h2[:, b], hTh[:, ks, t * P:(t + 1) * P].bitcast(F32),
                                    ALU.subtract).then_inc(h2_lo, 1)

            for u in range(U0_OUT + 4, U0_GU):
                scale_unit(u)
            residual(0)
            for t in range(TT):
                if t < TT - 1:
                    residual(t + 1)
                modulate(t)

            def a_low(f):
                d.wait_ge(a_hi, f + 1)
                d.tensor_tensor(al[:, f % SPLIT, :], act[:, f, :], ah[:, f % SPLIT, :].bitcast(F32), ALU.subtract).then_inc(a_lo, 1)

            for f in range(FT):
                d.wait_ge(sg_ok, f + 1)
                d.wait_ge(up_ps, f + 1)
                d.tensor_tensor(act[:, f, :], ps[:, 2 * (f % 2) + 1, :], sg[:, f % 2, :], ALU.mult).then_inc(act_ok, 1)
                for u in (U0_GU + 2 * f + 4, U0_GU + 2 * f + 5):
                    if u >= U0_DOWN:
                        scale_unit(u)
                if 3 <= f < 3 + SPLIT:
                    a_low(f - 3)
            for f in range(FT):
                if f >= SPLIT:
                    a_low(f)
                if f + SPLIT < FT:
                    scale_unit(U0_DOWN + f + SPLIT)
            d.wait_ge(gfin_in, 16)
            for t in range(TT):
                d.wait_ge(d_ps, TT + t + 1)
                d.tensor_tensor(x1[:, t, :], ps[:, 2 * t:2 * t + 2, :].rearrange("p b n -> p (b n)"), x1[:, t, :], ALU.add).then_inc(x2_ok, 1)
                d.wait_ge(sq3, t + 1)
                d.tensor_scalar(rstd[:, t:t + 1], ssq[:, t:t + 1], 1.0 / D, EPS, ALU.mult, ALU.add).then_inc(var_ok, 1)
                d.wait_ge(rstd_ok, N_X2 + t)
                d.scalar_tensor_tensor(xb[:, t % 2, :], x1[:, t, :], rstd[:, t:t + 1], gfin[:, :], ALU.mult, ALU.mult).then_inc(y_ok, 1)

        @block.tensor
        def _(pe):
            mm = pe.matmul

            def product(o, ah_, al_, bh_, bl_, first, last):
                mm(o, ah_, bh_, start=first, stop=False)
                mm(o, ah_, bl_, start=False, stop=False)
                return mm(o, al_, bh_, start=False, stop=last)

            pe.wait_ge(ident_in, 16)
            pe.wait_ge(rows_in, 16 * 3)
            pe.wait_ge(biases_in, 16 * 4)
            pe.transpose(ps[:, 4, 0:P], rows[:, :], ident).then_inc(rowsT, 1)
            for k in range(KT):
                if k >= 4:
                    pe.wait_ge(xT_ok, k - 3)
                for t in range(TT):
                    if k == 0:
                        pe.wait_ge(xn_done, t + 1)
                    ins = pe.transpose(ps[:, k % 4, t * P:(t + 1) * P], xs[:, t, k * P:(k + 1) * P], ident)
                ins.then_inc(xT_ps, 1)

            def sum_columns(i, c0, ks):
                for n, k in enumerate(ks):
                    ins = mm(ps[:, 7, c0 + n:c0 + n + 1], acc[:, i, k * P:(k + 1) * P], ones[:, 0:1], start=True, stop=True)
                return ins

            def sum_rows(g, half, bank=7):
                pe.wait_ge(ada_used, ada_ops(KT * (g + 1) - 1))
                src = acc2 if g == 5 else acc[:, g % 2, :]
                mm(ps[:, bank, :], ones[:, :], src[:, half * 512:(half + 1) * 512], start=True, stop=True).then_inc(mod_sum, 1)

            def modulation(q):
                pe.wait_ge(ada_used, 16 * (q + 1))
                if q:
                    pe.wait_ge(mod_read, q)
                sum_columns(0, 4 * q, (2 * q, 2 * q + 1))
                sum_columns(1, 4 * q + 2, (2 * q, 2 * q + 1)).then_inc(mod_sum, 1)

            pe.wait_ge(ones_set, 2)
            modulation(0)

            def flat_transposes(b):
                if b == 0:
                    pe.wait_ge(flat_in, 16 * 8)
                else:
                    pe.wait_ge(flatT_ok, b)
                for j in range(4):
                    ins = pe.transpose(ps[:, 6, j * P:(j + 1) * P], flat[:, (4 * b + j) * P:(4 * b + j + 1) * P], ident)
                ins.then_inc(flatT_ps, 1)

            def rot_transposes(n):
                if n >= 2:
                    pe.wait_ge(rot_hi, n - 1)
                    pe.wait_ge(rot_lo, min(n - 1, 6))
                if n == 0 or n == 5:
                    pe.wait_ge(roped, TT if n == 0 else 3 * TT)
                    for t in range(TT):
                        ins = pe.transpose(ps[:, 4 + n % 2, t * P:(t + 1) * P], rot[:, t, 0:P], ident)
                else:
                    t = n - 1 if n < 5 else n - 6
                    pe.wait_ge(roped, (TT if n < 5 else 3 * TT) + t + 1)
                    for h in range(4):
                        ins = pe.transpose(ps[:, 4 + n % 2, h * P:(h + 1) * P], rot[:, t, h * P:(h + 1) * P], ident)
                ins.then_inc(rotT, 1)

            for v in range(U_PROJ):
                ch, q = divmod(v, UPC)
                n = CHUNKS[ch][1]
                s = v % SPLIT
                pe.wait_ge(w_lo, v + 1)
                bh = wh[:, s, 0:2 * n].rearrange("p (k n) -> p k n", k=2)
                bl = wl[:, s, 0:2 * n].rearrange("p (k n) -> p k n", k=2)
                for t in range(TT):
                    if v < UPC - 1 and t == TT // 2:
                        modulation(q + 1)
                    if ch and q == 0:
                        pe.wait_ge(proj_ev, TT * (ch - 1) + t + 1)
                    for kk in range(2):
                        k = 2 * q + kk
                        if ch == 0 and t == 0:
                            pe.wait_ge(h_lo, k + 1)
                        tok = slice(t * P, (t + 1) * P)
                        ins = product(ps[:, t, 0:n], hTh[:, k, tok], hTl[:, k, tok], bh[:, kk, :], bl[:, kk, :], k == 0, k == KT - 1)
                    if q == UPC - 1 and t < TT - 1:
                        ins.then_inc(o_ps, 1)
                ins.then_inc(unit_used, 1)
                for m in {6: [0], 9: [1, 2], 11: [3, 4], 14: [5], 17: [6, 7], 18: [8, 9]}.get(v, []):
                    rot_transposes(m)
                if 8 <= v <= 11:
                    flat_transposes(v - 8)
                if v == 7:
                    pe.wait_ge(mod_read, 4)
                    sum_rows(2, 0)
                if v == 9:
                    pe.wait_ge(mod_read, 5)
                    sum_rows(2, 1)
                if v == 13:
                    pe.wait_ge(flatT_ok, 4)
                    pe.wait_ge(w1_in, 32)
                    pe.wait_ge(mod_read, 6)
                    for kv in range(2):
                        for j in range(CL // 2):
                            ins = mm(ps[:, 7, kv * 2 * CP:(kv + 1) * 2 * CP], w1[:, kv, j, :], flatT[:, j, kv * 2 * CP:(kv + 1) * 2 * CP],
                                     start=j == 0, stop=j == CL // 2 - 1)
                    ins.then_inc(mlp1, 1)
                if v == 14:
                    pe.wait_ge(mlp1_silu, 1)
                    pe.wait_ge(w2_in, 32)
                    for kv in range(2):
                        for g in range(NG):
                            ins = mm(ps[0:CP, 6, kv * P + g * DH:kv * P + (g + 1) * DH], hs[:, kv, g * CP:(g + 1) * CP], w2[:, kv, :],
                                     start=True, stop=True)
                    ins.then_inc(mlp2, 1)
                if v == 15:
                    pe.wait_ge(ada_used, ada_ops(4 * KT - 1))
                    sum_columns(1, 32, range(KT)).then_inc(mod_sum, 1)
                if v == 17:
                    pe.wait_ge(kc_rot, 1)
                    pe.wait_ge(mod_read, 7)
                    pe.transpose(ps[:, 7, 0:CP], kcr[:, :], ident[0:CP, 0:CP]).then_inc(kcT, 1)
                if v == U_PROJ - 1:
                    pe.wait_ge(kcT_lo, 1)
                    pe.wait_ge(ada_used, ada_ops(5 * KT - 1))
                    sum_columns(0, 40, range(KT)).then_inc(mod_sum, 1)

            def scores(n):
                i = n // 16
                b, hd = divmod(n % 16, 8)
                h, g = divmod(hd, 2)
                w = (i + 1) * P
                if n == RV_STEPS + 4:
                    pe.wait_ge(proj_ev, TT * (K_RV + 1))
                elif n >= 2:
                    pe.wait_ge(p_exp, n - 1 if n < RV_STEPS + 4 else n - 2)
                g0, g1 = g * DH, (g + 1) * DH
                qs = slice(i * P, (i + 1) * P)
                o = ps[:, s_bank(n), 0:w]
                product(o, QTh[g0:g1, h, qs], QTl[g0:g1, h, qs], KTh[g0:g1, b, 0:w], KTl[g0:g1, b, 0:w], True, False)
                mm(ps[:, s_bank(n), i * P:w], identR[:, :], maskR[:, :], start=False, stop=True).then_inc(s_ps, 1)

            def transposes(n):
                i = n // 16
                pe.wait_ge(p_exp, n + 1)
                if n:
                    pe.wait_ge(pT_ok, n)
                for j in range(i + 1):
                    ins = pe.transpose(ps[:, 2, j * P:(j + 1) * P], Pr[:, n % 3, j * P:(j + 1) * P], ident)
                ins.then_inc(p_T, 1)

            def values(n):
                i = n // 16
                b, hd = divmod(n % 16, 8)
                h, g = divmod(hd, 2)
                head = g * HPG + h
                pe.wait_ge(pT_ok, n + 1)
                if hd == 0 and i:
                    pe.wait_ge(y_sum, 3 * (i - 1) + b + 2)
                for j in range(i + 1):
                    ins = mm(ps[:, 4 + b, head * DH:(head + 1) * DH], PT[:, n % 2, j * P:(j + 1) * P],
                             V[:, j, b, g * DH:(g + 1) * DH], start=j == 0, stop=j == i)
                ins.then_inc(pv, 1)

            def cmp_scores(i):
                if i == 0:
                    pe.wait_ge(kcT_lo, 1)
                    pe.wait_ge(mod_read, 8)
                else:
                    pe.wait_ge(mix_lo, i)
                qs = slice(i * P, (i + 1) * P)
                for g in range(NG):
                    g0, g1 = g * DH, (g + 1) * DH
                    for h in range(HPG):
                        ins = product(ps[:, 6 + g, h * CP:(h + 1) * CP], QTh[g0:g1, h, qs], QTl[g0:g1, h, qs],
                                      KCh[g0:g1, :], KCl[g0:g1, :], True, True)
                ins.then_inc(cs_ps, 1)

            def ret_scores(i, h):
                p0 = (h % 2) * RDK
                if h == 0:
                    pe.wait_ge(cT_ok, i + 1)
                if RH * i + h:
                    pe.wait_ge(r_dec, RH * i + h)
                for j in range(i + 1):
                    ins = mm(ps[:, 6, j * P:(j + 1) * P], rkT[p0:p0 + RDK, h // 2, j * P:(j + 1) * P],
                             rqT[p0:p0 + RDK, h // 2, i * P:(i + 1) * P], start=True, stop=True)
                ins.then_inc(r_s, 1)

            def ret_values(i, h):
                pe.wait_ge(r_dec, RH * i + h + 1)
                pe.wait_ge(proj_ev, TT * K_RV + (1 if i == 0 else TT))
                if h == 0:
                    pe.wait_ge(y_sum, 3 * i + 1)
                for j in range(i + 1):
                    ins = mm(ps[:, 7, h * P:(h + 1) * P], ats[:, h % 2, j * P:(j + 1) * P], rv[:, j, h * P:(h + 1) * P],
                             start=j == 0, stop=j == i)
                ins.then_inc(r_y, 1)

            def mix_transposes(i):
                if i == 0:
                    pe.wait_ge(mod_read, 10)
                pe.wait_ge(y_sum, 3 * (i + 1))
                pe.wait_ge(r_norm, i + 1)
                for k in range(KT):
                    ins = pe.transpose(ps[:, 6 + k // 4, (k % 4) * P:(k % 4 + 1) * P], mix[:, i % 2, k * P:(k + 1) * P], ident)
                ins.then_inc(mixT_ps, 1)

            def rv_piece(t, q):
                if t == 0:
                    pe.wait_ge(w_lo, U_PROJ + q + 1)
                elif q == 0:
                    pe.wait_ge(proj_ev, TT * K_RV + t)
                s = (U_PROJ + q) % SPLIT
                bh = wh[:, s, :].rearrange("p (k n) -> p k n", k=2)
                bl = wl[:, s, :].rearrange("p (k n) -> p k n", k=2)
                tok = slice(t * P, (t + 1) * P)
                for kk in range(2):
                    k = 2 * q + kk
                    ins = product(ps[:, 3, :], hTh[:, k, tok], hTl[:, k, tok], bh[:, kk, :], bl[:, kk, :], k == 0, k == KT - 1)
                if q == UPC - 1:
                    ins.then_inc(o_ps, 1)

            pe.wait_ge(proj_ev, TT * K_RV)
            pe.wait_ge(rot_hi, 10)
            for n in range(16 * TT + 4):
                i, s = divmod(n, 16)
                if n < 16 * TT:
                    scores(n)
                if 3 <= n <= 16 * TT + 2:
                    transposes(n - 3)
                if n >= 4:
                    values(n - 4)
                if n < RV_STEPS:
                    rv_piece(*divmod(n, UPC))
                if s == 0 and i >= 1:
                    ret_values(i - 1, RH - 1)
                if n == RV_STEPS + 4:
                    pe.wait_ge(r_norm, 1)
                    sum_rows(5, 0)
                    sum_rows(5, 1, bank=6)
                if i >= 1 and s == mix_step(i):
                    mix_transposes(i - 1)
                if s == 8 and i < TT:
                    cmp_scores(i)
                if s == 10 and i < TT:
                    pe.wait_ge(c_exp, i + 1)
                    for g in range(NG):
                        ins = pe.transpose(ps[:, 6, g * P:(g + 1) * P], pc[:, g * HPG:(g + 1) * HPG, :], ident)
                    ins.then_inc(c_T, 1)
                if s == 11 and i < TT:
                    pe.wait_ge(cT_ok, i + 1)
                    pe.wait_ge(bd_ok, 1)
                    for g in range(NG):
                        ins = mm(ps[:, 7, g * 256:(g + 1) * 256], pcT[:, g, :], BD[:, g, :], start=True, stop=True)
                    ins.then_inc(c_o, 1)
                if s >= 12:
                    ret_scores(i, s - 12)
                if s >= 13:
                    ret_values(i, s - 13)

            def two_halves(t, u, stat, first, last):
                s = u % SPLIT
                for b in range(2):
                    cols_ = slice(b * 512, (b + 1) * 512)
                    ins = product(ps[:, 2 * t + b, :], stat[0], stat[1], wh[:, s, cols_], wl[:, s, cols_], first, last)
                return ins

            def out_unit(t, k):
                tok = slice(t * P, (t + 1) * P)
                return two_halves(t, U0_OUT + k, (hTh[:, k, tok], hTl[:, k, tok]), k == 0, k == KT - 1)

            pe.wait_ge(w_lo, U0_OUT + 2)
            for k in range(2):
                for t in range(2):
                    out_unit(t, k)
            mix_transposes(TT - 1)
            out_unit(2, 0)
            out_unit(2, 1)
            pe.wait_ge(mix_lo, TT)
            for k in range(KT - TAIL):
                if k >= 2:
                    pe.wait_ge(w_lo, U0_OUT + k + 1)
                for t in range(TT) if k >= 2 else (TT - 1,):
                    ins = out_unit(t, k)
                ins.then_inc(unit_used, 1)

            def h2_transposes(t):
                pe.wait_ge(xb_ok, t + 1)
                for b in range(2):
                    for k in range(4):
                        ins = pe.transpose(ps[:, 2 * t + b, k * P:(k + 1) * P], xb[:, t % 2, (4 * b + k) * P:(4 * b + k + 1) * P], ident)
                    ins.then_inc(xbT, 1)

            pe.wait_ge(w_lo, U0_OUT + KT)
            for t in range(TT):
                for k in range(KT - TAIL, KT):
                    ins = out_unit(t, k)
                ins.then_inc(d_ps, 1)
                if t >= 2:
                    h2_transposes(t - 2)
            h2_transposes(2)

            def gate_up(f, up, c0, c1):
                u = U0_GU + 2 * f + up
                s = u % SPLIT
                pe.wait_ge(w_lo, u + 1)
                o = ps[:, 2 * (f % 2) + up, c0:c1]
                for k in range(KT):
                    ks = slice(k * P, (k + 1) * P)
                    mm(o, wh[:, s, ks], hTh[:, k, c0:c1], start=k == 0, stop=False)
                    mm(o, wh[:, s, ks], hTl[:, k, c0:c1], start=False, stop=False)
                    ins = mm(o, wl[:, s, ks], hTh[:, k, c0:c1], start=False, stop=k == KT - 1)
                return ins

            pe.wait_ge(h2_lo, 4)
            gate_up(0, 0, 0, 2 * P)
            h2_transposes(3)
            pe.wait_ge(h2_lo, 6)
            gate_up(0, 0, 2 * P, 3 * P)
            gate_up(0, 1, 0, 3 * P)
            pe.wait_ge(h2_lo, 8)
            gate_up(0, 0, 3 * P, T).then_inc(gate_ps, 1)
            gate_up(0, 1, 3 * P, T).then_inc(up_ps, 1)
            for f in range(1, FT):
                if f >= 2:
                    pe.wait_ge(act_ok, f - 1)
                gate_up(f, 0, 0, T).then_inc(gate_ps, 1)
                gate_up(f, 1, 0, T).then_inc(up_ps, 1)

            for f in range(FT - TAIL):
                pe.wait_ge(w_lo, U0_DOWN + f + 1)
                pe.wait_ge(a_lo, f + 1)
                for t in range(TT) if f else (2, 3, 0, 1):
                    if f == 0 and t < 2:
                        pe.wait_ge(act_ok, FT - 1 + t)
                    tok = slice(t * P, (t + 1) * P)
                    ins = two_halves(t, U0_DOWN + f, (ah[:, f % SPLIT, tok], al[:, f % SPLIT, tok]), f == 0, False)
                ins.then_inc(a_used, 1)
            pe.wait_ge(w_lo, UNITS)
            pe.wait_ge(a_lo, FT)
            for t in range(TT):
                tok = slice(t * P, (t + 1) * P)
                for f in range(FT - TAIL, FT):
                    ins = two_halves(t, U0_DOWN + f, (ah[:, f % SPLIT, tok], al[:, f % SPLIT, tok]), False, f == FT - 1)
                ins.then_inc(d_ps, 1)


def shape_constants():
    k = np.zeros((P, K_N), np.float32)
    k[:, K_ID:K_ID + P] = np.eye(P, dtype=np.float32)
    q = np.arange(P)
    k[:, K_MASK:K_MASK + P] = np.where(q[None, :] > q[:, None], BIG, 0.0)

    def rope_rows(pos):
        half = DH // 2
        inv = np.float32(10000.0) ** (-np.arange(half, dtype=np.float32) / np.float32(half))
        ang = pos.astype(np.float32)[:, None] * inv
        cos, sin = np.cos(ang), np.sin(ang)
        return np.concatenate([cos, cos, -sin, sin], axis=1)

    r = rope_rows(np.arange(T))
    k[:, K_ROPE:K_ROPE + TT * P] = r.reshape(TT, P, P).transpose(1, 0, 2).reshape(P, TT * P)
    end = np.arange(CP) * CS + CL - 1
    seen = (end[None, :] <= np.arange(T)[:, None]) & (np.arange(CP) < NC)[None, :]
    m = np.where(seen, 0.0, BIG).astype(np.float32)
    k[:, K_CMASK:K_CMASK + TT * CP] = m.reshape(TT, P, CP).transpose(1, 0, 2).reshape(P, TT * CP)
    k[:, K_VALID] = (q >= CL - 1)
    k[0:CP, K_CROPE:K_CROPE + P] = rope_rows(end)
    log_g = np.log(1.0 - 2.0 ** (-5.0 - np.arange(RH)))
    x = np.arange(T)
    diff = (TT - 1 - x[None, :] // P) * P + x[None, :] % P - q[:, None]
    dec = np.where(diff[None] >= 0, np.exp(log_g[:, None, None] * np.maximum(diff, 0)[None]), 0.0)
    return k, np.ascontiguousarray(dec.transpose(1, 0, 2)).astype(np.float32)


_INS = ['x', 'c', 'ln_mix_g', 'ln_ffn_g', 'w_ada', 'b_ada', 'w_in', 'cmp_pe_k', 'cmp_w1_k', 'cmp_w2_k',
        'cmp_pe_v', 'cmp_w1_v', 'cmp_w2_v', 'w_out', 'w_ff_gate', 'w_ff_up', 'w_ff_down', 'ln_final_g']


def kernel(**inputs):
    import numpy as _np
    import concourse.bacc as _bacc
    from concourse import mybir as _mybir
    from concourse.bass_utils import run_bass_kernel_spmd as _run

    nc = _bacc.Bacc("TRN2", target_bir_lowering=False, num_devices=1)
    arrays, args = {}, []
    for name in _INS:
        a = _np.ascontiguousarray(inputs[name])
        if name != 'ln_final_g':
            a = a[0]
        arrays[f"in_{name}"] = a
        args.append(nc.dram_tensor(f"in_{name}", a.shape, _mybir.dt.from_np(a.dtype), kind="ExternalInput").ap())
    for name, a in zip(("consts", "decays"), shape_constants()):
        arrays[f"in_{name}"] = a
        args.append(nc.dram_tensor(f"in_{name}", a.shape, _mybir.dt.float32, kind="ExternalInput").ap())
    args.append(nc.dram_tensor("out_0", (T, D), _mybir.dt.float32, kind="ExternalOutput").ap())
    block_kernel(nc, *args)
    r = _run(nc, [arrays], core_ids=[0])
    return r.results[0]["out_0"].reshape(1, T, D)
```

```python
from contextlib import ExitStack

import numpy as np

import concourse.bass as bass
from concourse import mybir

F32 = mybir.dt.float32
F32R = mybir.dt.float32r
ALU = mybir.AluOpType
ACT = mybir.ActivationFunctionType
AX = mybir.AxisListType

P = 128
T, D, DFF = 512, 1024, 2816
TT, KT, FT = T // P, D // P, DFF // P
RH, RDK, RDV = 4, 64, 128
NH, NG, HPG, DH = 8, 2, 4, 64
CL, CS, CHID = 32, 16, 128
NC = T // CS - CL // CS + 1
CP = 32
EPS = 1e-6
BIG = 1e30
QSCALE = -(DH ** -0.5)

C_CMP = 2048
C_Q = 1536
C_WIN = 2560
C_RQK = 0
C_RV = 512
C_RG = 1024
CHUNKS = [(C_CMP, 512), (C_Q, 512), (C_RQK, 512), (C_WIN, 280), (C_RV, 512), (C_RG, 512)]
K_CMP, K_Q, K_RQK, K_WIN, K_RV, K_RG = range(6)
UPC = 4
U_PROJ = UPC * K_RV
U_IN, U_OUT, U_GU, U_DOWN = UPC * len(CHUNKS), KT, 2 * FT, FT
U0_OUT = U_IN
U0_GU = U0_OUT + U_OUT
U0_DOWN = U0_GU + U_GU
UNITS = U0_DOWN + U_DOWN
OUT_TAIL = KT // 2
DOWN_TAIL = 3
LATE_STEPS = 2 * TT * UPC
THREE = 36
assert THREE % 6 == 0 and THREE > LATE_STEPS
OUT_STEPS = (41, 43, 51, 55)
SPLIT = 4
RAW = 7
AHEAD = 4
EARLY = 8

ADA = [1, 0, 2, 4, 3, 5]
ADA_START = 16
ADA_LATE = 5 * KT
ADA_OPS = 4 * ADA_START

K_ID, K_MASK, K_ROPE, K_CMASK, K_VALID, K_CROPE = 0, 128, 256, 768, 896, 900
K_GROUP = 1028
K_N = 1030


def stream():
    items = []
    for q in range(UPC):
        items += [("early", 4 * q + j) for j in range(4)] + [("w", q)]
    a = ADA_START
    for u in range(3, UNITS):
        if u > 3:
            items.append(("w", u))
        if u <= U_PROJ + 2:
            upto = ADA_START - (-(ADA_LATE - ADA_START) * (u - 2) // U_PROJ)
        else:
            upto = KT * len(ADA)
        while a < upto:
            items.append(("ada", a))
            a += 1
    return items


def block_kernel(nc, x, c, ln_mix_g, ln_ffn_g, w_ada, b_ada, w_in, cmp_pe_k, cmp_w1_k, cmp_w2_k,
                 cmp_pe_v, cmp_w1_v, cmp_w2_v, w_out, w_ff_gate, w_ff_up, w_ff_down, ln_final_g,
                 consts, decays, out):
    items = stream()
    ring = [it for it in items if it[0] != "early"]
    place = {it: (n % RAW, 16 * (n // RAW + 1)) for n, it in enumerate(ring)}
    ada_after = {}
    last_w = -1
    for kind, j in items:
        if kind == "w":
            last_w = j
        elif kind == "ada" and j < ADA_LATE:
            ada_after.setdefault(last_w, []).append(j)

    def ada_ops(j):
        return 8 * (j // 2 + 1) - (j + 1) % 2 if j < ADA_START else ADA_OPS + j - ADA_START + 1

    with ExitStack() as ctx:
        KB = 1024
        BASE = 16512

        def at(name, shape, dt, kb):
            return nc.alloc_sbuf_tensor_at(name, shape, dt, offset=BASE + int(kb * KB))

        small_at = [112 * KB + 4128]

        def small(name, shape, dt=F32):
            kb = small_at[0] / KB
            small_at[0] += (4 * int(np.prod(shape[1:])) + 31) // 32 * 32
            return at(name, shape, dt, kb)

        hTh = at("hTh", [P, KT, T], F32R, 0)
        hTl = at("hTl", [P, KT, T], F32R, 16)
        ga1 = at("ga1", [P, D], F32, 32)
        ga2 = at("ga2", [P, D], F32, 36)
        gfin = at("gfin", [P, D], F32, 40)
        acc2 = at("acc2", [P, D], F32, 40)
        flatT = at("flatT", [P, CL // 2, P], F32, 36)
        wh = at("wh", [P, SPLIT, D], F32R, 44)
        wl = at("wl", [P, SPLIT, D], F32R, 60)
        raw = at("raw", [P, RAW, D], F32, 76)
        acc = at("acc", [P, 2, D], F32, 104)
        cst = at("cst", [P, K_N], F32, 112)
        R = 122
        xT = at("xT", [P, KT, T], F32, R)
        early = at("early", [P, EARLY, D], F32, R + 16)
        xs = at("xs", [P, TT, D], F32, R + 54)
        hf = at("hf", [P, 2, T], F32, R + 70)
        junk = at("junk", [P, D], F32, R + 74)
        QTh = at("QTh", [P, HPG, T], F32R, R)
        QTl = at("QTl", [P, HPG, T], F32R, R + 8)
        KTh = at("KTh", [P, 2, T], F32R, R + 16)
        KTl = at("KTl", [P, 2, T], F32R, R + 20)
        V = at("V", [P, TT, 2, P], F32, R + 24)
        rqT = at("rqT", [P, 2, T], F32, R + 28)
        rkT = at("rkT", [P, 2, T], F32, R + 32)
        w1 = at("w1", [P, 2, CL // 2, CHID], F32, R + 36)
        rv = at("rv", [P, TT, RH * RDV], F32, R + 36)
        rg = at("rg", [P, TT, RH * RDV], F32, R + 44)
        stage = at("stage", [P, TT, 512], F32, R + 54)
        rot = at("rot", [P, TT, 512], F32, R + 62)
        rt = at("rt", [P, 2, 512], F32, R + 70)
        flat = at("flat", [P, CL * DH], F32, R + 74)
        Pr = at("Pr", [P, 3, T], F32, R + 54)
        PT = at("PT", [P, 2, T], F32, R + 60)
        mix = at("mix", [P, 2, D], F32, R + 64)
        ats = at("ats", [P, 2, T], F32, R + 72)
        stage_w = at("stage_w", [P, TT, P], F32, R + 74)
        rot_w = at("rot_w", [P, TT, P], F32, R + 44)
        decay = at("decay", [P, RH, T], F32, R + 76)
        sc = at("sc", [P, NH, CP], F32, 104)
        pc = at("pc", [P, NH, CP], F32, 105)
        pcT = at("pcT", [P, NG, P], F32, 106)
        tmpo = at("tmpo", [P, T], F32, 107)
        sqj = at("sqj", [P, T], F32, 109)
        wxh = at("wxh", [P, OUT_TAIL, D], F32R, R + 16)
        wxl = at("wxl", [P, OUT_TAIL, D], F32R, R + 32)
        x1 = at("x1", [P, TT, D], F32, R)
        act = at("act", [P, FT, T], F32, R + 16)
        ah = at("ah", [P, SPLIT, T], F32R, R + 60)
        al = at("al", [P, SPLIT, T], F32R, R + 68)
        xb = at("xb", [P, 2, D], F32, R + 76)
        sg = at("sg", [P, 2, T], F32, R + 76)
        h2 = at("h2", [P, 2, 4, P], F32, 108)
        BD = small("BD", [P, NG, HPG * DH])
        w2 = small("w2", [P, 2, DH])
        identR = small("identR", [P, P], F32R)
        maskR = small("maskR", [P, P], F32R)
        KCh = small("KCh", [P, NG, CP], F32R)
        KCl = small("KCl", [P, NG, CP], F32R)
        rows = at("rows", [P, P], F32, 108)
        cols = small("cols", [P, 88])
        cs = small("cs", [P, KT])
        mods = small("mods", [P, 4, KT])
        crow = at("crow", [KT, P], F32, R + 53)
        ones = at("ones", [P, P], F32, R + 52)
        ssq = small("ssq", [P, TT])
        ssq2 = small("ssq2", [P, TT])
        rstd = small("rstd", [P, TT])
        expo = small("expo", [P, TT])
        mn = small("mn", [P, 8])
        den = small("den", [P, 2, 2, NH])
        gates = small("gates", [P, TT, 3 * NH])
        rgt = small("rgt", [P, NH])
        mnc = small("mnc", [P, NH])
        yss = small("yss", [P, RH])
        hs = small("hs", [P, 2, 2 * CP])
        assert small_at[0] <= 122 * KB, small_at[0] / KB
        kcr = at("kcr", [CP, P], F32, R + 52.5)

        ident = cst[:, K_ID:K_ID + P]
        rope = cst[:, K_ROPE:K_ROPE + TT * P].rearrange("p (t n) -> p t n", t=TT)
        cmask = cst[:, K_CMASK:K_CMASK + TT * CP].rearrange("p (t n) -> p t n", t=TT)

        ps = ctx.enter_context(nc.psum_tensor("ps", [P, 8, 512], F32))

        kv_dram = nc.dram_tensor("kv_scratch", (T, 2 * P), F32, kind="Internal").ap()

        def sem(name):
            return ctx.enter_context(nc.semaphore(name))

        raw_in = [sem(f"raw_in{i}") for i in range(RAW)]
        early_in = [sem(f"early_in{i}") for i in range(EARLY)]
        rows_in, biases_in, ident_in, const_in, w1_in, w2_in = sem("rows_in"), sem("biases_in"), sem("ident_in"), sem("const_in"), sem("w1_in"), sem("w2_in")
        bias1_in, bias2_in = sem("bias1_in"), sem("bias2_in")
        gfin_in, decay_in, flat_in = sem("gfin_in"), sem("decay_in"), sem("flat_in")
        x_in = [sem(f"x_in{t}") for t in range(TT)]
        xagain_in, kv_out = sem("xagain_in"), sem("kv_out")
        out_done = [sem(f"out_done{t}") for t in range(TT)]
        w_hi, w_lo, unit_used, ada_used = sem("w_hi"), sem("w_lo"), sem("unit_used"), sem("ada_used")
        ones_set, rowsT, cols_ok, c_silu, mod_sum, mod_read = (sem(n) for n in ("ones_set", "rowsT", "cols_ok", "c_silu", "mod_sum", "mod_read"))
        w_scaled = sem("w_scaled")
        h2b_ok, sqv_done = sem("h2b_ok"), sem("sqv_done")
        h_full = sem("h_full")
        sq_done, xn_done, xT_ps, xT_ok, h_hi, h_lo = (sem(n) for n in ("sq_done", "xn_done", "xT_ps", "xT_ok", "h_hi", "h_lo"))
        proj_ev, roped, rotT, rot_hi, rot_lo = (sem(n) for n in ("proj_ev", "roped", "rotT", "rot_hi", "rot_lo"))
        flat_zero, flatT_ps, flatT_ok, mlp1, mlp1_silu, mlp2, kc_rot, bd_ok, kcT, kcT_hi, kcT_lo = (
            sem(n) for n in ("flat_zero", "flatT_ps", "flatT_ok", "mlp1", "mlp1_silu", "mlp2", "kc_rot", "bd_ok", "kcT", "kcT_hi", "kcT_lo"))
        late_ps, rg_ok = sem("late_ps"), sem("rg_ok")
        consts_r, var_ok, rstd_ok = sem("consts_r"), sem("var_ok"), sem("rstd_ok")
        N_X, N_RET, N_X1, N_X2 = 1, 2, 2 + TT, 2 + 2 * TT
        s_ps, s_min, p_exp, p_T, pT_ok, pv = (sem(n) for n in ("s_ps", "s_min", "p_exp", "p_T", "pT_ok", "pv"))
        cs_ps, c_pre, c_exp, c_den, c_T, cT_ok, c_o = (sem(n) for n in ("cs_ps", "c_pre", "c_exp", "c_den", "c_T", "cT_ok", "c_o"))
        y_sum, r_s, r_dec, r_y, r_sq, r_norm = (sem(n) for n in ("y_sum", "r_s", "r_dec", "r_y", "r_sq", "r_norm"))
        mixT_ps, mix_hi, mix_lo = (sem(n) for n in ("mixT_ps", "mix_hi", "mix_lo"))
        o_ps, x1_ok, sq2, xb_ok, xbT, h2_ok, h2_hi, h2_lo = (sem(n) for n in ("o_ps", "x1_ok", "sq2", "xb_ok", "xbT", "h2_ok", "h2_hi", "h2_lo"))
        gate_ps, up_ps, sg_ok, act_ok, a_hi, a_lo, a_used = (sem(n) for n in ("gate_ps", "up_ps", "sg_ok", "act_ok", "a_hi", "a_lo", "a_used"))
        d_ps, x2_ok, sq3, y_ok = (sem(n) for n in ("d_ps", "x2_ok", "sq3", "y_ok"))
        gates_ok = sem("gates_ok")
        xn_done2 = sem("xn_done2")
        c_in, cT = sem("c_in"), sem("cT")
        y_ps, y_scaled = sem("y_ps"), sem("y_scaled")
        dve_step = sem("dve_step")

        block = ctx.enter_context(nc.Block())

        def unit(u):
            if u < U0_OUT:
                c0, n = CHUNKS[u // UPC]
                k = 2 * (u % UPC)
                return (w_in[k * P:(k + 2) * P, c0:c0 + n].rearrange("(k p) n -> p k n", p=P),
                        lambda s: s[:, 0:2 * n].rearrange("p (k n) -> p k n", k=2))
            if u < U0_GU:
                k = u - U0_OUT
                return w_out[k * P:(k + 1) * P, :], lambda s: s
            if u < U0_DOWN:
                f, up = divmod(u - U0_GU, 2)
                w = w_ff_up if up else w_ff_gate
                return (w[:, f * P:(f + 1) * P].rearrange("(k p) n -> p k n", p=P),
                        lambda s: s.rearrange("p (k n) -> p k n", k=KT))
            f = u - U0_DOWN
            return w_ff_down[f * P:(f + 1) * P, :], lambda s: s

        def mix_step(i):
            return 6 if i == 1 else 5

        def s_bank(n):
            return n % 2 if n < THREE else (0, 1, 3)[n % 3]

        def split(u, n):
            if U0_OUT + KT - OUT_TAIL <= u < U0_GU:
                k = u - U0_OUT - KT + OUT_TAIL
                return wxh[:, k, 0:n], wxl[:, k, 0:n]
            return wh[:, u % SPLIT, 0:n], wl[:, u % SPLIT, 0:n]

        def size(u):
            return 2 * CHUNKS[u // UPC][1] if u < U0_OUT else D

        @block.sync
        def _(sp):
            def refill(n):
                if n >= RAW:
                    kind, j = ring[n - RAW]
                    if kind == "w":
                        sp.wait_ge(w_lo, j + 1)
                    else:
                        sp.wait_ge(ada_used, ada_ops(j))
                kind, j = ring[n]
                slot = n % RAW
                if kind == "w":
                    src, view = unit(j)
                    sp.dma_start(view(raw[:, slot, :]), src).then_inc(raw_in[slot], 16)
                else:
                    g, k = divmod(j, KT)
                    col = ADA[g] * D
                    sp.dma_start(raw[:, slot, :], w_ada[k * P:(k + 1) * P, col:col + D]).then_inc(raw_in[slot], 16)

            def load_early(j):
                if j >= EARLY:
                    sp.wait_ge(ada_used, ada_ops(j - EARLY))
                q, kh, i = j // 4, j // 2 % 2, j % 2
                col = ADA[i] * D + 2 * q * P
                sp.dma_start(early[:, j % EARLY, :].rearrange("p (k n) -> p k n", k=4),
                             w_ada[4 * kh * P:4 * (kh + 1) * P, col:col + 2 * P].rearrange("(k p) n -> p k n", p=P))\
                  .then_inc(early_in[j % EARLY], 16)

            sp.dma_start(crow[:, :], c.rearrange("(r n) -> r n", n=P)).then_inc(c_in, 16)
            sp.dma_start(cst[:, 0:P], consts[:, 0:P]).then_inc(ident_in, 16)
            for t in range(TT):
                sp.dma_start(xs[:, t, :], x[t * P:(t + 1) * P, :]).then_inc(x_in[t], 16)
            for kind, j in items:
                if kind == "early":
                    load_early(j)
                    continue
                if (kind, j) == ("w", 2):
                    sp.dma_start(cst[:, P:K_N], consts[:, P:K_N]).then_inc(const_in, 16)
                if kind == "w" and j in (9, 11):
                    sp.wait_ge(ada_used, ADA_OPS)
                    i = (j - 9) // 2
                    sp.dma_start(w1[:, i, :, :], (cmp_w1_k, cmp_w1_v)[i].rearrange("(j p) n -> p j n", p=P)).then_inc(w1_in, 16)
                if (kind, j) == ("w", 20):
                    sp.wait_ge(flatT_ok, 4)
                    sp.dma_start(decay[:, :, :], decays).then_inc(decay_in, 16)
                if (kind, j) == ("w", U0_GU - 1):
                    sp.wait_ge(mod_read, 10)
                    sp.dma_start(gfin[:, :], ln_final_g.partition_broadcast(P)).then_inc(gfin_in, 16)
                    sp.wait_ge(s_ps, 16 * TT)
                    sp.wait_ge(cs_ps, TT)
                    for t in range(TT):
                        sp.dma_start(x1[:, t, :], x[t * P:(t + 1) * P, :]).then_inc(xagain_in, 16)
                refill(ring.index((kind, j)))
            for t in range(TT):
                sp.wait_ge(y_ok, t + 1)
                sp.dma_start(out[t * P:(t + 1) * P, :], xb[:, t % 2, :]).then_inc(out_done[t], 16)
            for t in range(TT):
                sp.wait_ge(out_done[t], 16)

        @block.gpsimd
        def _(pool):
            pool.memset(rows[:, :], 0.0).then_inc(ones_set, 1)
            pool.memset(ones[:, :], 1.0).then_inc(ones_set, 1)
            pool.memset(BD[:, :, :], 0.0).then_inc(ones_set, 1)
            pool.memset(expo[:, :], -0.5).then_inc(ones_set, 1)
            pool.wait_ge(ones_set, 1)
            for dst, src in ((24, b_ada[0:2 * D]), (40, b_ada[3 * D:5 * D])):
                v = src.rearrange("(r n) -> r n", n=P)
                pool.dma_start(rows[dst:dst + v.shape[0], :], v).then_inc(biases_in, 16)
            for dst, pe_ in ((56, cmp_pe_k), (72, cmp_pe_v)):
                pool.dma_start(rows[dst:dst + CL // 2, :].rearrange("j (l d) -> j l d", d=DH),
                               pe_.rearrange("(j l) d -> j l d", l=2)).then_inc(biases_in, 16)

            def low(u):
                slot, count = place[("w", u)]
                n = size(u)
                pool.wait_ge(raw_in[slot], count)
                pool.wait_ge(w_hi, u + 1)
                hi, lo = split(u, n)
                pool.tensor_tensor(lo, raw[:, slot, 0:n], hi.bitcast(F32), ALU.subtract).then_inc(w_lo, 1)

            def power(n, buf):
                pool.wait_ge(var_ok, n)
                pool.tensor_tensor(buf, buf, expo[:, 0:buf.shape[1]], ALU.pow).then_inc(rstd_ok, 1)

            pool.wait_ge(ones_set, 4)
            power(N_X, rstd[:, :])
            pool.dma_start(ga1[:, :], b_ada[2 * D:3 * D].partition_broadcast(P)).then_inc(bias1_in, 16)
            for u in range(UNITS):
                for i in {U0_OUT: (0, 1), U0_OUT + 2: (2,), U0_OUT + 4: (3,)}.get(u, ()):
                    power(N_RET + i, yss[:, :])
                if u == U0_GU + SPLIT:
                    for t in range(TT):
                        power(N_X1 + t, rstd[:, t:t + 1])
                if u == 3:
                    pool.wait_ge(sq_done, TT // 2)
                    pool.memset(flat[:, :], 0.0).then_inc(flat_zero, 1)
                if u == 18:
                    pool.wait_ge(mlp1, 1)
                    pool.dma_start(ga2[:, :], b_ada[5 * D:6 * D].partition_broadcast(P)).then_inc(bias2_in, 16)
                low(u)
            for t in range(TT):
                power(N_X2 + t, rstd[:, t:t + 1])

        @block.scalar
        def _(a):
            def wait_used(u):
                if u < U_PROJ:
                    a.wait_ge(unit_used, u + 1)
                elif u < U0_OUT:
                    c_, q = divmod(u - U_PROJ, UPC)
                    a.wait_ge(late_ps, TT * UPC * c_ + (TT - 1) * UPC + q + 1)
                elif u < U0_GU:
                    a.wait_ge(unit_used, u + 1 - (U_IN - U_PROJ))
                elif u < U0_DOWN:
                    f, up = divmod(u - U0_GU, 2)
                    a.wait_ge(up_ps if up else gate_ps, f + 1)
                else:
                    a.wait_ge(a_used, u - U0_DOWN + 1)

            def high(u):
                slot, count = place[("w", u)]
                n = size(u)
                a.wait_ge(raw_in[slot], count)
                if U0_GU <= u < U0_GU + SPLIT:
                    wait_used(u - SPLIT - OUT_TAIL)
                elif u >= U0_GU or SPLIT <= u < U0_OUT + SPLIT:
                    wait_used(u - SPLIT)
                if U0_OUT <= u < U0_GU or u >= U0_DOWN:
                    a.wait_ge(w_scaled, u - U0_OUT + 1 if u < U0_GU else U_OUT + u - U0_DOWN + 1)
                a.activation(split(u, n)[0], raw[:, slot, 0:n], ACT.Copy).then_inc(w_hi, 1)

            a.wait_ge(ones_set, 1)
            for dst, src in ((8, ln_mix_g), (16, ln_ffn_g)):
                v = src.rearrange("(r n) -> r n", n=P)
                a.dma_start(rows[dst:dst + v.shape[0], :], v).then_inc(rows_in, 16)
            a.dma_start(w2[:, 0, :], cmp_w2_k).then_inc(w2_in, 16)
            a.dma_start(w2[:, 1, :], cmp_w2_v).then_inc(w2_in, 16)

            a.wait_ge(cT, 1)
            a.activation(cs[:, :], ps[:, 5, 0:KT], ACT.Silu).then_inc(c_silu, 1)
            for t in range(0, TT, 2):
                a.wait_ge(x_in[t], 16)
                if t:
                    a.wait_ge(sq_done, t // 2)
                a.activation(junk[:, :], xs[:, t, :], ACT.Square, accum_out=ssq[:, t:t + 1]).then_inc(sq_done, 1)
            a.wait_ge(ident_in, 16)
            a.activation(identR[:, :], ident, ACT.Copy).then_inc(consts_r, 1)
            a.wait_ge(rstd_ok, N_X)
            for t in (2, 3):
                a.activation(xs[:, t, :], xs[:, t, :], ACT.Copy, scale=rstd[:, t:t + 1]).then_inc(xn_done2, 1)
            high(0)
            for k in range(KT):
                a.wait_ge(xT_ps, k + 1)
                a.activation(xT[:, k, :], ps[:, k % 4, :], ACT.Copy).then_inc(xT_ok, 1)
            for k in range(KT):
                if k % 2 and k < KT - 1:
                    high(k // 2 + 1)
                a.wait_ge(mod_read, k // 2 + 1)
                a.wait_ge(xT_ok, k + 1)
                if k >= 2:
                    a.wait_ge(h_lo, k - 1)
                a.activation(hf[:, k % 2, :], xT[:, k, :], ACT.Identity, bias=mods[:, 1, k:k + 1],
                             scale=mods[:, 0, k:k + 1]).then_inc(h_full, 1)
                a.wait_ge(h_full, k + 1)
                a.activation(hTh[:, k, :], hf[:, k % 2, :], ACT.Copy).then_inc(h_hi, 1)

            def evacuate(ch, tiles=range(TT)):
                for t in tiles:
                    if ch >= K_RV:
                        a.wait_ge(late_ps, (TT * (ch - K_RV) + t + 1) * UPC)
                    elif t < TT - 1:
                        a.wait_ge(o_ps, (TT - 1) * ch + t + 1)
                    else:
                        a.wait_ge(unit_used, UPC * (ch + 1))
                    if K_CMP < ch < K_RV:
                        a.wait_ge(roped, TT * (ch - 1) + t + 1)
                    if ch == K_CMP:
                        a.activation(stage[:, t, 0:384], ps[:, t, 0:384], ACT.Copy)
                        ins = a.activation(V[:, t, 0, :], ps[:, t, 384:512], ACT.Copy)
                    elif ch == K_Q:
                        a.wait_ge(kv_out, 16 * TT)
                        ins = a.activation(stage[:, t, :], ps[:, t, :], ACT.Copy)
                    elif ch == K_WIN:
                        a.activation(stage_w[:, t, :], ps[:, t, 0:P], ACT.Copy)
                        a.activation(V[:, t, 1, :], ps[:, t, P:2 * P], ACT.Copy)
                        ins = a.activation(gates[:, t, :], ps[:, t, 2 * P:2 * P + 3 * NH], ACT.Tanh, scale=0.5)
                    elif ch == K_RQK:
                        ins = a.activation(stage[:, t, :], ps[:, t, :], ACT.Copy)
                    elif ch == K_RG:
                        ins = a.activation(rg[:, t, :], ps[:, 3, :], ACT.Tanh, scale=0.5)
                    else:
                        ins = a.activation(rv[:, t, :], ps[:, 3, :], ACT.Copy)
                    ins.then_inc(proj_ev, 1)
                    if ch == K_CMP:
                        a.wait_ge(proj_ev, t + 1)
                        a.dma_start(kv_dram[t * P:(t + 1) * P, :], stage[:, t, 0:2 * P]).then_inc(kv_out, 16)

            def load_blocks():
                a.wait_ge(kv_out, 16 * TT)
                a.wait_ge(flat_zero, 1)
                for kv in range(2):
                    for g in range(NG):
                        row = (kv * NG + g) * CP
                        col = (kv * NG + g) * DH
                        src = kv_dram[0:NC * CS, col:col + DH].rearrange("(c l) d -> c l d", l=CS)
                        nxt = kv_dram[CS:(NC + 1) * CS, col:col + DH].rearrange("(c l) d -> c l d", l=CS)
                        dst = flat[row:row + NC, :].rearrange("c (h l d) -> c h l d", h=2, d=DH)
                        a.dma_start(dst[:, 0], src).then_inc(flat_in, 16)
                        a.dma_start(dst[:, 1], nxt).then_inc(flat_in, 16)

            def rot_high(n):
                a.wait_ge(rotT, n + 1)
                src = ps[:, 4 + n % 2, :]
                if n == 0 or n == 9:
                    ins = a.activation(KTh[:, n // 9, :], src, ACT.Copy)
                elif n < 5:
                    t = n - 1
                    ins = a.activation(QTh[:, :, t * P:(t + 1) * P], src.rearrange("p (h q) -> p h q", h=HPG),
                                       ACT.Copy, scale=QSCALE)
                else:
                    t = n - 5
                    v = src.rearrange("p (h q) -> p h q", h=4)
                    a.activation(rqT[:, :, t * P:(t + 1) * P], v[:, 0:2], ACT.Copy)
                    ins = a.activation(rkT[:, :, t * P:(t + 1) * P], v[:, 2:4], ACT.Copy, scale=RDK ** -0.5)
                ins.then_inc(rot_hi, 1)

            a.wait_ge(const_in, 16)
            a.activation(maskR[:, :], cst[:, K_MASK:K_MASK + P], ACT.Copy).then_inc(consts_r, 1)
            for v in range(U_PROJ):
                if v and v % UPC == 0:
                    evacuate(v // UPC - 1)
                if v:
                    high(v + 3)
                if v == 5:
                    load_blocks()
                for n in {7: [0], 10: [1, 2], 12: [3, 4], 14: [5, 6]}.get(v, []):
                    rot_high(n)
                if v == 15:
                    a.wait_ge(mlp1, 1)
                    a.activation(hs[:, :, :], ps[:, 7, 0:4 * CP].rearrange("p (i n) -> p i n", i=2), ACT.Silu).then_inc(mlp1_silu, 1)
            evacuate(K_WIN)
            high(U_PROJ + 3)
            rot_high(7)
            rot_high(8)

            def exp(n):
                i = n // 16
                w = (i + 1) * P
                b, hd = divmod(n % 16, 8)
                head = hd % NG * HPG + hd // NG
                a.wait_ge(s_min, n + 1)
                if n >= 3:
                    a.wait_ge(p_T, n - 2)
                a.activation(Pr[:, n % 3, 0:w], ps[:, s_bank(n), 0:w], ACT.Exp, bias=mn[:, n % 8:n % 8 + 1], scale=-1.0,
                             accum_out=den[:, i % 2, b, head:head + 1]).then_inc(p_exp, 1)

            def pT_copy(n):
                w = (n // 16 + 1) * P
                a.wait_ge(p_T, n + 1)
                if n >= 2:
                    a.wait_ge(pv, n - 1)
                a.activation(PT[:, n % 2, 0:w], ps[:, 2, 0:w], ACT.Copy).then_inc(pT_ok, 1)

            def mix_high(i):
                a.wait_ge(mixT_ps, i + 1)
                a.activation(hTh[:, :, i * P:(i + 1) * P], ps[:, 6:8, :].rearrange("p b (k q) -> p (b k) q", k=4),
                             ACT.Copy).then_inc(mix_hi, 1)

            def ret_squares(i):
                a.wait_ge(r_y, RH * (i + 1))
                for h in range(RH):
                    ins = a.activation(sqj[:, h * P:(h + 1) * P], ps[:, 7, h * P:(h + 1) * P], ACT.Square,
                                       accum_out=yss[:, h:h + 1])
                ins.then_inc(r_sq, 1)

            for n in range(16 * TT + 7):
                i, s = divmod(n, 16)
                if n % UPC == 0 and UPC <= n <= LATE_STEPS:
                    ch, t = divmod(n // UPC - 1, TT)
                    evacuate(K_RV + ch, [t])
                if 1 <= n <= 16 * TT:
                    exp(n - 1)
                if 3 <= n <= 16 * TT + 2:
                    pT_copy(n - 3)
                if n == 5:
                    a.wait_ge(kcT, 1)
                    for g in range(NG):
                        ins = a.activation(KCh[:, g, :], ps[:, 7, 0:CP], ACT.Copy, scale=cst[:, K_GROUP + g:K_GROUP + g + 1])
                    ins.then_inc(kcT_hi, 1)
                if n == 4:
                    rot_high(9)
                if 14 <= n < 14 + UPC:
                    high(U_PROJ + UPC + n - 14)
                if n - 1 in OUT_STEPS:
                    high(U0_OUT + OUT_STEPS.index(n - 1))
                if s == 1 and i >= 1:
                    ret_squares(i - 1)
                if i >= 1 and s == mix_step(i) + 1:
                    mix_high(i - 1)
                if s == 9 and i < TT:
                    a.wait_ge(c_pre, i + 1)
                    a.activation(pc[:, :, :], sc[:, :, :], ACT.Exp, scale=-1.0).then_inc(c_exp, 1)
                if s == 10 and i < TT:
                    a.wait_ge(c_T, i + 1)
                    a.activation(pcT[:, :, :], ps[:, 6, 0:2 * P].rearrange("p (g q) -> p g q", g=NG), ACT.Copy).then_inc(cT_ok, 1)

            a.wait_ge(pv, 16 * TT)
            a.wait_ge(r_norm, TT)
            for u in range(U0_OUT + SPLIT, U0_GU + SPLIT):
                high(u)

            def x1_square(t):
                a.wait_ge(x1_ok, t + 1)
                a.activation(xb[:, t % 2, :], x1[:, t, :], ACT.Square, accum_out=ssq[:, t:t + 1]).then_inc(sq2, 1)

            def modulate(t):
                a.wait_ge(xbT, 2 * t + 2)
                if t:
                    a.wait_ge(h2_lo, 2 * t - 1)
                for k in range(4):
                    ins = a.activation(h2[:, 1, k, :], ps[:, 2 * t + 1, k * P:(k + 1) * P], ACT.Identity,
                                       bias=mods[:, 3, 4 + k:5 + k], scale=mods[:, 2, 4 + k:5 + k])
                ins.then_inc(h2b_ok, 1)
                a.wait_ge(h2b_ok, t + 1)
                a.activation(hTh[:, 4:8, t * P:(t + 1) * P], h2[:, 1], ACT.Copy).then_inc(h2_hi, 1)
                a.wait_ge(h2_ok, t + 1)
                a.activation(hTh[:, 0:4, t * P:(t + 1) * P], h2[:, 0], ACT.Copy).then_inc(h2_hi, 1)

            x1_square(0)
            for t in range(TT):
                if t < TT - 1:
                    x1_square(t + 1)
                modulate(t)

            def a_high(f):
                a.wait_ge(act_ok, f + 1)
                if f >= SPLIT:
                    a.wait_ge(a_used, f - SPLIT + 1)
                a.activation(ah[:, f % SPLIT, :], act[:, f, :], ACT.Copy).then_inc(a_hi, 1)

            for f in range(FT):
                a.wait_ge(gate_ps, f + 1)
                if f >= 2:
                    a.wait_ge(act_ok, f - 1)
                a.activation(sg[:, f % 2, :], ps[:, 2 * (f % 2), :], ACT.Silu).then_inc(sg_ok, 1)
                high(U0_GU + 2 * f + 4)
                high(U0_GU + 2 * f + 5)
                if 2 <= f < 2 + SPLIT:
                    a_high(f - 2)

            for f in range(SPLIT, FT):
                a_high(f)
                high(U0_DOWN + f)
            for t in range(TT):
                for half in range(2):
                    a.wait_ge(x2_ok, 2 * t + half + 1)
                    cols_ = slice(half * 512, (half + 1) * 512)
                    if t >= 2 and half == 0:
                        a.wait_ge(out_done[t - 2], 16)
                    a.activation(xb[:, t % 2, cols_], x1[:, t, cols_], ACT.Square,
                                 accum_out=(ssq, ssq2)[half][:, t:t + 1]).then_inc(sq3, 1)

        @block.vector
        def _(v_):
            d = v_
            steps = [0]

            def then(ins):
                steps[0] += 1
                ins.then_inc(dve_step, 1)
                d.wait_ge(dve_step, steps[0])

            def ada_early(q, ops):
                for o in ops:
                    p, (kk, i) = 2 * q + o // 8, divmod(o % 8, 2)
                    j, k = 2 * p + i, 4 * (p % 2) + kk
                    d.wait_ge(early_in[j % EARLY], 16 * (j // EARLY + 1))
                    dst = acc[:, i, 2 * q * P:2 * (q + 1) * P]
                    src = early[:, j % EARLY, 2 * kk * P:2 * (kk + 1) * P]
                    if k == 0:
                        d.tensor_scalar(dst, src, cs[:, k:k + 1], None, ALU.mult).then_inc(ada_used, 1)
                    else:
                        d.wait_ge(ada_used, 16 * q + o - 1)
                        d.scalar_tensor_tensor(dst, src, cs[:, k:k + 1], dst, ALU.mult, ALU.add).then_inc(ada_used, 1)

            def ada(j):
                g, k = divmod(j, KT)
                slot, count = place[("ada", j)]
                if k == 0 and g in (3, 4):
                    d.wait_ge(mod_sum, {3: 4, 4: 6}[g])
                if k == 0 and g == 5:
                    d.wait_ge(mlp1, 1)
                d.wait_ge(raw_in[slot], count)
                dst = acc2[:, :] if g == 5 else acc[:, g % 2, :]
                if k == 0:
                    d.tensor_scalar(dst, raw[:, slot, :], cs[:, k:k + 1], None, ALU.mult).then_inc(ada_used, 1)
                else:
                    d.wait_ge(ada_used, ada_ops(j) - 1)
                    d.scalar_tensor_tensor(dst, raw[:, slot, :], cs[:, k:k + 1], dst, ALU.mult, ALU.add).then_inc(ada_used, 1)

            def mod_columns(n, i, c0, k0, k1, b_off, g_off):
                d.wait_ge(mod_sum, n)
                dst = mods[:, i, k0:k1]
                add = d.tensor_tensor(dst, ps[:, 7, c0:c0 + k1 - k0], cols[:, b_off + k0:b_off + k1], ALU.add)
                if g_off is None:
                    return add
                then(add)
                return d.tensor_tensor(dst, dst, cols[:, g_off + k0:g_off + k1], ALU.mult)

            for t in range(1, TT, 2):
                d.wait_ge(x_in[t], 16)
                then(d.tensor_tensor_reduce(out=hf[:, :, :].rearrange("p a b -> p (a b)"), in0=xs[:, t, :], in1=xs[:, t, :], scale=1.0,
                                            scalar=0.0, op0=ALU.mult, op1=ALU.add, accum_out=ssq[:, t:t + 1]))
            d.wait_ge(sq_done, TT // 2)
            d.tensor_scalar(rstd[:, :], ssq[:, :], 1.0 / D, EPS, ALU.mult, ALU.add).then_inc(var_ok, 1)
            d.wait_ge(rowsT, 1)
            d.tensor_copy(cols[:, :], ps[:, 4, 0:88]).then_inc(cols_ok, 1)
            d.wait_ge(cols_ok, 1)
            for i in (0, 2):
                off = 32 if i == 0 else 48
                then(d.tensor_scalar(cols[:, off:off + KT], cols[:, off:off + KT], 1.0, None, ALU.add))
            d.wait_ge(rstd_ok, N_X)
            for t in range(TT // 2):
                d.tensor_scalar(xs[:, t, :], xs[:, t, :], rstd[:, t:t + 1], None, ALU.mult).then_inc(xn_done, 1)

            def mod_rows(n, ga, half, bank=7):
                d.wait_ge(mod_sum, n)
                d.wait_ge(bias1_in if ga is ga1 else bias2_in, 16)
                h = ga[:, half * 512:(half + 1) * 512]
                d.tensor_tensor(h, ps[:, bank, :], h, ALU.add).then_inc(mod_read, 1)

            d.wait_ge(c_silu, 1)
            def h_low(k):
                d.wait_ge(h_hi, k + 1)
                d.tensor_tensor(hTl[:, k, :], hf[:, k % 2, :], hTh[:, k, :].bitcast(F32), ALU.subtract).then_inc(h_lo, 1)

            ada_early(0, range(16))
            ada_early(1, range(AHEAD))
            for q in range(UPC):
                mod_columns(q + 1, 0, 4 * q, 2 * q, 2 * q + 2, 32, 8)
                mod_columns(q + 1, 1, 4 * q + 2, 2 * q, 2 * q + 2, 24, None).then_inc(mod_read, 1)
                if q < UPC - 1:
                    ada_early(q + 1, range(AHEAD, AHEAD + 3))
                h_low(2 * q)
                if q < UPC - 1:
                    ada_early(q + 1, range(AHEAD + 3, AHEAD + 5))
                h_low(2 * q + 1)
                if q < UPC - 1:
                    ada_early(q + 1, range(AHEAD + 5, 16))
                if q < UPC - 2:
                    ada_early(q + 2, range(AHEAD))

            def scale_unit(u):
                slot, count = place[("w", u)]
                ga = ga1 if u < U0_GU else ga2
                if u == U0_OUT:
                    d.wait_ge(mod_read, 6)
                if u == U0_DOWN:
                    d.wait_ge(mod_read, 10)
                d.wait_ge(raw_in[slot], count)
                d.tensor_tensor(raw[:, slot, :], raw[:, slot, :], ga[:, :], ALU.mult).then_inc(w_scaled, 1)

            def rotate(src, table, n, dst, view=lambda x: x, parts=P):
                a0 = rt[0:parts, 0, 0:n * DH].rearrange("p (h x) -> p h x", x=DH)
                a1 = rt[0:parts, 1, 0:n * DH].rearrange("p (h x) -> p h x", x=DH)
                cos = table[:, 0:DH].unsqueeze(1).broadcast_to([parts, n, DH])
                s0 = table[:, DH:DH + 32].unsqueeze(1).broadcast_to([parts, n, 32])
                s1 = table[:, DH + 32:2 * DH].unsqueeze(1).broadcast_to([parts, n, 32])
                d.tensor_tensor(a0, src, cos, ALU.mult)
                d.tensor_tensor(a1[:, :, 0:32], src[:, :, 32:64], s0, ALU.mult)
                then(d.tensor_tensor(a1[:, :, 32:64], src[:, :, 0:32], s1, ALU.mult))
                return d.tensor_tensor(dst, view(a0), view(a1), ALU.add)

            def rope_chunk(ch, tiles):
                for t in tiles:
                    if TT * ch + t:
                        d.wait_ge(roped, TT * ch + t)
                    d.wait_ge(proj_ev, TT * ch + t + 1)
                    if ch == K_CMP:
                        src = stage[:, t, 2 * P:3 * P].rearrange("p (h x) -> p h x", x=DH)
                        dst = rot[:, t, 0:P].rearrange("p (h x) -> p h x", x=DH)
                        rotate(src, rope[:, t, :], 2, dst).then_inc(roped, 1)
                    elif ch == K_Q:
                        if t == 0:
                            d.wait_ge(rotT, 1)
                        src = stage[:, t, :].rearrange("p (h x) -> p h x", x=DH)
                        dst = rot[:, t, :].rearrange("p (h g x) -> p g h x", g=NG, x=DH)
                        rotate(src, rope[:, t, :], NH, dst, lambda z: z.rearrange("p (g h) x -> p g h x", g=NG)).then_inc(roped, 1)
                    elif ch == K_WIN:
                        if t == 0:
                            d.wait_ge(mlp1, 1)
                        src = stage_w[:, t, :].rearrange("p (h x) -> p h x", x=DH)
                        dst = rot_w[:, t, :].rearrange("p (h x) -> p h x", x=DH)
                        rotate(src, rope[:, t, :], 2, dst).then_inc(roped, 1)
                    else:
                        if t == 0:
                            d.wait_ge(rotT, 5)
                        src = stage[:, t, :].rearrange("p (h x) -> p h x", x=DH)
                        dst = rot[:, t, :].rearrange("p (h x) -> p h x", x=DH)
                        rotate(src, rope[:, t, :], NH, dst).then_inc(roped, 1)

            def rot_low(n):
                d.wait_ge(rotT, n + 1)
                d.wait_ge(rot_hi, n + 1)
                src = ps[:, 4 + n % 2, :]
                if n == 0 or n == 9:
                    ins = d.tensor_tensor(KTl[:, n // 9, :], src, KTh[:, n // 9, :].bitcast(F32), ALU.subtract)
                else:
                    t = n - 1
                    ins = d.scalar_tensor_tensor(QTl[:, :, t * P:(t + 1) * P], src.rearrange("p (h q) -> p h q", h=HPG), QSCALE,
                                                 QTh[:, :, t * P:(t + 1) * P].bitcast(F32), ALU.mult, ALU.subtract)
                ins.then_inc(rot_lo, 1)

            def flat_add(b):
                d.wait_ge(flatT_ps, b + 1)
                for kv in range(2):
                    src = ps[:, 6, :].rearrange("p (j n) -> p j n", j=4)[:, :, kv * 2 * CP:(kv + 1) * 2 * CP]
                    pe_ = cols[:, 56 + 16 * kv + 4 * b:60 + 16 * kv + 4 * b].unsqueeze(2).broadcast_to([P, 4, 2 * CP])
                    ins = d.tensor_tensor(flatT[:, 4 * b:4 * b + 4, kv * 2 * CP:(kv + 1) * 2 * CP], src, pe_, ALU.add)
                ins.then_inc(flatT_ok, 1)

            def compressed():
                d.wait_ge(mlp2, 1)
                d.wait_ge(roped, TT * (K_WIN + 1))
                kc = ps[0:CP, 6, 0:P].rearrange("p (g x) -> p g x", g=NG)
                rotate(kc, cst[0:CP, K_CROPE:K_CROPE + P], NG, kcr[:, :].rearrange("p (g x) -> p g x", g=NG),
                       parts=CP).then_inc(kc_rot, 1)
                d.wait_ge(kc_rot, 1)
                d.wait_ge(ones_set, 3)
                for g in range(NG):
                    for h in range(HPG):
                        ins = d.tensor_copy(BD[CP * h:CP * (h + 1), g, h * DH:(h + 1) * DH],
                                            ps[0:CP, 6, P + g * DH:P + (g + 1) * DH])
                ins.then_inc(bd_ok, 1)

            d.wait_ge(const_in, 16)
            for v in range(U_PROJ):
                for n in {7: [0], 10: [1, 2], 12: [3, 4]}.get(v, []):
                    rot_low(n)
                if 10 <= v <= 13:
                    flat_add(v - 10)
                if v == 8:
                    mod_rows(5, ga1, 0)
                if v == 10:
                    mod_rows(6, ga1, 1)
                if 4 <= v and v % UPC < 2:
                    rope_chunk(v // UPC - 1, (0, 1) if v % UPC == 0 else (2, 3))
                for j in ada_after.get(v + 3, []):
                    ada(j)

            def row_min(n):
                w = (n // 16 + 1) * P
                d.wait_ge(s_ps, n + 1)
                if n >= 8:
                    d.wait_ge(p_exp, n - 7)
                d.tensor_reduce(mn[:, n % 8:n % 8 + 1], ps[:, s_bank(n), 0:w], AX.X, ALU.min).then_inc(s_min, 1)

            def heads_view(ap, n=NH):
                return ap.rearrange("p (h x) -> p h x", h=n)

            def add_branch(i, b):
                d.wait_ge(pv, 16 * i + 8 * b)
                then(d.reciprocal(rgt[:, :], den[:, i % 2, b - 1, :]))
                then(d.tensor_tensor(rgt[:, :], rgt[:, :], gates[:, i, b * NH:(b + 1) * NH], ALU.mult))
                then(d.tensor_tensor(heads_view(tmpo[:, :]), heads_view(ps[:, 3 + b, :]),
                                     rgt[:, :].unsqueeze(2).broadcast_to([P, NH, DH]), ALU.mult))
                y = mix[:, i % 2, 512:1024]
                d.tensor_tensor(y, y, tmpo[:, :], ALU.add).then_inc(y_sum, 1)
                d.wait_ge(y_sum, 3 * i + b + 1)

            def cmp_scores(i):
                d.wait_ge(cs_ps, i + 1)
                for g in range(NG):
                    ins = d.tensor_tensor(sc[:, g * HPG:(g + 1) * HPG, :],
                                          ps[:, 6, 0:2 * P].rearrange("p (h g n) -> p g h n", h=HPG, g=NG)[:, g],
                                          cmask[:, i, :].unsqueeze(1).broadcast_to([P, HPG, CP]), ALU.add)
                then(ins)
                then(d.tensor_reduce(mnc[:, :], sc[:, :, :], AX.X, ALU.min))
                d.tensor_tensor(sc[:, :, :], sc[:, :, :], mnc[:, :].unsqueeze(2).broadcast_to([P, NH, CP]), ALU.subtract).then_inc(c_pre, 1)

            def cmp_gates(i):
                d.wait_ge(gates_ok, 1)
                d.wait_ge(c_exp, i + 1)
                then(d.tensor_reduce(mnc[:, :], pc[:, :, :], AX.X, ALU.add))
                then(d.reciprocal(mnc[:, :], mnc[:, :]))
                then(d.tensor_tensor(mnc[:, :], mnc[:, :], gates[:, i, 0:NH], ALU.mult))
                if i == 0:
                    then(d.tensor_scalar(mnc[:, :], mnc[:, :], cst[:, K_VALID:K_VALID + 1], None, ALU.mult))

            def cmp_out(i):
                d.wait_ge(c_o, i + 1)
                if i >= 2:
                    d.wait_ge(mixT_ps, i - 1)
                d.tensor_tensor(heads_view(mix[:, i % 2, 512:1024]), heads_view(ps[:, 7, :]),
                                mnc[:, :].unsqueeze(2).broadcast_to([P, NH, DH]), ALU.mult).then_inc(y_sum, 1)
                d.wait_ge(y_sum, 3 * i + 1)

            def ret_decay(i, h):
                d.wait_ge(r_s, RH * i + h + 1)
                if i == 0 and h == 0:
                    d.wait_ge(decay_in, 16)
                if RH * i + h >= 2:
                    d.wait_ge(r_y, RH * i + h - 1)
                w = (i + 1) * P
                d.tensor_tensor(ats[:, h % 2, 0:w], ps[:, 6, 0:w], decay[:, h, (TT - 1 - i) * P:TT * P], ALU.mult).then_inc(r_dec, 1)

            def ret_var(i):
                d.wait_ge(r_sq, i + 1)
                d.tensor_scalar(yss[:, :], yss[:, :], 1.0 / RDV, EPS, ALU.mult, ALU.add).then_inc(var_ok, 1)

            def ret_norm(i):
                d.wait_ge(rstd_ok, N_RET + i)
                then(d.tensor_tensor(heads_view(tmpo[:, :], RH), heads_view(ps[:, 7, :], RH),
                                     yss[:, :].unsqueeze(2).broadcast_to([P, RH, RDV]), ALU.mult))
                d.wait_ge(rg_ok, i + 1)
                d.scalar_tensor_tensor(mix[:, i % 2, 0:512], tmpo[:, :], 0.5, rg[:, i, :], ALU.mult, ALU.mult).then_inc(r_norm, 1)
                d.wait_ge(r_norm, i + 1)

            def mix_low(i):
                d.wait_ge(mix_hi, i + 1)
                d.tensor_tensor(hTl[:, :, i * P:(i + 1) * P], ps[:, 6:8, :].rearrange("p b (k q) -> p (b k) q", k=4),
                                hTh[:, :, i * P:(i + 1) * P].bitcast(F32), ALU.subtract).then_inc(mix_lo, 1)

            for n in range(16 * TT + 7):
                i, s = divmod(n, 16)
                if n < 16 * TT:
                    row_min(n)
                if n < 2:
                    rope_chunk(K_WIN, (2 * n, 2 * n + 1))
                if n == 2:
                    d.wait_ge(proj_ev, TT * K_RV)
                    d.tensor_scalar(gates[:, :, :], gates[:, :, :], 0.5, 0.5, ALU.mult, ALU.add).then_inc(gates_ok, 1)
                    mod_columns(7, 2, 32, 0, KT, 48, 16).then_inc(mod_read, 1)
                    compressed()
                if n == 5:
                    d.wait_ge(kcT_hi, 1)
                    for g in range(NG):
                        ins = d.scalar_tensor_tensor(KCl[:, g, :], ps[:, 7, 0:CP], cst[:, K_GROUP + g:K_GROUP + g + 1],
                                                     KCh[:, g, :].bitcast(F32), ALU.mult, ALU.subtract)
                    ins.then_inc(kcT_lo, 1)
                if n == 4:
                    rot_low(9)
                if n == 7:
                    mod_columns(8, 3, 40, 0, KT, 40, None).then_inc(mod_read, 1)
                if 3 <= n < 3 + KT:
                    ada(ADA_LATE + n - 3)
                if UPC * (TT + 1) <= n <= LATE_STEPS and n % UPC == 0:
                    t = n // UPC - TT - 1
                    d.wait_ge(proj_ev, TT * K_RG + t + 1)
                    d.scalar_tensor_tensor(rg[:, t, :], rg[:, t, :], 1.0, ps[:, 3, :], ALU.add, ALU.mult).then_inc(rg_ok, 1)
                if n == 2 * 16 + 2:
                    mod_rows(9, ga2, 0, bank=6)
                if n == 2 * 16 + 3:
                    mod_rows(10, ga2, 1, bank=6)
                if n in OUT_STEPS:
                    scale_unit(U0_OUT + OUT_STEPS.index(n))
                if s == 1 and i >= 1:
                    ret_var(i - 1)
                if i >= 1 and s == (5 if i == 1 else 2):
                    ret_norm(i - 1)
                if s == 4 and i >= 1:
                    add_branch(i - 1, 2)
                if i >= 1 and s == mix_step(i) + 1:
                    mix_low(i - 1)
                if s == 8 and i < TT:
                    cmp_scores(i)
                if s == 10 and i < TT:
                    cmp_gates(i)
                if s == 12:
                    cmp_out(i)
                if s == 13:
                    add_branch(i, 1)
                if s >= 12:
                    ret_decay(i, s - 12)

            def residual(t):
                d.wait_ge(d_ps, t + 1)
                d.wait_ge(xagain_in, 16 * TT)
                d.tensor_tensor(x1[:, t, :], ps[:, 2 * t:2 * t + 2, :].rearrange("p b n -> p (b n)"), x1[:, t, :], ALU.add).then_inc(x1_ok, 1)

            def variance(t):
                d.wait_ge(sq2, t + 1)
                d.tensor_scalar(rstd[:, t:t + 1], ssq[:, t:t + 1], 1.0 / D, EPS, ALU.mult, ALU.add).then_inc(var_ok, 1)

            def normed(t):
                d.wait_ge(rstd_ok, N_X1 + t)
                d.tensor_scalar(xb[:, t % 2, :], x1[:, t, :], rstd[:, t:t + 1], None, ALU.mult).then_inc(xb_ok, 1)

            def modulate(t):
                d.wait_ge(xbT, 2 * t + 1)
                if t:
                    d.wait_ge(h2_lo, 2 * t)
                for k in range(4):
                    ins = d.tensor_scalar(h2[:, 0, k, :], ps[:, 2 * t, k * P:(k + 1) * P], mods[:, 2, k:k + 1], mods[:, 3, k:k + 1],
                                          ALU.mult, ALU.add)
                ins.then_inc(h2_ok, 1)

            def h2_low(t):
                for b in (1, 0):
                    ks = slice(4 * b, 4 * b + 4)
                    d.wait_ge(h2_hi, 2 * t + 2 - b)
                    if b == 0:
                        d.wait_ge(h2_ok, t + 1)
                    d.tensor_tensor(hTl[:, ks, t * P:(t + 1) * P], h2[:, b], hTh[:, ks, t * P:(t + 1) * P].bitcast(F32),
                                    ALU.subtract).then_inc(h2_lo, 1)

            for u in range(U0_OUT + SPLIT, U0_GU):
                scale_unit(u)
            residual(0)
            variance(0)
            normed(0)
            for t in range(TT):
                if t < TT - 1:
                    residual(t + 1)
                modulate(t)
                if t < TT - 1:
                    variance(t + 1)
                h2_low(t)
                if t < TT - 1:
                    normed(t + 1)

            def a_low(f):
                d.wait_ge(a_hi, f + 1)
                d.tensor_tensor(al[:, f % SPLIT, :], act[:, f, :], ah[:, f % SPLIT, :].bitcast(F32), ALU.subtract).then_inc(a_lo, 1)

            for f in range(FT):
                d.wait_ge(sg_ok, f + 1)
                d.wait_ge(up_ps, f + 1)
                d.tensor_tensor(act[:, f, :], ps[:, 2 * (f % 2) + 1, :], sg[:, f % 2, :], ALU.mult).then_inc(act_ok, 1)
                for u in (U0_GU + 2 * f + 4, U0_GU + 2 * f + 5):
                    if u >= U0_DOWN:
                        scale_unit(u)
                if 3 <= f < 3 + SPLIT:
                    a_low(f - 3)
            for f in range(FT):
                if f >= SPLIT:
                    a_low(f)
                if f + SPLIT < FT:
                    scale_unit(U0_DOWN + f + SPLIT)
            d.wait_ge(gfin_in, 16)
            for t in range(TT):
                for half in range(2):
                    cols_ = slice(half * 512, (half + 1) * 512)
                    d.wait_ge(y_ps, 2 * t + half + 1)
                    d.tensor_tensor(x1[:, t, cols_], ps[:, 2 * t + half, :], x1[:, t, cols_], ALU.add).then_inc(x2_ok, 1)
                d.wait_ge(sq3, 2 * t + 2)
                then(d.tensor_tensor(ssq[:, t:t + 1], ssq[:, t:t + 1], ssq2[:, t:t + 1], ALU.add))
                d.tensor_scalar(rstd[:, t:t + 1], ssq[:, t:t + 1], 1.0 / D, EPS, ALU.mult, ALU.add).then_inc(var_ok, 1)
                d.tensor_tensor(x1[:, t, 0:512], x1[:, t, 0:512], gfin[:, 0:512], ALU.mult).then_inc(y_scaled, 1)
                d.wait_ge(y_scaled, t + 1)
                d.wait_ge(rstd_ok, N_X2 + t)
                d.tensor_scalar(xb[:, t % 2, 0:512], x1[:, t, 0:512], rstd[:, t:t + 1], None, ALU.mult)
                d.scalar_tensor_tensor(xb[:, t % 2, 512:D], x1[:, t, 512:D], rstd[:, t:t + 1], gfin[:, 512:D],
                                       ALU.mult, ALU.mult).then_inc(y_ok, 1)

        @block.tensor
        def _(pe):
            mm = pe.matmul

            def product(o, ah_, al_, bh_, bl_, first, last):
                mm(o, ah_, bh_, start=first, stop=False)
                mm(o, ah_, bl_, start=False, stop=False)
                return mm(o, al_, bh_, start=False, stop=last)

            pe.wait_ge(ident_in, 16)
            pe.wait_ge(c_in, 16)
            pe.transpose(ps[:, 5, 0:KT], crow[:, :], ident[0:KT, 0:KT]).then_inc(cT, 1)
            pe.wait_ge(rows_in, 16 * 2)
            pe.wait_ge(biases_in, 16 * 4)
            pe.transpose(ps[:, 4, 0:P], rows[:, :], ident).then_inc(rowsT, 1)
            def sum_columns(i, c0, ks):
                for n, k in enumerate(ks):
                    ins = mm(ps[:, 7, c0 + n:c0 + n + 1], acc[:, i, k * P:(k + 1) * P], ones[:, 0:1], start=True, stop=True)
                return ins

            def modulation(q):
                pe.wait_ge(ada_used, 16 * (q + 1))
                if q:
                    pe.wait_ge(mod_read, q)
                sum_columns(0, 4 * q, (2 * q, 2 * q + 1))
                sum_columns(1, 4 * q + 2, (2 * q, 2 * q + 1)).then_inc(mod_sum, 1)

            pe.wait_ge(ones_set, 2)
            for k in range(KT):
                if k == 6:
                    modulation(0)
                if k >= 4:
                    pe.wait_ge(xT_ok, k - 3)
                for t in range(TT):
                    if k == 0:
                        pe.wait_ge(xn_done if t < 2 else xn_done2, t % 2 + 1)
                    ins = pe.transpose(ps[:, k % 4, t * P:(t + 1) * P], xs[:, t, k * P:(k + 1) * P], ident)
                ins.then_inc(xT_ps, 1)

            def sum_rows(g, half, bank=7):
                pe.wait_ge(ada_used, ada_ops(KT * (g + 1) - 1))
                src = acc2 if g == 5 else acc[:, g % 2, :]
                mm(ps[:, bank, :], ones[:, :], src[:, half * 512:(half + 1) * 512], start=True, stop=True).then_inc(mod_sum, 1)


            def flat_transposes(b):
                if b == 0:
                    pe.wait_ge(flat_in, 16 * 8)
                else:
                    pe.wait_ge(flatT_ok, b)
                for j in range(4):
                    ins = pe.transpose(ps[:, 6, j * P:(j + 1) * P], flat[:, (4 * b + j) * P:(4 * b + j + 1) * P], ident)
                ins.then_inc(flatT_ps, 1)

            def rot_transposes(n):
                if n >= 2:
                    pe.wait_ge(rot_hi, n - 1)
                    pe.wait_ge(rot_lo, min(n - 1, 5))
                if n == 0 or n == 9:
                    pe.wait_ge(roped, TT if n == 0 else 4 * TT)
                    for t in range(TT):
                        src = rot[:, t, 0:P] if n == 0 else rot_w[:, t, :]
                        ins = pe.transpose(ps[:, 4 + n % 2, t * P:(t + 1) * P], src, ident)
                else:
                    t = (n - 1) % 4
                    pe.wait_ge(roped, (TT if n < 5 else 2 * TT) + t + 1)
                    for h in range(4):
                        ins = pe.transpose(ps[:, 4 + n % 2, h * P:(h + 1) * P], rot[:, t, h * P:(h + 1) * P], ident)
                ins.then_inc(rotT, 1)

            for v in range(U_PROJ):
                ch, q = divmod(v, UPC)
                n = CHUNKS[ch][1]
                pe.wait_ge(w_lo, v + 1)
                bh, bl = (w.rearrange("p (k n) -> p k n", k=2) for w in split(v, 2 * n))
                for t in range(TT):
                    if v < UPC - 1 and t == TT // 2:
                        modulation(q + 1)
                    if ch and q == 0:
                        pe.wait_ge(proj_ev, TT * (ch - 1) + t + 1)
                    for kk in range(2):
                        k = 2 * q + kk
                        if ch == 0 and t == 0:
                            pe.wait_ge(h_lo, k + 1)
                        tok = slice(t * P, (t + 1) * P)
                        ins = product(ps[:, t, 0:n], hTh[:, k, tok], hTl[:, k, tok], bh[:, kk, :], bl[:, kk, :], k == 0, k == KT - 1)
                    if q == UPC - 1 and t < TT - 1:
                        ins.then_inc(o_ps, 1)
                ins.then_inc(unit_used, 1)
                for m in {6: [0], 9: [1, 2], 11: [3, 4], 13: [5, 6], 15: [7, 8]}.get(v, []):
                    rot_transposes(m)
                if 9 <= v <= 12:
                    flat_transposes(v - 9)
                if v == 7:
                    pe.wait_ge(mod_read, 4)
                    sum_rows(2, 0)
                if v == 9:
                    pe.wait_ge(mod_read, 5)
                    sum_rows(2, 1)
                if v == 14:
                    pe.wait_ge(flatT_ok, 4)
                    pe.wait_ge(w1_in, 32)
                    pe.wait_ge(mod_read, 6)
                    for kv in range(2):
                        for j in range(CL // 2):
                            ins = mm(ps[:, 7, kv * 2 * CP:(kv + 1) * 2 * CP], w1[:, kv, j, :], flatT[:, j, kv * 2 * CP:(kv + 1) * 2 * CP],
                                     start=j == 0, stop=j == CL // 2 - 1)
                    ins.then_inc(mlp1, 1)
                if v == 15:
                    pe.wait_ge(mlp1_silu, 1)
                    pe.wait_ge(w2_in, 32)
                    for kv in range(2):
                        for g in range(NG):
                            ins = mm(ps[0:CP, 6, kv * P + g * DH:kv * P + (g + 1) * DH], hs[:, kv, g * CP:(g + 1) * CP], w2[:, kv, :],
                                     start=True, stop=True)
                    ins.then_inc(mlp2, 1)
                    pe.wait_ge(ada_used, ada_ops(4 * KT - 1))
                    sum_columns(1, 32, range(KT)).then_inc(mod_sum, 1)

            def scores(n):
                i = n // 16
                b, hd = divmod(n % 16, 8)
                h, g = divmod(hd, 2)
                w = (i + 1) * P
                if n == THREE + 2:
                    pe.wait_ge(rg_ok, TT)
                elif n < 2:
                    pe.wait_ge(proj_ev, TT * K_WIN + n + 1)
                else:
                    pe.wait_ge(p_exp, n - 1 if n < THREE + 2 else n - 2)
                if n == 8:
                    pe.wait_ge(rot_hi, 10)
                    pe.wait_ge(rot_lo, 6)
                g0, g1 = g * DH, (g + 1) * DH
                qs = slice(i * P, (i + 1) * P)
                o = ps[:, s_bank(n), 0:w]
                product(o, QTh[g0:g1, h, qs], QTl[g0:g1, h, qs], KTh[g0:g1, b, 0:w], KTl[g0:g1, b, 0:w], True, False)
                mm(ps[:, s_bank(n), i * P:w], identR[:, :], maskR[:, :], start=False, stop=True).then_inc(s_ps, 1)

            def transposes(n):
                i = n // 16
                pe.wait_ge(p_exp, n + 1)
                if n:
                    pe.wait_ge(pT_ok, n)
                else:
                    pe.wait_ge(rot_hi, 9)
                for j in range(i + 1):
                    ins = pe.transpose(ps[:, 2, j * P:(j + 1) * P], Pr[:, n % 3, j * P:(j + 1) * P], ident)
                ins.then_inc(p_T, 1)

            def values(n):
                i = n // 16
                b, hd = divmod(n % 16, 8)
                h, g = divmod(hd, 2)
                head = g * HPG + h
                pe.wait_ge(pT_ok, n + 1)
                if hd == 0 and i:
                    pe.wait_ge(y_sum, 3 * (i - 1) + b + 2)
                for j in range(i + 1):
                    ins = mm(ps[:, 4 + b, head * DH:(head + 1) * DH], PT[:, n % 2, j * P:(j + 1) * P],
                             V[:, j, b, g * DH:(g + 1) * DH], start=j == 0, stop=j == i)
                ins.then_inc(pv, 1)

            def cmp_scores(i):
                if i == 0:
                    pe.wait_ge(kcT_lo, 1)
                    pe.wait_ge(mod_read, 8)
                else:
                    pe.wait_ge(mix_lo, i)
                qs = slice(i * P, (i + 1) * P)
                for h in range(HPG):
                    ins = product(ps[:, 6, h * NG * CP:(h + 1) * NG * CP], QTh[:, h, qs], QTl[:, h, qs],
                                  KCh[:, :, :].rearrange("p g n -> p (g n)"), KCl[:, :, :].rearrange("p g n -> p (g n)"), True, True)
                ins.then_inc(cs_ps, 1)

            def ret_scores(i, h):
                p0 = (h % 2) * RDK
                if h == 0:
                    pe.wait_ge(cT_ok, i + 1)
                if RH * i + h:
                    pe.wait_ge(r_dec, RH * i + h)
                for j in range(i + 1):
                    ins = mm(ps[:, 6, j * P:(j + 1) * P], rkT[p0:p0 + RDK, h // 2, j * P:(j + 1) * P],
                             rqT[p0:p0 + RDK, h // 2, i * P:(i + 1) * P], start=True, stop=True)
                ins.then_inc(r_s, 1)

            def ret_values(i, h):
                pe.wait_ge(r_dec, RH * i + h + 1)
                pe.wait_ge(proj_ev, TT * K_RV + (1 if i == 0 else TT))
                if h == 0:
                    pe.wait_ge(y_sum, 3 * i + 1)
                for j in range(i + 1):
                    ins = mm(ps[:, 7, h * P:(h + 1) * P], ats[:, h % 2, j * P:(j + 1) * P], rv[:, j, h * P:(h + 1) * P],
                             start=j == 0, stop=j == i)
                ins.then_inc(r_y, 1)

            def mix_transposes(i):
                if i == 1:
                    pe.wait_ge(mod_read, 10)
                pe.wait_ge(y_sum, 3 * (i + 1))
                pe.wait_ge(r_norm, i + 1)
                for k in range(KT):
                    ins = pe.transpose(ps[:, 6 + k // 4, (k % 4) * P:(k % 4 + 1) * P], mix[:, i % 2, k * P:(k + 1) * P], ident)
                ins.then_inc(mixT_ps, 1)

            def late_piece(c_, t, q):
                u = U_PROJ + UPC * c_ + q
                if t == 0:
                    pe.wait_ge(w_lo, u + 1)
                if q == 0:
                    if c_ and t:
                        pe.wait_ge(rg_ok, t)
                    else:
                        pe.wait_ge(proj_ev, TT * K_RV + TT * c_ + t)
                bh, bl = (w.rearrange("p (k n) -> p k n", k=2) for w in split(u, D))
                tok = slice(t * P, (t + 1) * P)
                for kk in range(2):
                    k = 2 * q + kk
                    ins = product(ps[:, 3, :], hTh[:, k, tok], hTl[:, k, tok], bh[:, kk, :], bl[:, kk, :], k == 0, k == KT - 1)
                ins.then_inc(late_ps, 1)

            pe.wait_ge(rot_hi, 5)
            pe.wait_ge(rot_lo, 5)
            for n in range(16 * TT + 4):
                i, s = divmod(n, 16)
                if n < 16 * TT:
                    scores(n)
                if 3 <= n <= 16 * TT + 2:
                    transposes(n - 3)
                if n >= 4:
                    values(n - 4)
                if n < LATE_STEPS:
                    late_piece(n // UPC // TT, n // UPC % TT, n % UPC)
                if n == 3:
                    rot_transposes(9)
                if n == 4:
                    pe.wait_ge(kc_rot, 1)
                    pe.wait_ge(mod_read, 7)
                    pe.transpose(ps[:, 7, 0:CP], kcr[:, :], ident[0:CP, 0:CP]).then_inc(kcT, 1)
                if n == 6:
                    pe.wait_ge(kcT_lo, 1)
                    pe.wait_ge(ada_used, ada_ops(5 * KT - 1))
                    sum_columns(0, 40, range(KT)).then_inc(mod_sum, 1)
                if s == 0 and i >= 1:
                    ret_values(i - 1, RH - 1)
                if n == 2 * 16 + 2:
                    sum_rows(5, 0, bank=6)
                if n == 2 * 16 + 3:
                    pe.wait_ge(mod_read, 9)
                    sum_rows(5, 1, bank=6)
                if i >= 1 and s == mix_step(i):
                    mix_transposes(i - 1)
                if s == 8 and i < TT:
                    cmp_scores(i)
                if s == 10 and i < TT:
                    pe.wait_ge(c_exp, i + 1)
                    for g in range(NG):
                        ins = pe.transpose(ps[:, 6, g * P:(g + 1) * P], pc[:, g * HPG:(g + 1) * HPG, :], ident)
                    ins.then_inc(c_T, 1)
                if s == 11 and i < TT:
                    pe.wait_ge(cT_ok, i + 1)
                    pe.wait_ge(bd_ok, 1)
                    for g in range(NG):
                        ins = mm(ps[:, 7, g * 256:(g + 1) * 256], pcT[:, g, :], BD[:, g, :], start=True, stop=True)
                    ins.then_inc(c_o, 1)
                if s >= 12:
                    ret_scores(i, s - 12)
                if s >= 13:
                    ret_values(i, s - 13)

            def two_halves(t, u, stat, first, last, half=None):
                hi, lo = split(u, D)
                for b in range(2) if half is None else (half,):
                    cols_ = slice(b * 512, (b + 1) * 512)
                    ins = product(ps[:, 2 * t + b, :], stat[0], stat[1], hi[:, cols_], lo[:, cols_], first, last)
                return ins

            def out_unit(t, k):
                tok = slice(t * P, (t + 1) * P)
                return two_halves(t, U0_OUT + k, (hTh[:, k, tok], hTl[:, k, tok]), k == 0, k == KT - 1)

            pe.wait_ge(w_lo, U0_OUT + 2)
            for k in range(2):
                for t in range(2):
                    out_unit(t, k)
            mix_transposes(TT - 1)
            out_unit(2, 0)
            out_unit(2, 1)
            pe.wait_ge(mix_lo, TT)
            for k in range(KT - OUT_TAIL):
                if k >= 2:
                    pe.wait_ge(w_lo, U0_OUT + k + 1)
                for t in range(TT) if k >= 2 else (TT - 1,):
                    ins = out_unit(t, k)
                ins.then_inc(unit_used, 1)

            def h2_transposes(t):
                pe.wait_ge(xb_ok, t + 1)
                for b in range(2):
                    for k in range(4):
                        ins = pe.transpose(ps[:, 2 * t + b, k * P:(k + 1) * P], xb[:, t % 2, (4 * b + k) * P:(4 * b + k + 1) * P], ident)
                    ins.then_inc(xbT, 1)

            pe.wait_ge(w_lo, U0_OUT + KT)
            for t in range(TT):
                for k in range(KT - OUT_TAIL, KT):
                    ins = out_unit(t, k)
                ins.then_inc(d_ps, 1)
                if t >= 1:
                    h2_transposes(t - 1)

            def gate_up(f, up, c0, c1):
                u = U0_GU + 2 * f + up
                hi, lo = split(u, D)
                if c0 == 0:
                    pe.wait_ge(w_lo, u + 1)
                o = ps[:, 2 * (f % 2) + up, c0:c1]
                for k in range(KT):
                    ks = slice(k * P, (k + 1) * P)
                    mm(o, hi[:, ks], hTh[:, k, c0:c1], start=k == 0, stop=False)
                    mm(o, hi[:, ks], hTl[:, k, c0:c1], start=False, stop=False)
                    ins = mm(o, lo[:, ks], hTh[:, k, c0:c1], start=False, stop=k == KT - 1)
                return ins

            pe.wait_ge(h2_lo, 4)
            gate_up(0, 0, 0, 2 * P)
            gate_up(0, 1, 0, 2 * P)
            h2_transposes(3)
            gate_up(1, 0, 0, 2 * P)
            gate_up(1, 1, 0, 2 * P)
            pe.wait_ge(h2_lo, 8)
            for f in range(2):
                gate_up(f, 0, 2 * P, T).then_inc(gate_ps, 1)
                gate_up(f, 1, 2 * P, T).then_inc(up_ps, 1)
            for f in range(2, FT):
                pe.wait_ge(act_ok, f - 1)
                gate_up(f, 0, 0, T).then_inc(gate_ps, 1)
                gate_up(f, 1, 0, T).then_inc(up_ps, 1)

            for f in range(FT - DOWN_TAIL):
                pe.wait_ge(w_lo, U0_DOWN + f + 1)
                pe.wait_ge(a_lo, f + 1)
                for t in range(TT) if f else (2, 3, 0, 1):
                    if f == 0 and t < 2:
                        pe.wait_ge(act_ok, FT - 1 + t)
                    tok = slice(t * P, (t + 1) * P)
                    ins = two_halves(t, U0_DOWN + f, (ah[:, f % SPLIT, tok], al[:, f % SPLIT, tok]), f == 0, False)
                ins.then_inc(a_used, 1)
            pe.wait_ge(w_lo, UNITS)
            pe.wait_ge(a_lo, FT)
            for t in range(TT):
                tok = slice(t * P, (t + 1) * P)
                for half in range(2):
                    for f in range(FT - DOWN_TAIL, FT):
                        ins = two_halves(t, U0_DOWN + f, (ah[:, f % SPLIT, tok], al[:, f % SPLIT, tok]), False, f == FT - 1, half)
                    ins.then_inc(y_ps, 1)


def shape_constants():
    k = np.zeros((P, K_N), np.float32)
    k[:, K_ID:K_ID + P] = np.eye(P, dtype=np.float32)
    q = np.arange(P)
    k[:, K_MASK:K_MASK + P] = np.where(q[None, :] > q[:, None], BIG, 0.0)

    def rope_rows(pos):
        half = DH // 2
        inv = np.float32(10000.0) ** (-np.arange(half, dtype=np.float32) / np.float32(half))
        ang = pos.astype(np.float32)[:, None] * inv
        cos, sin = np.cos(ang), np.sin(ang)
        return np.concatenate([cos, cos, -sin, sin], axis=1)

    r = rope_rows(np.arange(T))
    k[:, K_ROPE:K_ROPE + TT * P] = r.reshape(TT, P, P).transpose(1, 0, 2).reshape(P, TT * P)
    end = np.arange(CP) * CS + CL - 1
    seen = (end[None, :] <= np.arange(T)[:, None]) & (np.arange(CP) < NC)[None, :]
    m = np.where(seen, 0.0, BIG).astype(np.float32)
    k[:, K_CMASK:K_CMASK + TT * CP] = m.reshape(TT, P, CP).transpose(1, 0, 2).reshape(P, TT * CP)
    k[:, K_VALID] = (q >= CL - 1)
    for g in range(NG):
        k[:, K_GROUP + g] = (q // DH == g)
    k[0:CP, K_CROPE:K_CROPE + P] = rope_rows(end)
    log_g = np.log(1.0 - 2.0 ** (-5.0 - np.arange(RH)))
    x = np.arange(T)
    diff = (TT - 1 - x[None, :] // P) * P + x[None, :] % P - q[:, None]
    dec = np.where(diff[None] >= 0, np.exp(log_g[:, None, None] * np.maximum(diff, 0)[None]), 0.0)
    return k, np.ascontiguousarray(dec.transpose(1, 0, 2)).astype(np.float32)


_INS = ['x', 'c', 'ln_mix_g', 'ln_ffn_g', 'w_ada', 'b_ada', 'w_in', 'cmp_pe_k', 'cmp_w1_k', 'cmp_w2_k',
        'cmp_pe_v', 'cmp_w1_v', 'cmp_w2_v', 'w_out', 'w_ff_gate', 'w_ff_up', 'w_ff_down', 'ln_final_g']


def kernel(**inputs):
    import numpy as _np
    import concourse.bacc as _bacc
    from concourse import mybir as _mybir
    from concourse.bass_utils import run_bass_kernel_spmd as _run

    nc = _bacc.Bacc("TRN2", target_bir_lowering=False, num_devices=1)
    arrays, args = {}, []
    for name in _INS:
        a = _np.ascontiguousarray(inputs[name])
        if name != 'ln_final_g':
            a = a[0]
        arrays[f"in_{name}"] = a
        args.append(nc.dram_tensor(f"in_{name}", a.shape, _mybir.dt.from_np(a.dtype), kind="ExternalInput").ap())
    for name, a in zip(("consts", "decays"), shape_constants()):
        arrays[f"in_{name}"] = a
        args.append(nc.dram_tensor(f"in_{name}", a.shape, _mybir.dt.float32, kind="ExternalInput").ap())
    args.append(nc.dram_tensor("out_0", (T, D), _mybir.dt.float32, kind="ExternalOutput").ap())
    block_kernel(nc, *args)
    r = _run(nc, [arrays], core_ids=[0])
    return r.results[0]["out_0"].reshape(1, T, D)
```
